# Optimizing a Trainium2 kernel written in Bass

```python
import jax
import jax.numpy as jnp
from jax import lax
import numpy as np

D_MODEL = 1024
BATCH = 1
SEQ = 256
DEPTH = 2

GRID_W = 64
CTX_LEN = 256
N_EVEN = (DEPTH + 1) // 2
N_ODD = DEPTH // 2
EPS = 1e-6
A_HEADS = 4
A_DK = 128
A_DV = 128
A_KW = A_HEADS * A_DK
A_WIDTH = A_HEADS * A_DV
CHUNK = 64
B_HEADS = 8
B_DH = 64
B_WIDTH = B_HEADS * B_DH
WIN_ROWS = 8
WIN_COLS = 16
Q_BLOCK_ROWS = 2
IN_SIZES = (A_KW, A_KW, A_KW, A_WIDTH, A_WIDTH, B_WIDTH, B_WIDTH, B_WIDTH)
IN_WIDTH = 3 * A_KW + 2 * A_WIDTH + 3 * B_WIDTH
POOL_WINDOWS = (2, 4, 8, 16)
C_GROUP = D_MODEL // 4
N_EXPERTS = 16
N_GROUPS = 4
EXPERTS_PER_GROUP = N_EXPERTS // N_GROUPS
TOP_K = 2
D_EXPERT = 512

kernel_name = 'hybrid_hgrn2_natten_pool_moe_dit'

def rms_norm(x, g):
    xf = x.astype(jnp.float32)
    y = xf * lax.rsqrt(jnp.mean(xf * xf, axis=-1, keepdims=True) + EPS)
    return (y * g.astype(jnp.float32)).astype(x.dtype)

def adaln(cond, w, b):
    return jnp.split(jax.nn.silu(cond) @ w + b, 6, axis=-1)

def modulate(u, shift, scale):
    return u * (1 + scale) + shift

def to_heads(t, h):
    b_, l_, hd = t.shape
    return t.reshape(b_, l_, h, hd // h).transpose(0, 2, 1, 3)

def hgrn_lower_bounds(lb_logits):
    p = jax.nn.softmax(lb_logits.astype(jnp.float32), axis=0)
    return jnp.cumsum(p, axis=0)[1:] - p[0]

def gated_scan(q, k, v, log_f, s0):
    b_, h_, l_, _ = q.shape
    n = l_ // CHUNK

    def to_chunks(t):
        return jnp.moveaxis(t.reshape(b_, h_, n, CHUNK, t.shape[-1]), 2, 0)

    causal = jnp.tril(jnp.ones((CHUNK, CHUNK), bool))[:, :, None]

    def step(s, inp):
        qi, ki, vi, fi = inp
        bc = jnp.cumsum(fi, axis=2)
        diff = bc[:, :, :, None, :] - bc[:, :, None, :, :]
        decay = jnp.exp(jnp.where(causal, diff, -jnp.inf))
        scores = jnp.einsum('bhtk,bhsk,bhtsk->bhts', qi, ki, decay)
        o = (jnp.einsum('bhts,bhsv->bhtv', scores, vi)
             + jnp.einsum('bhtk,bhkv->bhtv', qi * jnp.exp(bc), s))
        b_last = bc[:, :, -1:, :]
        s_new = (jnp.exp(b_last[:, :, 0, :, None]) * s
                 + jnp.einsum('bhsk,bhsv->bhkv', ki * jnp.exp(b_last - bc), vi))
        return s_new, o

    s_fin, oc = lax.scan(step, s0, (to_chunks(q), to_chunks(k), to_chunks(v), to_chunks(log_f)))
    return jnp.moveaxis(oc, 0, 2).reshape(b_, h_, l_, v.shape[-1]), s_fin

def context_final_state(k, v, log_f):
    bc = jnp.cumsum(log_f, axis=2)
    return jnp.einsum('bhsk,bhsv->bhkv', k * jnp.exp(bc[:, :, -1:, :] - bc), v)

def hgrn2_direction(q_c, i_c, f_c, q_l, i_l, f_l, lb_dir, reverse, ctx_out):
    def heads(t):
        t = to_heads(t, A_HEADS)
        return t[:, :, ::-1] if reverse else t

    def gates(f_raw):
        f = lb_dir + (1.0 - lb_dir) * jax.nn.sigmoid(f_raw.astype(jnp.float32))
        return heads(1.0 - f), heads(jnp.log(f))

    scale = A_DK ** -0.5
    k_c, lf_c = gates(f_c)
    v_c = heads(i_c.astype(jnp.float32))
    if ctx_out:
        s0 = jnp.zeros(k_c.shape[:2] + (A_DK, A_DV), jnp.float32)
        o_c, s_c = gated_scan(heads(q_c.astype(jnp.float32)) * scale, k_c, v_c, lf_c, s0)
    else:
        o_c, s_c = None, context_final_state(k_c, v_c, lf_c)
    k_l, lf_l = gates(f_l)
    o_l, _ = gated_scan(heads(q_l.astype(jnp.float32)) * scale, k_l, heads(i_l.astype(jnp.float32)), lf_l, s_c)
    if reverse:
        o_l = o_l[:, :, ::-1]
        o_c = None if o_c is None else o_c[:, :, ::-1]
    return o_c, o_l

def hgrn2_readout(o, g, norm_g):
    o = o * lax.rsqrt(jnp.mean(o * o, axis=-1, keepdims=True) + EPS)
    b_, h_, l_, v_ = o.shape
    o = o.transpose(0, 2, 1, 3).reshape(b_, l_, h_ * v_) * norm_g.astype(jnp.float32)
    return (o * jax.nn.silu(g.astype(jnp.float32))).astype(g.dtype)

def neighbourhood_attention(q, k, v, k_ctx, v_ctx, rpb):
    b_, n_, h_, dh = q.shape
    rows = n_ // GRID_W
    wr = min(WIN_ROWS, rows)
    wc = WIN_COLS
    nwin = wr * wc
    qb = Q_BLOCK_ROWS * GRID_W
    scale = dh ** -0.5
    cols = jnp.arange(GRID_W)
    key_cols = jnp.clip(cols - wc // 2, 0, GRID_W - wc)[:, None] + jnp.arange(wc)
    dc = key_cols - cols[:, None] + (WIN_COLS - 1)
    rpb = rpb.astype(jnp.float32)

    def block(blk):
        r = blk * Q_BLOCK_ROWS + jnp.arange(Q_BLOCK_ROWS)
        key_rows = jnp.clip(r - wr // 2, 0, rows - wr)[:, None] + jnp.arange(wr)
        dr = key_rows - r[:, None] + (WIN_ROWS - 1)
        idx = (key_rows[:, None, :, None] * GRID_W + key_cols[None, :, None, :]).reshape(qb, nwin)
        bias = rpb[:, dr[:, None, :, None], dc[None, :, None, :]].reshape(h_, qb, nwin)
        q_blk = lax.dynamic_slice_in_dim(q, blk * qb, qb, axis=1)
        k_win = jnp.take(k, idx, axis=1)
        v_win = jnp.take(v, idx, axis=1)
        s_win = jnp.einsum('bqhd,bqkhd->bhqk', q_blk, k_win).astype(jnp.float32) * scale + bias
        s_ctx = jnp.einsum('bqhd,bchd->bhqc', q_blk, k_ctx).astype(jnp.float32) * scale
        p = jax.nn.softmax(jnp.concatenate([s_win, s_ctx], axis=-1), axis=-1).astype(q.dtype)
        return (jnp.einsum('bhqk,bqkhd->bqhd', p[..., :nwin], v_win)
                + jnp.einsum('bhqc,bchd->bqhd', p[..., nwin:], v_ctx))

    out = lax.map(block, jnp.arange(rows // Q_BLOCK_ROWS))
    return jnp.moveaxis(out, 0, 1).reshape(b_, n_, h_ * dh)

def context_attention(q, k, v):
    s = jnp.einsum('bqhd,bkhd->bhqk', q, k).astype(jnp.float32) * (q.shape[-1] ** -0.5)
    p = jax.nn.softmax(s, axis=-1).astype(q.dtype)
    o = jnp.einsum('bhqk,bkhd->bqhd', p, v)
    return o.reshape(o.shape[0], o.shape[1], -1)

def even_mixer(u_c, u_l, w_in, w_out, lb, a_norm_g, rpb, ctx_out):
    offs = [int(o) for o in np.cumsum(IN_SIZES)[:-1]]
    qa_c, ff_c, fb_c, ia_c, ga_c, qb_c, kb_c, vb_c = jnp.split(u_c @ w_in, offs, axis=-1)
    qa_l, ff_l, fb_l, ia_l, ga_l, qb_l, kb_l, vb_l = jnp.split(u_l @ w_in, offs, axis=-1)
    o_cf, o_lf = hgrn2_direction(qa_c, ia_c, ff_c, qa_l, ia_l, ff_l, lb[0], False, ctx_out)
    o_cb, o_lb = hgrn2_direction(qa_c, ia_c, fb_c, qa_l, ia_l, fb_l, lb[1], True, ctx_out)
    a_l = hgrn2_readout(o_lf + o_lb, ga_l, a_norm_g)
    bh = lambda t: t.reshape(t.shape[0], t.shape[1], B_HEADS, B_DH)
    b_l = neighbourhood_attention(bh(qb_l), bh(kb_l), bh(vb_l), bh(kb_c), bh(vb_c), rpb)
    y_l = jnp.concatenate([a_l, b_l.astype(a_l.dtype)], axis=-1) @ w_out
    if not ctx_out:
        return None, y_l
    a_c = hgrn2_readout(o_cf + o_cb, ga_c, a_norm_g)
    b_c = context_attention(bh(qb_c), bh(kb_c), bh(vb_c))
    y_c = jnp.concatenate([a_c, b_c.astype(a_c.dtype)], axis=-1) @ w_out
    return y_c, y_l

def pool_mixer(u, w_pool, pool_scale):
    b_, l_, d_ = u.shape
    uf = u.astype(jnp.float32)
    csum = jnp.concatenate([jnp.zeros((b_, 1, d_), jnp.float32), jnp.cumsum(uf, axis=1)], axis=1)
    t = np.arange(l_)
    outs = []
    for g, win in enumerate(POOL_WINDOWS):
        ch = slice(g * C_GROUP, (g + 1) * C_GROUP)
        lo = np.clip(t - win // 2, 0, l_)
        hi = np.clip(t + win // 2, 0, l_)
        count = (hi - lo).astype(np.float32)[:, None]
        cg = csum[:, :, ch]
        mean = (cg[:, hi] - cg[:, lo]) / count
        outs.append(jnp.einsum('bld,de->ble', mean - uf[:, :, ch], w_pool[g].astype(jnp.float32)))
    return (jnp.concatenate(outs, axis=-1) * pool_scale.astype(jnp.float32)).astype(u.dtype)

def grouped_moe(u, w_router, b_router, w_gate, w_up, w_down):
    s = jax.nn.sigmoid(jnp.einsum('bld,de->ble', u, w_router).astype(jnp.float32))
    sb = s + b_router.astype(jnp.float32)
    grp = sb.reshape(sb.shape[:-1] + (N_GROUPS, EXPERTS_PER_GROUP))
    group_score = jnp.sum(lax.top_k(grp, 2)[0], axis=-1)
    sel_group = jnp.argmax(group_score, axis=-1)
    in_group = (jnp.arange(N_EXPERTS) // EXPERTS_PER_GROUP) == sel_group[..., None]
    _, idx = lax.top_k(jnp.where(in_group, sb, -jnp.inf), TOP_K)
    w_sel = jnp.take_along_axis(s, idx, axis=-1)
    w_sel = w_sel / jnp.sum(w_sel, axis=-1, keepdims=True)
    gates = jnp.sum(jax.nn.one_hot(idx, N_EXPERTS, dtype=jnp.float32) * w_sel[..., None], axis=-2).astype(u.dtype)
    y = jnp.zeros_like(u)
    for e in range(N_EXPERTS):
        h = jax.nn.silu(u @ w_gate[e]) * (u @ w_up[e])
        y = y + gates[..., e:e + 1] * (h @ w_down[e])
    return y

def setup_inputs(seed: int = 0) -> dict:
    key = jax.random.key(seed)
    ks = jax.random.split(key, 21)

    def nrm(k, shape, s):
        return jax.random.normal(k, shape, jnp.float32) * s

    return {
        'x': nrm(ks[0], (BATCH, SEQ, D_MODEL), 1.0),
        'c': nrm(ks[1], (BATCH, D_MODEL), 1.0),
        'ctx': nrm(ks[2], (BATCH, CTX_LEN, D_MODEL), 1.0),
        'c_ctx': nrm(ks[3], (D_MODEL,), 1.0),
        'w_mod': nrm(ks[4], (DEPTH, D_MODEL, 6 * D_MODEL), 0.5 * D_MODEL ** -0.5),
        'b_mod': nrm(ks[5], (DEPTH, 6 * D_MODEL), 0.02),
        'norm1_g': 1.0 + nrm(ks[6], (DEPTH, D_MODEL), 0.05),
        'norm2_g': 1.0 + nrm(ks[7], (DEPTH, D_MODEL), 0.05),
        'w_in': nrm(ks[8], (N_EVEN, D_MODEL, IN_WIDTH), D_MODEL ** -0.5),
        'w_out': nrm(ks[9], (N_EVEN, A_WIDTH + B_WIDTH, D_MODEL), (A_WIDTH + B_WIDTH) ** -0.5),
        'lb_logits': nrm(ks[10], (N_EVEN + 1, 2, A_KW), 0.5),
        'a_norm_g': 1.0 + nrm(ks[11], (N_EVEN, A_WIDTH), 0.05),
        'rpb': nrm(ks[12], (N_EVEN, B_HEADS, 2 * WIN_ROWS - 1, 2 * WIN_COLS - 1), 0.1),
        'w_pool': nrm(ks[13], (N_ODD, len(POOL_WINDOWS), C_GROUP, C_GROUP), C_GROUP ** -0.5),
        'pool_scale': 1.0 + nrm(ks[14], (N_ODD, D_MODEL), 0.1),
        'w_router': nrm(ks[15], (D_MODEL, N_EXPERTS), D_MODEL ** -0.5),
        'b_router': nrm(ks[16], (N_EXPERTS,), 0.01),
        'w_gate': nrm(ks[17], (DEPTH, N_EXPERTS, D_MODEL, D_EXPERT), D_MODEL ** -0.5),
        'w_up': nrm(ks[18], (DEPTH, N_EXPERTS, D_MODEL, D_EXPERT), D_MODEL ** -0.5),
        'w_down': nrm(ks[19], (DEPTH, N_EXPERTS, D_EXPERT, D_MODEL), D_EXPERT ** -0.5),
        'final_g': 1.0 + nrm(ks[20], (D_MODEL,), 0.05),
    }

def reference(x, c, ctx, c_ctx, w_mod, b_mod, norm1_g, norm2_g, w_in, w_out, lb_logits, a_norm_g,
              rpb, w_pool, pool_scale, w_router, b_router, w_gate, w_up, w_down, final_g):
    last_even = ((DEPTH - 1) // 2) * 2
    lbs = hgrn_lower_bounds(lb_logits)
    cond_l = c[:, None, :]
    cond_c = c_ctx[None, None, :]
    h_c, h_l = ctx, x
    for layer in range(DEPTH):
        j = layer // 2
        ctx_in = layer <= last_even
        ctx_out = layer < last_even
        sh1, sc1, g1, sh2, sc2, g2 = adaln(cond_l, w_mod[layer], b_mod[layer])
        u_l = modulate(rms_norm(h_l, norm1_g[layer]), sh1, sc1)
        if ctx_in:
            mc = adaln(cond_c, w_mod[layer], b_mod[layer])
            u_c = modulate(rms_norm(h_c, norm1_g[layer]), mc[0], mc[1])
        if layer % 2 == 0:
            y_c, y_l = even_mixer(u_c, u_l, w_in[j], w_out[j], lbs[j], a_norm_g[j], rpb[j], ctx_out)
        else:
            y_l = pool_mixer(u_l, w_pool[j], pool_scale[j])
            y_c = pool_mixer(u_c, w_pool[j], pool_scale[j]) if ctx_out else None
        h_l = h_l + g1 * y_l
        h_l = h_l + g2 * grouped_moe(modulate(rms_norm(h_l, norm2_g[layer]), sh2, sc2),
                                     w_router, b_router, w_gate[layer], w_up[layer], w_down[layer])
        if ctx_out:
            h_c = h_c + mc[2] * y_c
            h_c = h_c + mc[5] * grouped_moe(modulate(rms_norm(h_c, norm2_g[layer]), mc[3], mc[4]),
                                            w_router, b_router, w_gate[layer], w_up[layer], w_down[layer])
    return rms_norm(h_l, final_g)


_drawn_inputs = setup_inputs


def setup_inputs(seed=0):
    import zlib

    import numpy as np

    out = dict(_drawn_inputs(seed))
    spreads = {}
    factors = {'a_norm_g': 3.051, 'rpb': 8.0}
    for name, (base, spread) in spreads.items():
        noise = np.random.default_rng([zlib.crc32(name.encode()), seed]).standard_normal(out[name].shape)
        drawn = base * np.exp(spread * noise) if base else spread * noise
        out[name] = jnp.asarray(drawn.astype(out[name].dtype))
    for name, factor in factors.items():
        out[name] = (out[name] * factor).astype(out[name].dtype)
    return out
```

```python
from contextlib import ExitStack

import numpy as np

import concourse.bass as bass
from concourse import mybir

F32 = mybir.dt.float32
U8 = mybir.dt.uint8
I32 = mybir.dt.int32
ACT = mybir.ActivationFunctionType
ALU = mybir.AluOpType
AX = mybir.AxisListType

P = 128
D = 1024
KC = D // P
T = 256
NT = T // P
F = 512
H = 4
DK = 128
BH = 8
DH = 64
GW = 64
RPB_R, RPB_C = 15, 31
NG, NE = 4, 4
EPS = 1e-6
CAP = 128
RING = 4
NEG = -1.0e30

C_ID, C_TRI, C_IOTA, C_SEL, C_ONES, C_COLM = 0, 128, 256, 384, 512, 640
C_W4, C_W16, C_E2, C_REV, C_N = 896, 900, 916, 918, 1046
LEVELS = (128, 64, 32, 16, 8, 4, 2, 1)
WINDOWS = (2, 4, 8, 16)


def shape_constants():
    cst = np.zeros((P, C_N), np.float32)
    i = np.arange(P)
    cst[:, C_ID:C_ID + P] = np.eye(P)
    cst[:, C_TRI:C_TRI + P] = i[:, None] < i[None, :]
    cst[:, C_IOTA:C_IOTA + P] = i[None, :]
    cst[:, C_SEL:C_SEL + P] = (i % 32 == 0)[:, None]
    cst[:, C_ONES:C_ONES + P] = 1.0
    col, key = i % GW, np.arange(T) % GW
    low = np.clip(col - 8, 0, GW - 16)
    inside = (key[None, :] >= low[:, None]) & (key[None, :] < low[:, None] + 16)
    backwards = i + GW - 1 - 2 * col
    cst[:, C_COLM:C_COLM + T] = np.where(inside, 0.0, NEG)[backwards]
    cst[i, C_REV + backwards] = 1.0
    cst[:, C_W4:C_W4 + 4] = np.arange(4, 0, -1)
    cst[:, C_W16:C_W16 + 16] = np.arange(16, 0, -1)
    cst[:, C_E2] = i % 32 == 0
    cst[:, C_E2 + 1] = i % 32 == 16
    masks = np.zeros((P, 15, P), np.float32)
    for n, m in enumerate(LEVELS[1:]):
        same = (i[:, None] // (2 * m)) == (i[None, :] // (2 * m))
        first, second = i % (2 * m) < m, i % (2 * m) >= m
        masks[:, 2 * n] = same & first[:, None] & second[None, :]
        masks[:, 2 * n + 1] = same & second[:, None] & first[None, :]
    masks[:, 14] = np.eye(P)
    t = np.arange(T)
    bands = np.zeros((T, len(WINDOWS), T), np.float32)
    for g, w in enumerate(WINDOWS):
        lo, hi = np.clip(t - w // 2, 0, T), np.clip(t + w // 2, 0, T)
        inside = (t[:, None] >= lo[None, :]) & (t[:, None] < hi[None, :])
        bands[:, g] = inside / (hi - lo).astype(np.float32)[None, :] - np.eye(T)
    return cst, masks, bands


Q_A, F_F, F_B, I_A, G_A, Q_B, K_B, V_B = range(8)
RING_A = (
    [("mod", 0, s) for s in range(4)]
    + [("in", I_A), ("in", F_F), ("in", F_B), ("in", Q_A), ("in", G_A), ("in", K_B)]
    + [("mod", 1, s) for s in range(4)] + [("in", Q_B)]
    + [("mod", 2, s) for s in range(4)] + [("in", V_B)]
    + [("mod", b, s) for b in (3, 4, 5) for s in range(4)]
    + [("out", 0), ("out", 1)]
)
MOE_ORDER = [("g", 0), ("u", 0), ("g", 1), ("u", 1), ("d", 0), ("g", 2), ("u", 2), ("d", 1),
             ("g", 3), ("u", 3), ("d", 2), ("d", 3)]
NM = len(MOE_ORDER)
N_MOE0 = len(RING_A)
N_POOL = N_MOE0 + NG * NM
N_MOE1 = N_POOL + 1
SLOT_A = {item: n for n, item in enumerate(RING_A)}

UNITS = ([(I_A, m) for m in range(4)] + [(F_F, m) for m in range(4)] + [(F_B, m) for m in range(4)]
         + [(Q_A, m) for m in range(4)] + [(G_A, m) for m in range(2)]
         + [(K_B, m) for m in range(4)] + [(Q_B, m) for m in range(4)] + [(V_B, m) for m in range(4)])
U_END = {p: max(n for n, u in enumerate(UNITS) if u[0] == p) + 1 for p in range(8)}
U_EARLY = U_END[G_A]
FILL = [[18, 19, 20], [21], ["m1"], [22, 23], [24, 25], ["m2"], [26], [27], [28], [29, "m3", "m4", "m5"]]
NLEV = len(LEVELS) + 1
PROJ_BANKS = (4, 5, 6)
MOD_BANK = 7


def build(nc, x, c, ctx, c_ctx, w_mod, b_mod, norm1_g, norm2_g, w_in, w_out, lb_logits, a_norm_g, rpb,
          w_pool, pool_scale, w_router, b_router, w_gate, w_up, w_down, final_g, cst_d, masks_d, bands_d, out):
    with ExitStack() as stack:
        def sb(name, shape, dt=F32):
            return stack.enter_context(nc.sbuf_tensor("sb_" + name, shape, dt))

        def sem(name):
            return stack.enter_context(nc.semaphore(name))

        ring = sb("ring", [P, RING, KC * F])
        h = sb("h", [P, NT, D])
        cst = sb("cst", [P, C_N])
        masks = sb("masks", [P, 15, P], U8)
        modrow = sb("modrow", [P, 6, F])
        prow = sb("prow", [40, P])
        parT = sb("parT", [P, 40])
        small = sb("small", [P, 400])
        flag = sb("flag", [1, 2], I32)
        KB = 256
        arena = sb("arena", [P, int(114.25 * KB)])
        psum = [stack.enter_context(nc.psum_tensor(f"bank{i}", [P, F], F32)) for i in range(8)]

        def area(kb, shape):
            n = int(np.prod(shape))
            a = arena[:, int(kb * KB):int(kb * KB) + n]
            if len(shape) == 2:
                return a.rearrange("p (a b) -> p a b", a=shape[0])
            if len(shape) == 3:
                return a.rearrange("p (a b c) -> p a b c", a=shape[0], b=shape[1])
            return a

        uT = area(0, [KC, 2 * T])
        lf = area(16, [8, 2 * T])
        kl = area(32, [8, T])
        kc = area(40, [8, T])
        X = area(48, [8, 2, T + 1])
        v = area(64.25, [2 * NT, F])
        qa = area(72.25, [H, T])
        gn = area(76.25, [NT, F])
        qb = area(80.25, [4, T])
        kbT = area(84.25, [4, 2 * T])
        vb = area(92.25, [2 * NT, F])
        S = area(100.25, [8, P])
        qt = area(104.25, [2, H, T])
        anorm = area(112.25, [F])
        junk = area(16, [D])
        masksf = area(48, [15, P])
        xnl = area(84.25, [NT, D])
        cx = area(92.25, [NT, D])
        csil = small[:, 0:256].rearrange("p (k n) -> p k n", k=KC)
        modT = area(20, [16, 2])
        A1T = area(21, [KC, 2])
        kcdT = area(16, [NT, 8, P])
        kcd = area(24, [8, T])
        Z = [area(16, [8, T]), area(24, [8, T])]
        ATd = area(40, [NT, H, P])
        ATo = area(44, [2, H, P])
        cat = area(0, [NT, D])
        catT = area(8, [KC, T])
        prob = [area(16, [F]), area(18, [F])]
        probT = [area(20, [F]), area(22, [F])]
        bias = [area(24 + n, [T]) for n in range(4)]
        ytmp = area(28, [2, F])
        MB = area(48, [6, D])
        yacc = area(0, [NT, D])
        u2 = area(8, [NT, D])
        u2T = area(16, [KC, T])
        xgT = area(24, [KC, CAP])
        yg = area(28, [D])
        sg = [area(32, [F]), area(34, [F])]
        hh = [area(36, [F]), area(38, [F])]
        hT = area(40, [4, P])
        Pg = area(42, [NT, P])
        PT = area(43, [NT, P])
        wr = area(44, [KC, 16])
        rs = area(44.5, [3 * KB])
        scl = area(72.25, [D])
        mtmp = area(76.25, [2 * D])
        bands = area(84.25, [NT, 4, T])
        pT = area(92.25, [8, T])
        brt = area(100.25, [16])

        ss = small[:, 256:260]
        ms = small[:, 260:264]
        rstd = small[:, 264:268]
        ssq = small[:, 268:276]
        rstdo = small[:, 276:284]
        nmax = small[:, 284:286]
        den = small[:, 286:302]
        rden = small[:, 302:318]
        half = small[:, 318:319]
        junk2 = [area(28 + 0.5 * n, [P]) for n in range(NT)]
        silc = small[:, 320:336]
        lbs = small[:, 336:352]
        lbw = small[:, 352:400]
        ident = cst[:, C_ID:C_ID + P]

        s_cst, s_par, s_x, s_cx = sem("s_cst"), sem("s_par"), sem("s_x"), sem("s_cx")
        s_bm, s_an = sem("s_bm"), sem("s_an")
        s_masks, masks_ready, lb_arg, lb_exp, g_sig, ro_rstd = (
            sem("s_masks"), sem("masks_ready"), sem("lb_arg"), sem("lb_exp"), sem("g_sig"), sem("ro_rstd"))
        loaded = [sem(f"loaded{i}") for i in range(RING)]
        modrow_zero, half_set = sem("modrow_zero"), sem("half_set")
        par_ps, par_T, sig_c, csil_ready = sem("par_ps"), sem("par_T"), sem("sig_c"), sem("csil_ready")
        mod_used, mod_rows, modT_ps, A1_ready = sem("mod_used"), sem("mod_rows"), sem("modT_ps"), sem("A1_ready")
        sq_done, ms_ready, rstd_ready, xn_ready = sem("sq_done"), sem("ms_ready"), sem("rstd_ready"), sem("xn_ready")
        uT_ps, uT_dve, uT_act = sem("uT_ps"), sem("uT_dve"), sem("uT_act")
        proj_done, proj_out, g_out = sem("proj_done"), sem("proj_out"), sem("g_out")
        f_ready, lf_ready, X_ready = sem("f_ready"), sem("lf_ready"), sem("X_ready")
        kcd_exp, kcd_ready, kcdT_ps, kcdT_ready = sem("kcd_exp"), sem("kcd_ready"), sem("kcdT_ps"), sem("kcdT_ready")
        S_ps, S_ready, qt_exp, qt_ready = sem("S_ps"), sem("S_ready"), sem("qt_exp"), sem("qt_ready")
        z_arg, z_exp, z_ready, gram, merged = sem("z_arg"), sem("z_exp"), sem("z_ready"), sem("gram"), sem("merged")
        atd_zero = sem("atd_zero")
        av_done, osq, ro_ready, a_ready = sem("av_done"), sem("osq"), sem("ro_ready"), sem("a_ready")
        b_dma, b_ready = [sem(f"b_dma{n}") for n in range(4)], sem("b_ready")
        sc_ps, sc_max, p_exp = sem("sc_ps"), sem("sc_max"), sem("p_exp")
        pT_ps, pT_ready, pv_done = sem("pT_ps"), sem("pT_ready"), sem("pv_done")
        cat_ready, catT_ps, catT_ready, y_done = sem("cat_ready"), sem("catT_ps"), sem("catT_ready"), sem("y_done")
        h1_ready = sem("h1_ready")
        bc_ps, bc_out, mb_dma = sem("bc_ps"), sem("bc_out"), sem("mb_dma")
        dve_chain, act_chain, pool_chain = sem("dve_chain"), sem("act_chain"), sem("pool_chain")
        s_rt, s_scl, s_out = sem("s_rt"), sem("s_scl"), sem("s_out")
        L = dict((n, sem(f"moe_{n}")) for n in (
            "sq", "ms", "rstd", "u2", "u2T_ps", "u2T", "logits", "scores", "gates", "ranks", "routed",
            "h_ready", "yacc0"))
        pool_u, pool_ps, pool_T, pool_y, pool_h, s_bands = (
            sem("pool_u"), sem("pool_ps"), sem("pool_T"), sem("pool_y"), sem("pool_h"), sem("s_bands"))
        fin_sq, fin_ms, fin_rstd, fin_out = sem("fin_sq"), sem("fin_ms"), sem("fin_rstd"), sem("fin_out")
        PASS = [dict((n, sem(f"pass{k}_{n}")) for n in (
            "p_ready", "xg_ps", "xg", "route_ps", "gs", "g_ps", "u_ps", "silu", "hid", "hT_ps", "hT", "d_done",
            "yg", "scat_ps", "scat")) for k in range(2)]
        PER_TILE = {"g_ps": NE, "u_ps": NE, "silu": NE, "hid": NE, "hT_ps": NE, "hT": NE, "d_done": NE}
        BY = {"pe": ("xg_ps", "route_ps", "g_ps", "u_ps", "hT_ps", "d_done", "scat_ps"),
              "act": ("xg", "silu", "hT", "yg"), "dve": ("p_ready", "gs", "hid", "scat")}
        ov_loaded = [sem(f"ov_loaded{i}") for i in range(RING)]
        ov_chain = sem("ov_chain")

        def count_skipped(eng, name):
            for n in BY[name]:
                eng.sem_inc(PASS[1][n], NG * PER_TILE.get(n, 1))

        def chunks(w):
            return w.rearrange("(k p) n -> p k n", p=P)

        def slot(n):
            return ring[:, n % RING, :]

        def landed(n):
            return 16 * (n // RING + 1)

        def used_a(n):
            kind = RING_A[n][0]
            if kind == "mod":
                return mod_used, 4 * RING_A[n][1] + RING_A[n][2] + 1
            if kind == "in":
                return proj_done, U_END[RING_A[n][1]]
            return y_done, 2 * RING_A[n][1] + 2

        def taken(u):
            if UNITS[u][0] == G_A:
                return g_out, UNITS[u][1] + 1
            return proj_out, sum(p != G_A for p, _ in UNITS[:u + 1])

        def used_moe(sems, t, j):
            t, j = t + j // NM, j % NM
            kind, e = MOE_ORDER[j]
            return {"g": sems["g_ps"], "u": sems["u_ps"], "d": sems["d_done"]}[kind], t * NE + (e + 1)

        def moe_src(l, t, j):
            kind, e = MOE_ORDER[j]
            w = {"g": w_gate, "u": w_up, "d": w_down}[kind]
            at = t * NE + e
            w = w[l, at] if isinstance(at, int) else w[l, bass.ds(at, 1)].rearrange("o a n -> (o a) n")
            return w.rearrange("(k p) n -> p k n", p=P)

        def slot_as(n, k):
            return slot(n).rearrange("p (k n) -> p k n", k=k)

        def linker(eng, s, base=0):
            count = [0]

            def link(ins):
                count[0] += 1
                ins.then_inc(s, 1)
                eng.wait_ge(s, base + count[0])
            link.count = count
            return link

        block = stack.enter_context(nc.Block())

        @block.sync
        def _(sp):
            sp.dma_start(h[:], x[0].rearrange("(t p) d -> p t d", p=P)).then_inc(s_x, 16)
            sp.dma_start(cx, ctx[0].rearrange("(t p) d -> p t d", p=P)).then_inc(s_cx, 16)
            for n, item in enumerate(RING_A):
                if n >= RING:
                    sp.wait_ge(*used_a(n - RING))
                if item[0] == "mod":
                    _, b, s = item
                    src = w_mod[b // 3, 256 * s:256 * s + 256, 2048 * (b % 3):2048 * (b % 3) + 2048]
                elif item[0] == "in":
                    src = w_in[0][:, item[1] * F:(item[1] + 1) * F]
                else:
                    src = w_out[0][:, item[1] * F:(item[1] + 1) * F]
                src = src.rearrange("(k p) n -> p k n", p=P)
                sp.dma_start(slot_as(n, src.shape[1]), src).then_inc(loaded[n % RING], 16)

            def stream_moe(l, n0, before):
                sems, tb = PASS[0], l * NG

                def load(t, j):
                    n = n0 + j
                    src = moe_src(l, t, j)
                    sp.dma_start(slot_as(n, src.shape[1]), src).then_inc(loaded[n % RING], 16)

                for j in range(RING):
                    sp.wait_ge(*before(n0 + j - RING))
                    load(0, j)
                with sp.Fori(0, NG - 1) as t:
                    for j in range(RING, NM):
                        sp.wait_ge(*used_moe(sems, tb + t, j - RING))
                        load(t, j)
                    for j in range(RING):
                        sp.wait_ge(*used_moe(sems, tb + t, NM + j - RING))
                        load(t + 1, j)
                for j in range(RING, NM):
                    sp.wait_ge(*used_moe(sems, tb + NG - 1, j - RING))
                    load(NG - 1, j)

            def overflow_moe(l):
                sp.wait_ge(L["routed"], l + 1)
                go = sp.value_load(flag[0:1, l:l + 1])
                sems, tb = PASS[1], l * NG
                with sp.If(go > 0):
                    sp.wait_ge(PASS[0]["d_done"], (tb + NG) * NE)
                    for j in range(RING):
                        src = moe_src(l, 0, j)
                        sp.dma_start(slot_as(j, src.shape[1]), src).then_inc(ov_loaded[j], 16)
                    with sp.Fori(0, NG - 1) as t:
                        for j in range(RING, NM + RING):
                            sp.wait_ge(*used_moe(sems, tb + t, j - RING))
                            src = moe_src(l, t if j < NM else t + 1, j % NM)
                            sp.dma_start(slot_as(j, src.shape[1]), src).then_inc(ov_loaded[j % RING], 16)
                    for j in range(RING, NM):
                        sp.wait_ge(*used_moe(sems, tb + NG - 1, j - RING))
                        src = moe_src(l, NG - 1, j)
                        sp.dma_start(slot_as(j, src.shape[1]), src).then_inc(ov_loaded[j % RING], 16)
                    sp.wait_ge(sems["d_done"], (tb + NG) * NE)
                with sp.Else():
                    for i in range(RING):
                        sp.sem_inc(ov_loaded[i], 16 * NG * NM // RING)

            stream_moe(0, N_MOE0, used_a)
            overflow_moe(0)

            def before_pool(n):
                return used_moe(PASS[0], NG - 1, n - N_MOE0 - (NG - 1) * NM)
            sp.wait_ge(*before_pool(N_POOL - RING))
            sp.dma_start(slot(N_POOL)[:, 0:8 * T].rearrange("p (g n) -> p g n", g=8),
                         w_pool[0].rearrange("g (c p) n -> p (g c) n", p=P)).then_inc(loaded[N_POOL % RING], 16)

            def before_moe1(n):
                return (pool_y, 4) if n == N_POOL else before_pool(n)
            stream_moe(1, N_MOE1, before_moe1)
            overflow_moe(1)
            for tt in range(NT):
                sp.wait_ge(fin_out, tt + 1)
                sp.dma_start(out[0, tt * P:(tt + 1) * P, :], mtmp[:, tt * D:(tt + 1) * D]).then_inc(s_out, 16)
            sp.wait_ge(s_out, 16 * NT)

        @block.tensor
        def _(pe):
            mm = nc.tensor.matmul
            tr = nc.tensor.transpose
            pe.wait_ge(s_cst, 16)
            pe.wait_ge(s_par, 64)
            tr(psum[0][:, 0:40], prow[:], cst[0:40, C_ID:C_ID + 40]).then_inc(par_ps, 1)

            def mod_bank(b):
                for s in range(4):
                    n = SLOT_A[("mod", b, s)]
                    pe.wait_ge(loaded[n % RING], landed(n))
                    w = slot(n).rearrange("p (k j n) -> p k j n", k=2, j=4)
                    for kk in range(2):
                        k = 2 * s + kk
                        for j in range(4):
                            last = mm(psum[MOD_BANK][32 * j:32 * j + 32, :], csil[:, k, :], w[:, kk, j, :],
                                      start=k == 0, stop=k == KC - 1, tile_position=(0, 32 * j),
                                      skip_group_check=True)
                    last.then_inc(mod_used, 1)

            pe.wait_ge(csil_ready, 1)
            mod_bank(0)
            pe.wait_ge(mod_rows, 1)
            for cc in range(4):
                for j in range(4):
                    last = mm(psum[2 + j][:, 2 * cc:2 * cc + 2], modrow[32 * j:32 * j + 32, 0, cc * P:(cc + 1) * P],
                              cst[32 * j:32 * j + 32, C_E2:C_E2 + 2], start=True, stop=True,
                              tile_position=(32 * j, 0))
            last.then_inc(modT_ps, 1)

            pe.wait_ge(xn_ready, 4)
            pe.wait_ge(A1_ready, 1)
            for k in range(KC):
                for tt in range(4):
                    src = xnl if tt < NT else cx
                    last = tr(psum[k][:, tt * P:(tt + 1) * P], src[:, tt % NT, k * P:(k + 1) * P], ident)
                last.then_inc(uT_ps, 1)
            pe.wait_ge(uT_dve, KC // 2)
            pe.wait_ge(uT_act, KC // 2)

            def proj_unit(u):
                p, m = UNITS[u]
                n = SLOT_A[("in", p)]
                bank = psum[PROJ_BANKS[u % 3]]
                if m == 0:
                    pe.wait_ge(loaded[n % RING], landed(n))
                if u >= 3:
                    pe.wait_ge(*taken(u - 3))
                w = slot_as(n, KC)
                for k in range(KC):
                    if p in (I_A, G_A, V_B):
                        last = mm(bank[:], uT[:, k, m * P:(m + 1) * P], w[:, k, :], start=k == 0, stop=k == KC - 1)
                    else:
                        cols = T if p in (Q_A, Q_B) else 2 * T
                        last = mm(bank[:, 0:cols], w[:, k, m * P:(m + 1) * P], uT[:, k, 0:cols],
                                  start=k == 0, stop=k == KC - 1)
                last.then_inc(proj_done, 1)

            for u in range(U_EARLY):
                proj_unit(u)

            def fill(n):
                for what in FILL[n]:
                    if isinstance(what, int):
                        proj_unit(what)
                    else:
                        b = int(what[1:])
                        pe.wait_ge(mod_rows, b)
                        mod_bank(b)

            pe.wait_ge(kcd_ready, 1)
            for st in range(NT):
                for i in range(8):
                    last = tr(psum[2 * st + i // 4][:, (i % 4) * P:(i % 4 + 1) * P], kcd[:, i, st * P:(st + 1) * P], ident)
            last.then_inc(kcdT_ps, 1)
            proj_unit(FILL[0][0])
            pe.wait_ge(kcdT_ready, 1)
            for i in range(8):
                for st in range(NT):
                    last = mm(psum[i // 4][:, (i % 4) * P:(i % 4 + 1) * P], kcdT[:, st, i, :],
                              v[:, NT + st, (i % H) * P:(i % H + 1) * P], start=st == 0, stop=st == NT - 1)
            last.then_inc(S_ps, 1)
            for u in FILL[0][1:]:
                proj_unit(u)

            pe.wait_ge(S_ready, 1)
            for lev in range(NLEV):
                if lev < len(LEVELS):
                    pe.wait_ge(z_ready, lev + 1)
                if lev:
                    pe.wait_ge(merged, lev)
                z = Z[lev % 2]
                if lev == 0:
                    for d in range(2):
                        for hd in range(H):
                            i = d * H + hd
                            last = mm(psum[d][:, hd * P:(hd + 1) * P], z[:, i, d * P:(d + 1) * P],
                                      z[:, i, (1 - d) * P:(2 - d) * P], start=True, stop=True)
                elif lev < len(LEVELS):
                    for d in range(2):
                        for tt in range(NT):
                            for hd in range(H):
                                zz = z[:, d * H + hd, tt * P:(tt + 1) * P]
                                last = mm(psum[2 * d + tt][:, hd * P:(hd + 1) * P], zz, zz, start=True, stop=True)
                else:
                    for tt in range(NT):
                        for hd in range(H):
                            for d in range(2):
                                last = mm(psum[tt][:, hd * P:(hd + 1) * P], kl[:, d * H + hd, tt * P:(tt + 1) * P],
                                          qa[:, hd, tt * P:(tt + 1) * P], start=d == 0, stop=d == 1)
                last.then_inc(gram, 1)
                fill(lev + 1)

            pe.wait_ge(merged, NLEV)
            pe.wait_ge(qt_ready, 1)
            for tt in range(NT):
                for hd in range(H):
                    o = psum[tt][:, hd * P:(hd + 1) * P]
                    mm(o, ATd[:, tt, hd, :], v[:, tt, hd * P:(hd + 1) * P], start=True, stop=False)
                    mm(o, ATo[:, 1 - tt, hd, :], v[:, 1 - tt, hd * P:(hd + 1) * P], start=False, stop=False)
                    mm(o, qt[:, 0, hd, tt * P:(tt + 1) * P], S[:, hd, :], start=False, stop=False)
                    last = mm(o, qt[:, 1, hd, tt * P:(tt + 1) * P], S[:, H + hd, :], start=False, stop=True)
                last.then_inc(av_done, 1)

            def attn_scores(i):
                hd, qi = i // NT, i % NT
                r = DH * (hd % 2)
                mm(psum[2 + i % 2][:], qb[r:r + DH, hd // 2, qi * P:(qi + 1) * P], kbT[r:r + DH, hd // 2, :],
                   start=True, stop=False)
                pe.wait_ge(b_ready, i + 1)
                mm(psum[2 + i % 2][:, 0:T], cst[:, C_REV:C_REV + P], bias[i % 4], start=False,
                   stop=True).then_inc(sc_ps, 1)

            pe.wait_ge(*taken(len(UNITS) - 1))
            pe.wait_ge(mod_rows, 6)
            attn_scores(0)
            attn_scores(1)
            for i in range(BH * NT):
                hd, qi = i // NT, i % NT
                pe.wait_ge(p_exp, i + 1)
                for cc in range(4):
                    last = tr(psum[4 + i % 2][:, cc * P:(cc + 1) * P], prob[i % 2][:, cc * P:(cc + 1) * P], ident)
                last.then_inc(pT_ps, 1)
                if i + 2 < BH * NT:
                    attn_scores(i + 2)
                pe.wait_ge(pT_ready, i + 1)
                for cc in range(4):
                    last = mm(psum[6 + qi][:, hd * DH:(hd + 1) * DH], probT[i % 2][:, cc * P:(cc + 1) * P],
                              vb[:, cc, hd * DH:(hd + 1) * DH], start=cc == 0, stop=cc == 3)
                last.then_inc(pv_done, 1)

            def broadcast(first):
                l, p = divmod(first, 6)
                for j in range(4):
                    last = mm(psum[j][:], cst[32 * j:32 * j + 32, C_SEL:C_SEL + P],
                              modrow[32 * j:32 * j + 32, 3 * l + p // 2, :], start=True, stop=True,
                              tile_position=(32 * j, 0))
                last.then_inc(bc_ps, 1)

            pe.wait_ge(a_ready, NT)
            broadcast(2)
            pe.wait_ge(bc_out, 1)
            pe.wait_ge(cat_ready, 1)
            for k in range(KC):
                for tt in range(NT):
                    last = tr(psum[k // 2][:, (k % 2) * T + tt * P:(k % 2) * T + (tt + 1) * P],
                              cat[:, tt, k * P:(k + 1) * P], ident)
            last.then_inc(catT_ps, 1)
            pe.wait_ge(catT_ready, 1)
            for nh in range(2):
                n = SLOT_A[("out", nh)]
                pe.wait_ge(loaded[n % RING], landed(n))
                w = slot_as(n, KC)
                for tt in range(NT):
                    for k in range(KC):
                        last = mm(psum[4 + 2 * nh + tt][:], catT[:, k, tt * P:(tt + 1) * P], w[:, k, :],
                                  start=k == 0, stop=k == KC - 1)
                    last.then_inc(y_done, 1)
            broadcast(4)

            def route(l):
                s = L
                pe.wait_ge(s["u2"], NT * (l + 1))
                pe.wait_ge(bc_out, 2 if l == 0 else 5)
                for k in range(KC):
                    for tt in range(NT):
                        last = tr(psum[k // 2][:, (k % 2) * T + tt * P:(k % 2) * T + (tt + 1) * P],
                                  u2[:, tt, k * P:(k + 1) * P], ident)
                last.then_inc(s["u2T_ps"], 1)
                pe.wait_ge(s["u2T"], l + 1)
                pe.wait_ge(s_rt, 32)
                for tt in range(NT):
                    for k in range(KC):
                        last = mm(psum[4][:, tt * 16:(tt + 1) * 16], u2T[:, k, tt * P:(tt + 1) * P], wr[:, k, :],
                                  start=k == 0, stop=k == KC - 1)
                last.then_inc(s["logits"], 1)
                pe.wait_ge(s["gates"], l + 1)
                G = rs[:, 0:8]
                mm(psum[5][:, 0:4], cst[:, C_TRI:C_TRI + P], G[:, 0:4], start=True, stop=True)
                mm(psum[5][:, 4:8], cst[:, C_ONES:C_ONES + P], G[:, 0:4], start=True, stop=False)
                mm(psum[5][:, 4:8], cst[:, C_TRI:C_TRI + P], G[:, 4:8], start=False, stop=True)
                mm(psum[5][:, 8:12], cst[:, C_ONES:C_ONES + P], G[:, 0:4], start=True, stop=False)
                mm(psum[5][:, 8:12], cst[:, C_ONES:C_ONES + P], G[:, 4:8], start=False, stop=True).then_inc(s["ranks"], 1)

            def experts(sems, tb, n0, loads, land0, gates_c):
                with pe.Fori(0, NG) as tile:
                    t = tile + tb
                    def arrived(j):
                        n = n0 + j
                        pe.wait_ge(loads[n % RING], tile * (16 * NM // RING) + (land0 + landed(n)))
                    pe.wait_ge(sems["scat"], t + 1)
                    pe.wait_ge(sems["p_ready"], t + 1)
                    for k in range(KC):
                        for tt in range(NT):
                            last = mm(psum[2 + k // 4][:, (k % 4) * P:(k % 4) * P + CAP], u2[:, tt, k * P:(k + 1) * P],
                                      Pg[:, tt, 0:CAP], start=tt == 0, stop=tt == NT - 1)
                    last.then_inc(sems["xg_ps"], 1)
                    for tt in range(NT):
                        tr(psum[7][0:CAP, P + tt * P:P + (tt + 1) * P], Pg[:, tt, 0:CAP], ident)
                    for tt in range(NT):
                        last = mm(psum[7][0:CAP, 0:4], Pg[:, tt, 0:CAP], gates_c[:, tt * 4:tt * 4 + 4],
                                  start=tt == 0, stop=tt == NT - 1)
                    last.then_inc(sems["route_ps"], 1)
                    pe.wait_ge(sems["xg"], t + 1)

                    def up_or_gate(j, e, bank, done):
                        arrived(j)
                        w = slot_as(n0 + j, KC)
                        for k in range(KC):
                            last = mm(bank[0:CAP, :], xgT[:, k, :], w[:, k, :], start=k == 0, stop=k == KC - 1)
                        last.then_inc(done, 1)

                    def hidden_T(e):
                        pe.wait_ge(sems["hid"], t * NE + (e + 1))
                        for cc in range(4):
                            last = tr(psum[4][:, cc * P:cc * P + CAP], hh[e % 2][0:CAP, cc * P:(cc + 1) * P],
                                      cst[0:CAP, C_ID:C_ID + CAP])
                        last.then_inc(sems["hT_ps"], 1)

                    def down(j, e):
                        arrived(j)
                        pe.wait_ge(sems["hT"], t * NE + (e + 1))
                        w = slot_as(n0 + j, 4)
                        for cc in range(4):
                            for nh in range(2):
                                last = mm(psum[5 + nh][0:CAP, :], hT[:, cc, 0:CAP], w[:, cc, nh * F:(nh + 1) * F],
                                          start=e == 0 and cc == 0, stop=e == NE - 1 and cc == 3)
                        last.then_inc(sems["d_done"], 1)

                    for e in range(NE):
                        if e >= 2:
                            pe.wait_ge(sems["hid"], t * NE + (e - 1))
                        up_or_gate(MOE_ORDER.index(("g", e)), e, psum[2 * (e % 2)], sems["g_ps"])
                        if e:
                            hidden_T(e - 1)
                        up_or_gate(MOE_ORDER.index(("u", e)), e, psum[2 * (e % 2) + 1], sems["u_ps"])
                        if e:
                            down(MOE_ORDER.index(("d", e - 1)), e - 1)
                    hidden_T(NE - 1)
                    down(MOE_ORDER.index(("d", NE - 1)), NE - 1)
                    pe.wait_ge(sems["gs"], t + 1)
                    pe.wait_ge(sems["yg"], t + 1)
                    for tt in range(NT):
                        for nh in range(2):
                            last = mm(psum[2 * tt + nh][:], PT[0:CAP, tt, :], yg[0:CAP, nh * F:(nh + 1) * F],
                                      start=True, stop=True)
                    last.then_inc(sems["scat_ps"], 1)

            def moe(l, n0):
                route(l)
                experts(PASS[0], l * NG, n0, loaded, 0, rs[:, 8:16])
                pe.wait_ge(L["routed"], l + 1)
                go = pe.value_load(flag[0:1, l:l + 1])
                with pe.If(go > 0):
                    experts(PASS[1], l * NG, 0, ov_loaded, l * 16 * NG * NM // RING, rs[:, 8:16])
                    pe.wait_ge(PASS[1]["scat"], (l + 1) * NG + 1)
                with pe.Else():
                    count_skipped(pe, "pe")

            moe(0, N_MOE0)

            pe.wait_ge(L["h_ready"], 1)
            for n, first in enumerate((6, 8, 10)):
                if n:
                    pe.wait_ge(bc_out, 2 + n)
                broadcast(first)
            pe.wait_ge(pool_u, NT)
            pe.wait_ge(bc_out, 5)
            pe.wait_ge(s_bands, 16)
            for g in range(4):
                for cc in range(2):
                    k = 2 * g + cc
                    for st in range(NT):
                        last = mm(psum[g][:, cc * T:(cc + 1) * T], u2[:, st, k * P:(k + 1) * P], bands[:, st, g, :],
                                  start=st == 0, stop=st == NT - 1)
            last.then_inc(pool_ps, 1)
            pe.wait_ge(pool_T, 1)
            pe.wait_ge(loaded[N_POOL % RING], landed(N_POOL))
            w = slot(N_POOL)[:, 0:8 * T].rearrange("p (g n) -> p g n", g=8)
            for tt in range(NT):
                for gh in range(2):
                    for g in (2 * gh, 2 * gh + 1):
                        for cc in range(2):
                            last = mm(psum[4 + 2 * tt + gh][:, (g % 2) * T:(g % 2 + 1) * T],
                                      pT[:, 2 * g + cc, tt * P:(tt + 1) * P], w[:, 2 * g + cc, :],
                                      start=cc == 0, stop=cc == 1)
                    last.then_inc(pool_y, 1)
            pe.wait_ge(pool_h, 1)
            moe(1, N_MOE1)

        @block.scalar
        def _(act):
            link = linker(act, act_chain)
            A = nc.scalar.activation
            act.dma_start(cst[:], cst_d).then_inc(s_cst, 16)
            act.dma_start(prow[0:8, :], c.rearrange("b (k p) -> (b k) p", p=P)).then_inc(s_par, 16)
            act.dma_start(prow[8:16, :], c_ctx.rearrange("(k p) -> k p", p=P)).then_inc(s_par, 16)
            act.dma_start(prow[16:24, :], norm1_g[0].rearrange("(k p) -> k p", p=P)).then_inc(s_par, 16)
            act.dma_start(prow[24:40, :], lb_logits.rearrange("l d (h p) -> (l d h) p", p=P)).then_inc(s_par, 16)
            act.wait_ge(par_T, 1)
            A(silc, parT[:, 0:16], ACT.Sigmoid).then_inc(sig_c, 1)
            act.wait_ge(lb_arg, 1)
            A(lbw[:, 0:16], lbw[:, 0:16], ACT.Exp).then_inc(lb_exp, 1)
            act.wait_ge(s_x, 16)
            act.wait_ge(s_cx, 16)
            for tt in range(4):
                link(A(junk, h[:, tt] if tt < NT else cx[:, tt - NT], ACT.Square, accum_out=ss[:, tt:tt + 1]))
            A(half, cst[:, C_ONES:C_ONES + 1], ACT.Copy, scale=-0.5).then_inc(sq_done, 1)
            act.wait_ge(A1_ready, 1)
            for k in range(1, KC, 2):
                act.wait_ge(uT_ps, k + 1)
                for w in range(2):
                    last = A(uT[:, k, w * T:(w + 1) * T], psum[k][:, w * T:(w + 1) * T], ACT.Identity,
                             bias=modT[:, k, w:w + 1], scale=A1T[:, k, w:w + 1])
                last.then_inc(uT_act, 1)
            act.wait_ge(uT_dve, KC // 2)

            def take(u):
                p, m = UNITS[u]
                bank = psum[PROJ_BANKS[u % 3]]
                act.wait_ge(proj_done, u + 1)
                if p == I_A:
                    ins = A(v[:, m, :], bank[:], ACT.Copy)
                elif p in (F_F, F_B):
                    ins = A(lf[:, (p - F_F) * H + m, :], bank[:], ACT.Sigmoid)
                elif p == Q_A:
                    ins = A(qa[:, m, :], bank[:, 0:T], ACT.Copy, scale=float(np.float32(DK ** -0.5)))
                elif p == G_A:
                    A(gn[:, m, :], bank[:], ACT.Sigmoid).then_inc(g_sig, 1)
                    return
                elif p == K_B:
                    ins = A(kbT[:, m, :], bank[:], ACT.Copy)
                elif p == Q_B:
                    ins = A(qb[:, m, :], bank[:, 0:T], ACT.Copy, scale=DH ** -0.5)
                else:
                    ins = A(vb[:, m, :], bank[:], ACT.Copy)
                ins.then_inc(proj_out, 1)

            for u in range(U_EARLY):
                take(u)
            for d in range(2):
                act.wait_ge(f_ready, d + 1)
                A(lf[:, d * H:(d + 1) * H, :], lf[:, d * H:(d + 1) * H, :], ACT.Ln).then_inc(lf_ready, 1)
            act.wait_ge(X_ready, 2)
            for hd in range(H):
                A(kcd[:, hd, :], X[:, hd, 1, 1:T + 1], ACT.Exp, bias=X[:, hd, 1, T:T + 1], scale=-1.0)
            A(kcd[:, H:2 * H, :], X[:, H:2 * H, 1, 0:T], ACT.Exp).then_inc(kcd_exp, 1)
            A(qt[:, 0], X[:, 0:H, 0, 1:T + 1], ACT.Exp)
            for hd in range(H):
                last = A(qt[:, 1, hd, :], X[:, H + hd, 0, 0:T], ACT.Exp, bias=X[:, H + hd, 0, T:T + 1], scale=-1.0)
            last.then_inc(qt_exp, 1)
            for u in FILL[0]:
                take(u)
            for lev in range(NLEV):
                if lev < len(LEVELS):
                    act.wait_ge(z_arg, lev + 1)
                    A(Z[lev % 2], Z[lev % 2], ACT.Exp).then_inc(z_exp, 1)
                if lev:
                    for u in FILL[lev]:
                        if isinstance(u, int):
                            take(u)
            for u in FILL[NLEV]:
                if isinstance(u, int):
                    take(u)
            for tt in range(NT):
                act.wait_ge(av_done, tt + 1)
                for hd in range(H):
                    ins = A(junk2[tt], psum[tt][:, hd * P:(hd + 1) * P], ACT.Square,
                            accum_out=ssq[:, tt * H + hd:tt * H + hd + 1])
                    if hd < H - 1:
                        link(ins)
                ins.then_inc(osq, 1)
            for i in range(BH * NT):
                act.wait_ge(sc_max, i + 1)
                A(prob[i % 2], psum[2 + i % 2][:], ACT.Exp, bias=nmax[:, i % 2:i % 2 + 1],
                  accum_out=den[:, i:i + 1]).then_inc(p_exp, 1)
                act.wait_ge(pT_ps, i + 1)
                A(probT[i % 2], psum[4 + i % 2][:], ACT.Copy).then_inc(pT_ready, 1)
            act.wait_ge(catT_ps, 1)
            for n in range(4):
                last = A(catT[:, 2 * n:2 * n + 2, :], psum[n][:].rearrange("p (k t) -> p k t", k=2), ACT.Copy)
            last.then_inc(catT_ready, 1)

            def stats(ready, count, sq):
                act.wait_ge(ready, count)
                for tt in range(NT):
                    ins = A(area(24, [D]), h[:, tt], ACT.Square, accum_out=ss[:, tt:tt + 1])
                    if tt < NT - 1:
                        link(ins)
                ins.then_inc(sq, 1)

            def route(l):
                s = L
                act.wait_ge(s["u2T_ps"], l + 1)
                for n in range(4):
                    last = A(u2T[:, 2 * n:2 * n + 2, :], psum[n][:].rearrange("p (k t) -> p k t", k=2), ACT.Copy)
                last.then_inc(s["u2T"], 1)
                act.wait_ge(s["logits"], l + 1)
                A(rs[:, 16:48], psum[4][:, 0:32], ACT.Sigmoid).then_inc(s["scores"], 1)

            def experts(sems, tb):
                with act.Fori(0, NG) as tile:
                    t = tile + tb
                    act.wait_ge(sems["xg_ps"], t + 1)
                    for n in range(2):
                        last = A(xgT[:, 4 * n:4 * n + 4, :], psum[2 + n][:].rearrange("p (k n) -> p k n", k=4)[:, :, 0:CAP],
                                 ACT.Copy)
                    last.then_inc(sems["xg"], 1)
                    for e in range(NE):
                        act.wait_ge(sems["g_ps"], t * NE + (e + 1))
                        A(sg[e % 2][0:CAP], psum[2 * (e % 2)][0:CAP, :], ACT.Silu).then_inc(sems["silu"], 1)
                        if e:
                            act.wait_ge(sems["hT_ps"], t * NE + e)
                            A(hT[:, :, 0:CAP], psum[4][:].rearrange("p (c n) -> p c n", c=4)[:, :, 0:CAP],
                              ACT.Copy).then_inc(sems["hT"], 1)
                    act.wait_ge(sems["hT_ps"], t * NE + NE)
                    A(hT[:, :, 0:CAP], psum[4][:].rearrange("p (c n) -> p c n", c=4)[:, :, 0:CAP],
                      ACT.Copy).then_inc(sems["hT"], 1)
                    act.wait_ge(sems["d_done"], t * NE + NE)
                    for nh in range(2):
                        last = A(yg[0:CAP, nh * F:(nh + 1) * F], psum[5 + nh][0:CAP, :], ACT.Copy)
                    last.then_inc(sems["yg"], 1)

            def moe(l):
                route(l)
                experts(PASS[0], l * NG)
                act.wait_ge(L["routed"], l + 1)
                go = act.value_load(flag[0:1, l:l + 1])
                with act.If(go > 0):
                    experts(PASS[1], l * NG)
                    act.wait_ge(PASS[1]["scat"], (l + 1) * NG + 1)
                with act.Else():
                    count_skipped(act, "act")

            stats(h1_ready, 4, L["sq"])
            moe(0)
            stats(L["h_ready"], 1, fin_sq)
            stats(pool_h, 1, L["sq"])
            moe(1)
            stats(L["h_ready"], 2, fin_sq)

        @block.vector
        def _(dve):
            V = nc.vector
            link = linker(dve, dve_chain)
            dve.wait_ge(par_ps, 1)
            V.tensor_copy(parT[:], psum[0][:, 0:40]).then_inc(par_T, 1)
            dve.wait_ge(par_T, 1)
            l0, l1 = parT[:, 24:32], parT[:, 32:40]
            link(V.tensor_tensor(lbw[:, 16:24], l0, l1, ALU.max))
            V.tensor_tensor(lbw[:, 0:8], l0, lbw[:, 16:24], ALU.subtract)
            V.tensor_tensor(lbw[:, 8:16], l1, lbw[:, 16:24], ALU.subtract).then_inc(lb_arg, 1)
            dve.wait_ge(sig_c, 1)
            link(V.tensor_tensor(silc, silc, parT[:, 0:16], ALU.mult))
            for w in range(2):
                last = V.tensor_copy(csil[:, :, 16 * w:16 * w + 16],
                                     silc[:, 8 * w:8 * w + 8].unsqueeze(2).to_broadcast([P, KC, 16]))
            last.then_inc(csil_ready, 1)
            dve.wait_ge(lb_exp, 1)
            link(V.tensor_tensor(lbw[:, 16:24], lbw[:, 0:8], lbw[:, 8:16], ALU.add))
            link(V.reciprocal(lbw[:, 24:32], lbw[:, 16:24]))
            V.tensor_tensor(lbw[:, 32:40], lbw[:, 0:8], lbw[:, 24:32], ALU.mult)
            link(V.tensor_tensor(lbw[:, 40:48], lbw[:, 8:16], lbw[:, 24:32], ALU.mult))
            link(V.tensor_tensor(lbs[:, 0:8], lbw[:, 32:40], lbw[:, 40:48], ALU.add))
            link(V.tensor_tensor(lbs[:, 0:8], lbs[:, 0:8], lbw[:, 32:40], ALU.subtract))
            link(V.tensor_scalar(lbs[:, 8:16], lbs[:, 0:8], -1.0, 1.0, ALU.mult, ALU.add))
            dve.wait_ge(sq_done, 1)
            V.tensor_scalar(ms, ss, 1.0 / D, EPS, ALU.mult, ALU.add).then_inc(ms_ready, 1)
            dve.wait_ge(rstd_ready, 1)
            for tt in range(4):
                src = h[:, tt] if tt < NT else cx[:, tt - NT]
                dst = xnl[:, tt] if tt < NT else cx[:, tt - NT]
                V.tensor_scalar(dst, src, rstd[:, tt:tt + 1], None, ALU.mult).then_inc(xn_ready, 1)

            def mod_rows_out(b):
                dve.wait_ge(mod_used, 4 * b + 4)
                dve.wait_ge(s_bm, 48)
                V.tensor_tensor(modrow[:, b, :], psum[MOD_BANK][:], modrow[:, b, :], ALU.add).then_inc(mod_rows, 1)

            mod_rows_out(0)
            dve.wait_ge(modT_ps, 1)
            for j in range(4):
                last = V.tensor_copy(modT[:, 4 * j:4 * j + 4, :], psum[2 + j][:, 0:8].rearrange("p (a b) -> p a b", a=4))
            link(last)
            V.scalar_tensor_tensor(A1T, modT[:, KC:2 * KC, :], 1.0,
                                   parT[:, 16:24].unsqueeze(2).to_broadcast([P, KC, 2]), ALU.add,
                                   ALU.mult).then_inc(A1_ready, 1)
            dve.wait_ge(A1_ready, 1)
            for k in range(0, KC, 2):
                dve.wait_ge(uT_ps, k + 1)
                for w in range(2):
                    last = V.tensor_scalar(uT[:, k, w * T:(w + 1) * T], psum[k][:, w * T:(w + 1) * T],
                                           A1T[:, k, w:w + 1], modT[:, k, w:w + 1], ALU.mult, ALU.add)
                last.then_inc(uT_dve, 1)
            dve.wait_ge(uT_dve, KC // 2)
            dve.wait_ge(uT_act, KC // 2)
            for d in range(2):
                for hd in range(H):
                    i = d * H + hd
                    dve.wait_ge(proj_out, 4 + i + 1)
                    link(V.tensor_scalar(lf[:, i, :], lf[:, i, :], lbs[:, 8 + i:9 + i], lbs[:, i:i + 1], ALU.mult, ALU.add))
                    V.tensor_scalar(kl[:, i, :], lf[:, i, 0:T], -1.0, 1.0, ALU.mult, ALU.add)
                    last = V.tensor_scalar(kc[:, i, :], lf[:, i, T:2 * T], -1.0, 1.0, ALU.mult, ALU.add)
                last.then_inc(f_ready, 1)
            dve.wait_ge(s_an, 16)
            for m in range(NT):
                dve.wait_ge(proj_done, U_END[Q_A] + m + 1)
                dve.wait_ge(g_sig, m + 1)
                V.tensor_tensor(gn[:, m, :], psum[PROJ_BANKS[(U_END[Q_A] + m) % 3]][:], gn[:, m, :],
                                ALU.mult).then_inc(g_out, 1)
                dve.wait_ge(g_out, m + 1)
                link(V.tensor_tensor(gn[:, m, :], gn[:, m, :], anorm, ALU.mult))
            dve.wait_ge(masks_ready, 1)
            link(V.memset(X[:, :, :, 0:1], 0.0))
            for d in range(2):
                dve.wait_ge(lf_ready, d + 1)
                for hd in range(H):
                    i = d * H + hd
                    for w in range(2):
                        last = V.tensor_tensor_scan(X[:, i, w, 1:T + 1], cst[:, C_ONES:C_ONES + 1].to_broadcast([P, T]),
                                                    lf[:, i, w * T:(w + 1) * T], 0.0, ALU.mult, ALU.add)
                last.then_inc(X_ready, 1)
            dve.wait_ge(X_ready, 2)
            dve.wait_ge(kcd_exp, 1)
            V.tensor_tensor(kcd, kcd, kc, ALU.mult).then_inc(kcd_ready, 1)
            dve.wait_ge(qt_exp, 1)
            for d in range(2):
                last = V.tensor_tensor(qt[:, d], qt[:, d], qa, ALU.mult)
            last.then_inc(qt_ready, 1)
            dve.wait_ge(kcdT_ps, 1)
            for n in range(4):
                last = V.tensor_copy(kcdT[:, n // 2, (n % 2) * 4:(n % 2) * 4 + 4, :],
                                     psum[n][:].rearrange("p (a b) -> p a b", a=4))
            last.then_inc(kcdT_ready, 1)
            dve.wait_ge(S_ps, 1)
            for n in range(2):
                last = V.tensor_copy(S[:, 4 * n:4 * n + 4, :], psum[n][:].rearrange("p (a b) -> p a b", a=4))
            last.then_inc(S_ready, 1)

            def halves(a, m, second):
                b = a.rearrange("p h (b f m) -> p h b f m", f=2, m=m)
                return b[:, :, :, 1, :] if second else b[:, :, :, 0, :]

            def level_args(lev):
                m = LEVELS[lev]
                if lev >= 2:
                    dve.wait_ge(gram, lev - 1)
                for d in range(2):
                    x0 = X[:, d * H:(d + 1) * H, 0, 0:T]
                    x1 = X[:, d * H:(d + 1) * H, 0, 1 - d:1 - d + T]
                    mid = halves(x0, m, True)[:, :, :, 0:1].to_broadcast([P, H, P // m, m])
                    z = Z[lev % 2][:, d * H:(d + 1) * H, :]
                    V.tensor_tensor(halves(z, m, False), mid, halves(x1, m, False), ALU.subtract)
                    last = V.tensor_tensor(halves(z, m, True), halves(x1, m, True), mid, ALU.subtract)
                last.then_inc(z_arg, 1)

            def level_mult(lev):
                m = LEVELS[lev]
                dve.wait_ge(z_exp, lev + 1)
                for d in range(2):
                    z = Z[lev % 2][:, d * H:(d + 1) * H, :]
                    kk = kl[:, d * H:(d + 1) * H, :]
                    for second in (False, True):
                        src = qa if second == (d == 0) else kk
                        last = V.tensor_tensor(halves(z, m, second), halves(z, m, second), halves(src, m, second), ALU.mult)
                last.then_inc(z_ready, 1)

            def level_merge(lev):
                dve.wait_ge(gram, lev + 1)
                if lev == 0:
                    dve.wait_ge(atd_zero, 1)
                    V.tensor_copy(ATo[:, 0], psum[0][:].rearrange("p (a b) -> p a b", a=H))
                    V.tensor_copy(ATo[:, 1], psum[1][:].rearrange("p (a b) -> p a b", a=H)).then_inc(merged, 1)
                    return
                diag = lev == NLEV - 1
                pairs = [(0, tt) for tt in range(NT)] if diag else [(d, tt) for d in range(2) for tt in range(NT)]
                for n, (d, tt) in enumerate(pairs):
                    mask = masks[:, 14 if diag else 2 * (lev - 1) + d, :].unsqueeze(1).to_broadcast([P, H, P])
                    ins = V.copy_predicated(ATd[:, tt], mask, psum[2 * d + tt][:].rearrange("p (a b) -> p a b", a=H))
                    if n < len(pairs) - 1:
                        link(ins)
                ins.then_inc(merged, 1)
                dve.wait_ge(merged, lev + 1)

            level_args(0)
            level_mult(0)
            for lev in range(NLEV):
                if lev + 1 < len(LEVELS):
                    level_args(lev + 1)
                if lev:
                    for what in FILL[lev]:
                        if isinstance(what, str):
                            mod_rows_out(int(what[1:]))
                level_merge(lev)
                if lev + 1 < len(LEVELS):
                    level_mult(lev + 1)
            for what in FILL[NLEV]:
                if isinstance(what, str):
                    mod_rows_out(int(what[1:]))
            for tt in range(NT):
                dve.wait_ge(osq, tt + 1)
                V.tensor_scalar(ssq[:, tt * H:(tt + 1) * H], ssq[:, tt * H:(tt + 1) * H], 1.0 / DK, EPS, ALU.mult,
                                ALU.add).then_inc(ro_ready, 1)
            for tt in range(NT):
                dve.wait_ge(ro_rstd, tt + 1)
                for hd in range(H):
                    last = V.scalar_tensor_tensor(cat[:, tt, hd * P:(hd + 1) * P], psum[tt][:, hd * P:(hd + 1) * P],
                                                  rstdo[:, tt * H + hd:tt * H + hd + 1],
                                                  gn[:, tt, hd * P:(hd + 1) * P], ALU.mult, ALU.mult)
                last.then_inc(a_ready, 1)
            for i in range(BH * NT):
                bank = psum[2 + i % 2]
                dve.wait_ge(sc_ps, i + 1)
                V.tensor_reduce(nmax[:, i % 2:i % 2 + 1], bank[:], axis=AX.X, op=ALU.max, negate=True).then_inc(sc_max, 1)
            dve.wait_ge(pv_done, BH * NT)
            link(V.reciprocal(rden, den))
            for tt in range(NT):
                r = rden.rearrange("p (h q) -> p h q", q=NT)[:, :, tt:tt + 1].to_broadcast([P, BH, DH])
                last = V.tensor_tensor(cat[:, tt, F:2 * F].rearrange("p (h d) -> p h d", h=BH),
                                       psum[6 + tt][:].rearrange("p (h d) -> p h d", h=BH), r, ALU.mult)
            last.then_inc(cat_ready, 1)

            def broadcast_out(n, first):
                dve.wait_ge(bc_ps, n + 1)
                for j in range(4):
                    p = first % 6 + j // 2
                    dst = MB[:, p, (j % 2) * F:(j % 2 + 1) * F]
                    if p in (1, 4):
                        dve.wait_ge(mb_dma, 16 if first < 6 else 48)
                        last = V.scalar_tensor_tensor(dst, psum[j][:], 1.0, dst, ALU.add, ALU.mult)
                    else:
                        last = V.tensor_copy(dst, psum[j][:])
                last.then_inc(bc_out, 1)
                dve.wait_ge(bc_out, n + 1)

            broadcast_out(0, 2)
            for n in range(4):
                nh, tt = n // 2, n % 2
                dve.wait_ge(y_done, n + 1)
                link(V.tensor_tensor(ytmp[:, n % 2, :], psum[4 + n][:], MB[:, 2, nh * F:(nh + 1) * F], ALU.mult))
                V.tensor_tensor(h[:, tt, nh * F:(nh + 1) * F], h[:, tt, nh * F:(nh + 1) * F], ytmp[:, n % 2, :],
                                ALU.add).then_inc(h1_ready, 1)
            broadcast_out(1, 4)

            def mean_square(sq, count, out_sem):
                dve.wait_ge(sq, count)
                V.tensor_scalar(ms[:, 0:NT], ss[:, 0:NT], 1.0 / D, EPS, ALU.mult, ALU.add).then_inc(out_sem, 1)

            def norm_mod(rstd_sem, count, gain, shift, done, done_count):
                dve.wait_ge(rstd_sem, count)
                for tt in range(NT):
                    link(V.scalar_tensor_tensor(u2[:, tt], h[:, tt], rstd[:, tt:tt + 1], MB[:, gain], ALU.mult, ALU.mult))
                    V.tensor_tensor(u2[:, tt], u2[:, tt], MB[:, shift], ALU.add).then_inc(done, 1)
                dve.wait_ge(done, done_count)

            G, gc, s_, sbi = rs[:, 0:8], rs[:, 8:16], rs[:, 16:48], rs[:, 48:80]
            d1, d2, d3 = rs[:, 80:104], rs[:, 104:120], rs[:, 120:128]
            gsc, gm, w4 = rs[:, 128:136], rs[:, 136:138], rs[:, 138:146]
            m16, o1, m2 = rs[:, 146:178], rs[:, 178:210], rs[:, 210:242]
            t32, red, gts = rs[:, 242:274], rs[:, 274:276], rs[:, 276:308]
            rk, cnt, rg = rs[:, 308:316], rs[:, 316:318], rs[:, 320:328]
            gslot = rs[:, 328:332]

            def v3(a, b, c_):
                return a.rearrange("p (a b c) -> p a b c", a=NT, b=b, c=c_)

            def v2(a, b):
                return a.rearrange("p (a b) -> p a b", a=NT, b=b)

            def bc1(a, n):
                return a.unsqueeze(2).to_broadcast([P, NT, n])

            def first_max(dst, src, n, weights, tmp):
                link(V.tensor_reduce(red, v2(src, n), axis=AX.X, op=ALU.max))
                link(V.tensor_tensor(v2(tmp, n), v2(src, n), bc1(red, n), ALU.is_equal))
                link(V.tensor_tensor(v2(tmp, n), v2(tmp, n), weights.unsqueeze(1).to_broadcast([P, NT, n]), ALU.mult))
                link(V.tensor_reduce(red, v2(tmp, n), axis=AX.X, op=ALU.max))
                link(V.tensor_tensor(v2(dst, n), v2(tmp, n), bc1(red, n), ALU.is_equal))

            def route(l):
                s = L
                dve.wait_ge(s["scores"], l + 1)
                link(V.tensor_tensor(v2(sbi, 16), v2(s_, 16), brt.unsqueeze(1).to_broadcast([P, NT, 16]), ALU.add))
                a = v3(sbi, NG, NE)
                V.tensor_tensor(v3(d1, NG, 3), a[:, :, :, 0:3], a[:, :, :, 1:4], ALU.add)
                V.tensor_tensor(v3(d2, NG, 2), a[:, :, :, 0:2], a[:, :, :, 2:4], ALU.add)
                link(V.tensor_tensor(v3(d3, NG, 1), a[:, :, :, 0:1], a[:, :, :, 3:4], ALU.add))
                V.tensor_reduce(v2(gsc, NG), v3(d1, NG, 3), axis=AX.X, op=ALU.max)
                link(V.tensor_reduce(v2(w4, NG), v3(d2, NG, 2), axis=AX.X, op=ALU.max))
                link(V.tensor_tensor(gsc, gsc, w4, ALU.max))
                link(V.tensor_tensor(gsc, gsc, d3, ALU.max))
                first_max(G, gsc, NG, cst[:, C_W4:C_W4 + 4], w4)
                in_g = v2(G, NG).unsqueeze(3).to_broadcast([P, NT, NG, NE])
                link(V.tensor_scalar(w4, G, -NEG, NEG, ALU.mult, ALU.add))
                link(V.tensor_tensor(v3(m16, NG, NE), v3(sbi, NG, NE), in_g, ALU.mult))
                link(V.tensor_tensor(v3(m16, NG, NE), v3(m16, NG, NE),
                                     v2(w4, NG).unsqueeze(3).to_broadcast([P, NT, NG, NE]), ALU.add))
                first_max(o1, m16, 16, cst[:, C_W16:C_W16 + 16], t32)
                link(V.scalar_tensor_tensor(m16, o1, 2 * NEG, m16, ALU.mult, ALU.add))
                first_max(m2, m16, 16, cst[:, C_W16:C_W16 + 16], t32)
                link(V.tensor_tensor(o1, o1, m2, ALU.add))
                link(V.tensor_tensor(gts, o1, s_, ALU.mult))
                link(V.tensor_reduce(red, v2(gts, 16), axis=AX.X, op=ALU.add))
                link(V.reciprocal(red, red))
                link(V.tensor_tensor(v2(gts, 16), v2(gts, 16), bc1(red, 16), ALU.mult))
                V.tensor_reduce(v2(gc, NE), v3(gts, NG, NE).rearrange("p a g e -> p a e g"), axis=AX.X,
                                op=ALU.add).then_inc(s["gates"], 1)
                dve.wait_ge(s["ranks"], l + 1)
                link(V.tensor_scalar(rk, psum[5][:, 0:8], 1.0, None, ALU.add))
                link(V.tensor_tensor(rk, rk, G, ALU.mult))
                V.tensor_scalar(rg, rk, -1.0, None, ALU.add)
                link(V.tensor_reduce(cnt[:, 0:1], psum[5][:, 8:12], axis=AX.X, op=ALU.max))
                V.tensor_scalar(flag[0:1, l:l + 1], cnt[0:1, 0:1], CAP + 0.5, None, ALU.is_gt).then_inc(s["routed"], 1)
                dve.wait_ge(s["routed"], l + 1)

            def experts(sems, tb):
                with dve.Fori(0, NG) as tile:
                    t = tile + tb
                    for tt in range(NT):
                        last = V.tensor_scalar(Pg[:, tt, :], cst[:, C_IOTA:C_IOTA + P], rg[:, bass.ds(tile + 4 * tt, 1)], None,
                                               ALU.is_equal)
                    last.then_inc(sems["p_ready"], 1)
                    dve.wait_ge(sems["route_ps"], t + 1)
                    V.tensor_copy(gslot[0:CAP], psum[7][0:CAP, 0:4])
                    V.tensor_copy(PT[0:CAP], psum[7][0:CAP, P:3 * P].rearrange("p (a b) -> p a b", a=NT)).then_inc(sems["gs"], 1)
                    dve.wait_ge(sems["gs"], t + 1)
                    for e in range(NE):
                        dve.wait_ge(sems["silu"], t * NE + (e + 1))
                        dve.wait_ge(sems["u_ps"], t * NE + (e + 1))
                        V.scalar_tensor_tensor(hh[e % 2][0:CAP], sg[e % 2][0:CAP], gslot[0:CAP, e:e + 1],
                                               psum[2 * (e % 2) + 1][0:CAP, :], ALU.mult, ALU.mult).then_inc(sems["hid"], 1)
                    dve.wait_ge(sems["scat_ps"], t + 1)
                    for tt in range(NT):
                        for nh in range(2):
                            last = V.tensor_tensor(yacc[:, tt, nh * F:(nh + 1) * F], psum[2 * tt + nh][:],
                                                   yacc[:, tt, nh * F:(nh + 1) * F], ALU.add)
                    last.then_inc(sems["scat"], 1)
                    dve.wait_ge(sems["scat"], t + 2)

            def moe(l):
                route(l)
                dve.wait_ge(L["yacc0"], l + 1)
                if l == 0:
                    for k in range(2):
                        dve.sem_inc(PASS[k]["scat"], 1)
                experts(PASS[0], l * NG)
                go = dve.value_load(flag[0:1, l:l + 1])
                with dve.If(go > 0):
                    V.tensor_scalar(rg, rg, -float(CAP), None, ALU.add).then_inc(ov_chain, 1)
                    dve.wait_ge(ov_chain, l + 1)
                    experts(PASS[1], l * NG)
                with dve.Else():
                    dve.sem_inc(ov_chain, 1)
                    count_skipped(dve, "dve")
                for tt in range(NT):
                    link(V.tensor_tensor(yacc[:, tt], yacc[:, tt], MB[:, 5], ALU.mult))
                    ins = V.tensor_tensor(h[:, tt], h[:, tt], yacc[:, tt], ALU.add)
                    if tt == 0:
                        link(ins)
                ins.then_inc(L["h_ready"], 1)
                dve.wait_ge(L["h_ready"], l + 1)

            dve.wait_ge(h1_ready, 4)
            mean_square(L["sq"], 1, L["ms"])
            norm_mod(L["rstd"], 1, 4, 3, L["u2"], NT)
            dve.wait_ge(s_rt, 32)
            moe(0)
            for n, first in enumerate((6, 8, 10)):
                broadcast_out(2 + n, first)
            dve.wait_ge(s_scl, 16)
            link(V.tensor_tensor(MB[:, 2], MB[:, 2], scl, ALU.mult))
            mean_square(fin_sq, 1, fin_ms)
            norm_mod(fin_rstd, 1, 1, 0, pool_u, NT)
            dve.wait_ge(pool_ps, 1)
            for g in range(4):
                last = V.tensor_copy(pT[:, 2 * g:2 * g + 2, :], psum[g][:].rearrange("p (a b) -> p a b", a=2))
            last.then_inc(pool_T, 1)
            for n in range(4):
                tt, gh = n // 2, n % 2
                dve.wait_ge(pool_y, n + 1)
                link(V.tensor_tensor(mtmp[:, n % 2 * F:(n % 2 + 1) * F], psum[4 + n][:], MB[:, 2, gh * F:(gh + 1) * F], ALU.mult))
                ins = V.tensor_tensor(h[:, tt, gh * F:(gh + 1) * F], h[:, tt, gh * F:(gh + 1) * F],
                                      mtmp[:, n % 2 * F:(n % 2 + 1) * F], ALU.add)
                if n < 3:
                    link(ins)
            ins.then_inc(pool_h, 1)
            dve.wait_ge(pool_h, 1)
            mean_square(L["sq"], 2, L["ms"])
            norm_mod(L["rstd"], 2, 4, 3, L["u2"], 2 * NT)
            moe(1)
            mean_square(fin_sq, 2, fin_ms)
            dve.wait_ge(fin_rstd, 2)
            dve.wait_ge(s_scl, 32)
            for tt in range(NT):
                V.scalar_tensor_tensor(mtmp[:, tt * D:(tt + 1) * D], h[:, tt], rstd[:, tt:tt + 1], scl, ALU.mult,
                                       ALU.mult).then_inc(fin_out, 1)

        @block.gpsimd
        def _(pool):
            Gp = nc.gpsimd

            Gp.memset(modrow[:], 0.0).then_inc(modrow_zero, 1)
            pool.wait_ge(modrow_zero, 1)
            for l in range(2):
                pool.dma_start(modrow[0:P:32, 3 * l:3 * l + 3, :],
                               b_mod[l].rearrange("(b j n) -> j b n", b=3, j=4)).then_inc(s_bm, 16)
            pool.dma_start(modrow[16:P:32, 0, :], b_mod[0, 0:2048].rearrange("(j n) -> j n", j=4)).then_inc(s_bm, 16)
            pool.dma_start(masksf, masks_d).then_inc(s_masks, 16)
            pool.dma_start(anorm, a_norm_g[0:1, :].to_broadcast([P, F])).then_inc(s_an, 16)

            pool.wait_ge(s_masks, 16)
            Gp.tensor_copy(masks[:], masksf).then_inc(masks_ready, 1)

            def power(ready, count, dst, src, done):
                pool.wait_ge(ready, count)
                Gp.tensor_tensor(dst, src, half.to_broadcast([P, src.shape[1]]), ALU.pow).then_inc(done, 1)

            pool.wait_ge(sq_done, 1)
            power(ms_ready, 1, rstd, ms, rstd_ready)

            pool.wait_ge(kcdT_ps, 1)
            Gp.memset(ATd, 0.0).then_inc(atd_zero, 1)

            def load_bias(i):
                hd, qi = i // NT, i % NT
                for half_ in range(2):
                    r = 2 * qi + half_
                    off = hd * RPB_R * RPB_C + (7 - r) * RPB_C + 15 - (GW - 1)
                    src = bass.AP(tensor=rpb.tensor, offset=off, ap=[[1, GW], [RPB_C, 4], [1, GW]])
                    pool.dma_start(bias[i % 4][half_ * GW:(half_ + 1) * GW].rearrange("p (a b) -> p a b", a=4),
                                   src).then_inc(b_dma[i % 4], 16)

            pool.wait_ge(merged, NLEV)
            for i in range(4):
                load_bias(i)
            for i in range(BH * NT):
                pool.wait_ge(b_dma[i % 4], 32 * (i // 4 + 1))
                Gp.tensor_tensor(bias[i % 4], bias[i % 4], cst[:, C_COLM:C_COLM + T], ALU.add).then_inc(b_ready, 1)
                if i == 2:
                    for tt in range(NT):
                        power(ro_ready, tt + 1, rstdo[:, tt * H:(tt + 1) * H], ssq[:, tt * H:(tt + 1) * H], ro_rstd)
                if i >= 3 and i + 1 < BH * NT:
                    pool.wait_ge(sc_ps, i - 2)
                    load_bias(i + 1)
            pool.wait_ge(a_ready, NT)
            pool.dma_start(MB[:, 4], norm2_g[0:1, :].to_broadcast([P, D])).then_inc(mb_dma, 16)
            pool.wait_ge(h1_ready, 4)
            pool.dma_start(wr, w_router.rearrange("(k p) e -> p k e", p=P)).then_inc(s_rt, 16)
            pool.dma_start(brt, b_router.rearrange("(a e) -> a e", a=1).to_broadcast([P, 16])).then_inc(s_rt, 16)
            pool.dma_start(scl, pool_scale[0:1, :].to_broadcast([P, D])).then_inc(s_scl, 16)
            pool.dma_start(bands, bands_d.rearrange("(t p) g n -> p t g n", p=P)).then_inc(s_bands, 16)

            Gp.memset(yacc, 0.0).then_inc(L["yacc0"], 1)
            power(L["ms"], 1, rstd[:, 0:NT], ms[:, 0:NT], L["rstd"])
            pool.wait_ge(L["h_ready"], 1)
            pool.dma_start(MB[:, 1], norm1_g[1:2, :].to_broadcast([P, D])).then_inc(mb_dma, 16)
            pool.dma_start(MB[:, 4], norm2_g[1:2, :].to_broadcast([P, D])).then_inc(mb_dma, 16)
            Gp.memset(yacc, 0.0).then_inc(L["yacc0"], 1)
            power(fin_ms, 1, rstd[:, 0:NT], ms[:, 0:NT], fin_rstd)
            pool.wait_ge(pool_h, 1)
            pool.dma_start(scl, final_g.rearrange("(a n) -> a n", a=1).to_broadcast([P, D])).then_inc(s_scl, 16)
            power(L["ms"], 2, rstd[:, 0:NT], ms[:, 0:NT], L["rstd"])
            power(fin_ms, 2, rstd[:, 0:NT], ms[:, 0:NT], fin_rstd)


_INS = ["x", "c", "ctx", "c_ctx", "w_mod", "b_mod", "norm1_g", "norm2_g", "w_in", "w_out", "lb_logits", "a_norm_g",
        "rpb", "w_pool", "pool_scale", "w_router", "b_router", "w_gate", "w_up", "w_down", "final_g"]
_CONSTS = ["cst", "masks", "bands"]


def kernel(**inputs):
    import concourse.bacc as bacc
    from concourse.bass_utils import run_bass_kernel_spmd

    nc = bacc.Bacc("TRN2", target_bir_lowering=False, num_devices=1)
    named = {name: np.ascontiguousarray(inputs[name]) for name in _INS}
    named.update(zip(_CONSTS, shape_constants()))
    arrays, args = {}, []
    for name, a in named.items():
        arrays[f"in_{name}"] = a
        args.append(nc.dram_tensor(f"in_{name}", a.shape, mybir.dt.from_np(a.dtype), kind="ExternalInput").ap())
    out = nc.dram_tensor("out_0", (1, T, D), F32, kind="ExternalOutput").ap()
    build(nc, *args, out)
    r = run_bass_kernel_spmd(nc, [arrays], core_ids=[0])
    return r.results[0]["out_0"]
```

```python
from contextlib import ExitStack

import numpy as np

import concourse.bass as bass
from concourse import mybir

F32 = mybir.dt.float32
F32R = mybir.dt.float32r
U8 = mybir.dt.uint8
I32 = mybir.dt.int32
ACT = mybir.ActivationFunctionType
ALU = mybir.AluOpType
AX = mybir.AxisListType

P = 128
D = 1024
KC = D // P
T = 256
NT = T // P
F = 512
H = 4
DK = 128
BH = 8
DH = 64
GW = 64
RPB_R, RPB_C = 15, 31
NG, NE = 4, 4
EPS = 1e-6
CAP = 128
RING = 4
PARTS = 4
PW = KC * F // PARTS
NEG = -1.0e30

C_ID, C_TRI, C_IOTA, C_SEL, C_ONES, C_COLM = 0, 128, 256, 384, 512, 640
C_W4, C_W16, C_E2, C_REV, C_N = 896, 900, 916, 918, 1046
LEVELS = (128, 64, 32, 16, 8, 4, 2, 1)
WINDOWS = (2, 4, 8, 16)


def shape_constants():
    cst = np.zeros((P, C_N), np.float32)
    i = np.arange(P)
    cst[:, C_ID:C_ID + P] = np.eye(P)
    cst[:, C_TRI:C_TRI + P] = i[:, None] < i[None, :]
    cst[:, C_IOTA:C_IOTA + P] = i[None, :]
    cst[:, C_SEL:C_SEL + P] = (i % 32 == 0)[:, None]
    cst[:, C_ONES:C_ONES + P] = 1.0
    col, key = i % GW, np.arange(T) % GW
    low = np.clip(col - 8, 0, GW - 16)
    inside = (key[None, :] >= low[:, None]) & (key[None, :] < low[:, None] + 16)
    backwards = i + GW - 1 - 2 * col
    cst[:, C_COLM:C_COLM + T] = np.where(inside, 0.0, NEG)[backwards]
    cst[i, C_REV + backwards] = 1.0
    cst[:, C_W4:C_W4 + 4] = np.arange(4, 0, -1)
    cst[:, C_W16:C_W16 + 16] = np.arange(16, 0, -1)
    cst[:, C_E2] = i % 32 == 0
    cst[:, C_E2 + 1] = i % 32 == 16
    masks = np.zeros((P, 15, P), np.float32)
    for n, m in enumerate(LEVELS[1:]):
        same = (i[:, None] // (2 * m)) == (i[None, :] // (2 * m))
        first, second = i % (2 * m) < m, i % (2 * m) >= m
        masks[:, 2 * n] = same & first[:, None] & second[None, :]
        masks[:, 2 * n + 1] = same & second[:, None] & first[None, :]
    masks[:, 14] = np.eye(P)
    t = np.arange(T)
    bands = np.zeros((T, len(WINDOWS), T), np.float32)
    for g, w in enumerate(WINDOWS):
        lo, hi = np.clip(t - w // 2, 0, T), np.clip(t + w // 2, 0, T)
        inside = (t[:, None] >= lo[None, :]) & (t[:, None] < hi[None, :])
        bands[:, g] = inside / (hi - lo).astype(np.float32)[None, :] - np.eye(T)
    return cst, masks, bands


Q_A, F_F, F_B, I_A, G_A, Q_B, K_B, V_B = range(8)
RING_A = (
    [("mod", 0, s) for s in range(4)]
    + [("in", I_A), ("in", F_F), ("in", F_B), ("in", Q_A), ("in", G_A), ("in", K_B)]
    + [("mod", 1, s) for s in range(4)] + [("in", Q_B)]
    + [("mod", 2, s) for s in range(4)] + [("in", V_B)]
    + [("mod", b, s) for b in (3, 4, 5) for s in range(4)]
    + [("out", 0), ("out", 1)]
)
MOE_ORDER = [("g", 0), ("u", 0), ("g", 1), ("u", 1), ("d", 0), ("g", 2), ("u", 2), ("d", 1),
             ("g", 3), ("u", 3), ("d", 2), ("d", 3)]
NM = len(MOE_ORDER)
ITEM = {item: n for n, item in enumerate(MOE_ORDER)}
N_MOE0 = len(RING_A)
N_POOL = N_MOE0 + NG * NM
N_MOE1 = N_POOL + 1
SLOT_A = {item: n for n, item in enumerate(RING_A)}

UNITS = ([(I_A, m) for m in range(4)] + [(F_F, m) for m in range(4)] + [(F_B, m) for m in range(4)]
         + [(Q_A, m) for m in range(4)] + [(G_A, m) for m in range(2)]
         + [(K_B, m) for m in range(4)] + [(Q_B, m) for m in range(4)] + [(V_B, m) for m in range(4)])
U_END = {p: max(n for n, u in enumerate(UNITS) if u[0] == p) + 1 for p in range(8)}
U_EARLY = U_END[G_A]
FILL = [[18, 19, 20], [21], ["m1"], [22, 23], [24, 25], ["m2"], [26], [27], [28], [29, "m3", "m4", "m5"]]
NLEV = len(LEVELS) + 1
PROJ_BANKS = (4, 5, 6)
SCAT_BANKS = (2, 3, 4, 7)
MOD_BANK = 7


def build(nc, x, c, ctx, c_ctx, w_mod, b_mod, norm1_g, norm2_g, w_in, w_out, lb_logits, a_norm_g, rpb,
          w_pool, pool_scale, w_router, b_router, w_gate, w_up, w_down, final_g, cst_d, masks_d, bands_d, out):
    with ExitStack() as stack:
        def sb(name, shape, dt=F32):
            return stack.enter_context(nc.sbuf_tensor("sb_" + name, shape, dt))

        def sem(name):
            return stack.enter_context(nc.semaphore(name))

        ring = sb("ring", [P, RING, KC * F])
        h = sb("h", [P, NT, D])
        cst = sb("cst", [P, C_N])
        masks = sb("masks", [P, 15, P], U8)
        modrow = sb("modrow", [P, 6, F])
        prow = sb("prow", [40, P])
        parT = sb("parT", [P, 40])
        small = sb("small", [P, 400])
        flag = sb("flag", [1, 2], I32)
        KB = 256
        with nc.sbuf_tensor("sb_mixer_arena", [P, int(114.25 * KB)], F32) as mixer_arena:
            pass
        moe_arena = sb("moe_arena", [P, int(60.75 * KB)])
        with nc.sbuf_tensor("sb_between", [P, 28 * KB], F32) as between:
            pass
        split = sb("split", [P, 53 * KB], F32R)
        psum = [stack.enter_context(nc.psum_tensor(f"bank{i}", [P, F], F32)) for i in range(8)]

        def area(kb, shape, of=None):
            n = int(np.prod(shape))
            a = (mixer_arena if of is None else of)[:, int(kb * KB):int(kb * KB) + n]
            if len(shape) == 2:
                return a.rearrange("p (a b) -> p a b", a=shape[0])
            if len(shape) == 3:
                return a.rearrange("p (a b c) -> p a b c", a=shape[0], b=shape[1])
            return a

        uT = area(0, [KC, 2 * T])
        lf = area(16, [8, 2 * T])
        kl = area(32, [8, T])
        kc = area(40, [8, T])
        X = area(48, [8, 2, T + 1])
        v = area(64.25, [2 * NT, F])
        qa = area(72.25, [H, T])
        gn = area(76.25, [NT, F])
        qb = area(80.25, [4, T])
        kbT = area(84.25, [4, 2 * T])
        vb = area(92.25, [2 * NT, F])
        S = area(100.25, [8, P])
        qt = area(104.25, [2, H, T])
        anorm = area(112.25, [F])
        junk = area(16, [D])
        masksf = area(48, [15, P])
        xnl = area(84.25, [NT, D])
        cx = area(92.25, [NT, D])
        csil = small[:, 0:256].rearrange("p (k n) -> p k n", k=KC)
        modT = area(20, [16, 2])
        A1T = area(21, [KC, 2])
        kcdT = area(16, [NT, 8, P])
        kcd = area(24, [8, T])
        Z = [area(16, [8, T]), area(24, [8, T])]
        ATd = area(40, [NT, H, P])
        ATo = area(44, [2, H, P])
        cat = area(0, [NT, D])
        catT = area(8, [KC, T])
        prob = [area(16, [F]), area(18, [F])]
        probT = [area(20, [F]), area(22, [F])]
        bias = [area(24 + n, [T]) for n in range(4)]
        ytmp = area(28, [2, F])
        M = moe_arena
        yacc = area(0, [NT, D], M)
        u2 = area(8, [NT, D], M)
        u2T = area(16, [KC, T], M)
        sg = area(24, [F], M)
        hh = area(26, [F], M)
        scl = area(28, [D], M)
        Pg = area(32, [NT, P], M)
        wr = area(33, [KC, 16], M)
        brt = area(33.5, [16], M)
        rs = area(33.5625, [3 * KB], M)
        MB = area(36.75, [6, D], M)
        w_hi = [area(8 * q, [PW], split) for q in range(PARTS)]
        w_lo = [area(8 * q + 4, [PW], split) for q in range(PARTS)]
        x_hi, x_lo = area(32, [KC, CAP], split), area(36, [KC, CAP], split)
        hT_hi, hT_lo = area(40, [4, CAP], split), area(42, [4, CAP], split)
        yg_hi, yg_lo = area(44, [D], split), area(48, [D], split)
        PT = area(52, [NT, P], split)
        bands = area(0, [NT, 4, T], between)
        pT = area(8, [8, T], between)
        mtmp = area(16, [2 * D], between)
        sq_out = area(24, [D], between)

        ss = small[:, 256:260]
        ms = small[:, 260:264]
        rstd = small[:, 264:268]
        ssq = small[:, 268:276]
        rstdo = small[:, 276:284]
        nmax = small[:, 284:286]
        den = small[:, 286:302]
        rden = small[:, 302:318]
        half = small[:, 318:319]
        junk2 = [area(28 + 0.5 * n, [P]) for n in range(NT)]
        silc = small[:, 320:336]
        lbs = small[:, 336:352]
        lbw = small[:, 352:400]
        ident = cst[:, C_ID:C_ID + P]

        s_cst, s_par, s_x, s_cx = sem("s_cst"), sem("s_par"), sem("s_x"), sem("s_cx")
        s_bm, s_an = sem("s_bm"), sem("s_an")
        s_masks, masks_ready, lb_arg, lb_exp, g_sig, ro_rstd = (
            sem("s_masks"), sem("masks_ready"), sem("lb_arg"), sem("lb_exp"), sem("g_sig"), sem("ro_rstd"))
        loaded = [sem(f"loaded{i}") for i in range(RING)]
        modrow_zero, half_set = sem("modrow_zero"), sem("half_set")
        par_ps, par_T, sig_c, csil_ready = sem("par_ps"), sem("par_T"), sem("sig_c"), sem("csil_ready")
        mod_used, mod_rows, modT_ps, A1_ready = sem("mod_used"), sem("mod_rows"), sem("modT_ps"), sem("A1_ready")
        sq_done, ms_ready, rstd_ready, xn_ready = sem("sq_done"), sem("ms_ready"), sem("rstd_ready"), sem("xn_ready")
        uT_ps, uT_dve, uT_act = sem("uT_ps"), sem("uT_dve"), sem("uT_act")
        proj_done, proj_out, g_out = sem("proj_done"), sem("proj_out"), sem("g_out")
        f_ready, lf_ready, X_ready = sem("f_ready"), sem("lf_ready"), sem("X_ready")
        kcd_exp, kcd_ready, kcdT_ps, kcdT_ready = sem("kcd_exp"), sem("kcd_ready"), sem("kcdT_ps"), sem("kcdT_ready")
        S_ps, S_ready, qt_exp, qt_ready = sem("S_ps"), sem("S_ready"), sem("qt_exp"), sem("qt_ready")
        z_arg, z_exp, z_ready, gram, merged = sem("z_arg"), sem("z_exp"), sem("z_ready"), sem("gram"), sem("merged")
        atd_zero = sem("atd_zero")
        av_done, osq, ro_ready, a_ready = sem("av_done"), sem("osq"), sem("ro_ready"), sem("a_ready")
        b_dma, b_ready = [sem(f"b_dma{n}") for n in range(4)], sem("b_ready")
        sc_ps, sc_max, p_exp = sem("sc_ps"), sem("sc_max"), sem("p_exp")
        pT_ps, pT_ready, pv_done = sem("pT_ps"), sem("pT_ready"), sem("pv_done")
        cat_ready, catT_ps, catT_ready, y_done = sem("cat_ready"), sem("catT_ps"), sem("catT_ready"), sem("y_done")
        h1_ready = sem("h1_ready")
        bc_ps, bc_out, mb_dma = sem("bc_ps"), sem("bc_out"), sem("mb_dma")
        dve_chain, act_chain, pool_chain = sem("dve_chain"), sem("act_chain"), sem("pool_chain")
        s_rt, s_scl, s_out = sem("s_rt"), sem("s_scl"), sem("s_out")
        L = dict((n, sem(f"moe_{n}")) for n in (
            "sq", "ms", "rstd", "u2", "u2T_ps", "u2T", "logits", "scores", "gates", "ranks", "routed",
            "h_ready", "yacc0"))
        pool_u, pool_ps, pool_T, pool_y, pool_h, s_bands = (
            sem("pool_u"), sem("pool_ps"), sem("pool_T"), sem("pool_y"), sem("pool_h"), sem("s_bands"))
        fin_sq, fin_ms, fin_rstd, fin_out = sem("fin_sq"), sem("fin_ms"), sem("fin_rstd"), sem("fin_out")
        PASS = [dict((n, sem(f"pass{k}_{n}")) for n in (
            "hi", "lo", "part", "p_ready", "xg_ps", "xg_hi", "xg_lo", "route_ps", "gs", "silu", "hid", "hT_ps",
            "hT_hi", "hT_lo", "yg_hi", "yg_lo", "scat_ps", "scat")) for k in range(2)]
        TP = NM * PARTS
        PER_TILE = {"hi": TP, "lo": TP, "part": TP, "silu": NE, "hid": NE, "hT_ps": NE, "hT_hi": NE, "hT_lo": NE}
        BY = {"pe": ("xg_ps", "route_ps", "part", "hT_ps", "scat_ps"),
              "act": ("hi", "xg_hi", "silu", "hT_hi", "yg_hi"),
              "dve": ("lo", "p_ready", "xg_lo", "gs", "hid", "hT_lo", "yg_lo", "scat")}
        ov_loaded = [sem(f"ov_loaded{i}") for i in range(RING)]
        ov_chain = sem("ov_chain")

        def count_skipped(eng, name):
            for n in BY[name]:
                eng.sem_inc(PASS[1][n], NG * PER_TILE.get(n, 1))

        def chunks(w):
            return w.rearrange("(k p) n -> p k n", p=P)

        def slot(n):
            return ring[:, n % RING, :]

        def landed(n):
            return 16 * (n // RING + 1)

        def used_a(n):
            kind = RING_A[n][0]
            if kind == "mod":
                return mod_used, 4 * RING_A[n][1] + RING_A[n][2] + 1
            if kind == "in":
                return proj_done, U_END[RING_A[n][1]]
            return y_done, 2 * RING_A[n][1] + 2

        def taken(u):
            if UNITS[u][0] == G_A:
                return g_out, UNITS[u][1] + 1
            return proj_out, sum(p != G_A for p, _ in UNITS[:u + 1])

        def used_moe(sems, t, j):
            t, j = t + j // NM, j % NM
            return sems["lo"], t * TP + PARTS * (j + 1)

        def consumed(sems, t, j):
            return sems["part"], t * TP + PARTS * (j + 1)

        def moe_src(l, t, j):
            kind, e = MOE_ORDER[j]
            w = {"g": w_gate, "u": w_up, "d": w_down}[kind]
            at = t * NE + e
            w = w[l, at] if isinstance(at, int) else w[l, bass.ds(at, 1)].rearrange("o a n -> (o a) n")
            return w.rearrange("(k p) n -> p k n", p=P)

        def slot_as(n, k):
            return slot(n).rearrange("p (k n) -> p k n", k=k)

        def linker(eng, s, base=0):
            count = [0]

            def link(ins):
                count[0] += 1
                ins.then_inc(s, 1)
                eng.wait_ge(s, base + count[0])
            link.count = count
            return link

        block = stack.enter_context(nc.Block())

        @block.sync
        def _(sp):
            sp.dma_start(h[:], x[0].rearrange("(t p) d -> p t d", p=P)).then_inc(s_x, 16)
            sp.dma_start(cx, ctx[0].rearrange("(t p) d -> p t d", p=P)).then_inc(s_cx, 16)
            for n, item in enumerate(RING_A):
                if n >= RING:
                    sp.wait_ge(*used_a(n - RING))
                if item[0] == "mod":
                    _, b, s = item
                    src = w_mod[b // 3, 256 * s:256 * s + 256, 2048 * (b % 3):2048 * (b % 3) + 2048]
                elif item[0] == "in":
                    src = w_in[0][:, item[1] * F:(item[1] + 1) * F]
                else:
                    src = w_out[0][:, item[1] * F:(item[1] + 1) * F]
                src = src.rearrange("(k p) n -> p k n", p=P)
                sp.dma_start(slot_as(n, src.shape[1]), src).then_inc(loaded[n % RING], 16)

            def stream_moe(l, n0, before):
                sems, tb = PASS[0], l * NG

                def load(t, j):
                    n = n0 + j
                    src = moe_src(l, t, j)
                    sp.dma_start(slot_as(n, src.shape[1]), src).then_inc(loaded[n % RING], 16)

                for j in range(RING):
                    sp.wait_ge(*before(n0 + j - RING))
                    load(0, j)
                with sp.Fori(0, NG - 1) as t:
                    for j in range(RING, NM):
                        sp.wait_ge(*used_moe(sems, tb + t, j - RING))
                        load(t, j)
                    for j in range(RING):
                        sp.wait_ge(*used_moe(sems, tb + t, NM + j - RING))
                        load(t + 1, j)
                for j in range(RING, NM):
                    sp.wait_ge(*used_moe(sems, tb + NG - 1, j - RING))
                    load(NG - 1, j)

            def overflow_moe(l):
                sp.wait_ge(L["routed"], l + 1)
                go = sp.value_load(flag[0:1, l:l + 1])
                sems, tb = PASS[1], l * NG
                with sp.If(go > 0):
                    sp.wait_ge(PASS[0]["lo"], (tb + NG) * TP)
                    for j in range(RING):
                        src = moe_src(l, 0, j)
                        sp.dma_start(slot_as(j, src.shape[1]), src).then_inc(ov_loaded[j], 16)
                    with sp.Fori(0, NG - 1) as t:
                        for j in range(RING, NM + RING):
                            sp.wait_ge(*used_moe(sems, tb + t, j - RING))
                            src = moe_src(l, t if j < NM else t + 1, j % NM)
                            sp.dma_start(slot_as(j, src.shape[1]), src).then_inc(ov_loaded[j % RING], 16)
                    for j in range(RING, NM):
                        sp.wait_ge(*used_moe(sems, tb + NG - 1, j - RING))
                        src = moe_src(l, NG - 1, j)
                        sp.dma_start(slot_as(j, src.shape[1]), src).then_inc(ov_loaded[j % RING], 16)
                    sp.wait_ge(sems["lo"], (tb + NG) * TP)
                with sp.Else():
                    for i in range(RING):
                        sp.sem_inc(ov_loaded[i], 16 * NG * NM // RING)

            stream_moe(0, N_MOE0, used_a)
            overflow_moe(0)

            def before_pool(n):
                return used_moe(PASS[0], NG - 1, n - N_MOE0 - (NG - 1) * NM)
            sp.wait_ge(*before_pool(N_POOL - RING))
            sp.dma_start(slot(N_POOL)[:, 0:8 * T].rearrange("p (g n) -> p g n", g=8),
                         w_pool[0].rearrange("g (c p) n -> p (g c) n", p=P)).then_inc(loaded[N_POOL % RING], 16)

            def before_moe1(n):
                return (pool_y, 4) if n == N_POOL else before_pool(n)
            stream_moe(1, N_MOE1, before_moe1)
            overflow_moe(1)
            for tt in range(NT):
                sp.wait_ge(fin_out, tt + 1)
                sp.dma_start(out[0, tt * P:(tt + 1) * P, :], mtmp[:, tt * D:(tt + 1) * D]).then_inc(s_out, 16)
            sp.wait_ge(s_out, 16 * NT)

        @block.tensor
        def _(pe):
            mm = nc.tensor.matmul
            tr = nc.tensor.transpose
            pe.wait_ge(s_cst, 16)
            pe.wait_ge(s_par, 64)
            tr(psum[0][:, 0:40], prow[:], cst[0:40, C_ID:C_ID + 40]).then_inc(par_ps, 1)

            def mod_bank(b):
                for s in range(4):
                    n = SLOT_A[("mod", b, s)]
                    pe.wait_ge(loaded[n % RING], landed(n))
                    w = slot(n).rearrange("p (k j n) -> p k j n", k=2, j=4)
                    for kk in range(2):
                        k = 2 * s + kk
                        for j in range(4):
                            last = mm(psum[MOD_BANK][32 * j:32 * j + 32, :], csil[:, k, :], w[:, kk, j, :],
                                      start=k == 0, stop=k == KC - 1, tile_position=(0, 32 * j),
                                      skip_group_check=True)
                    last.then_inc(mod_used, 1)

            pe.wait_ge(csil_ready, 1)
            mod_bank(0)
            pe.wait_ge(mod_rows, 1)
            for cc in range(4):
                for j in range(4):
                    last = mm(psum[2 + j][:, 2 * cc:2 * cc + 2], modrow[32 * j:32 * j + 32, 0, cc * P:(cc + 1) * P],
                              cst[32 * j:32 * j + 32, C_E2:C_E2 + 2], start=True, stop=True,
                              tile_position=(32 * j, 0))
            last.then_inc(modT_ps, 1)

            pe.wait_ge(xn_ready, 4)
            pe.wait_ge(A1_ready, 1)
            for k in range(KC):
                for tt in range(4):
                    src = xnl if tt < NT else cx
                    last = tr(psum[k][:, tt * P:(tt + 1) * P], src[:, tt % NT, k * P:(k + 1) * P], ident)
                last.then_inc(uT_ps, 1)
            pe.wait_ge(uT_dve, KC // 2)
            pe.wait_ge(uT_act, KC // 2)

            def proj_unit(u):
                p, m = UNITS[u]
                n = SLOT_A[("in", p)]
                bank = psum[PROJ_BANKS[u % 3]]
                if m == 0:
                    pe.wait_ge(loaded[n % RING], landed(n))
                if u >= 3:
                    pe.wait_ge(*taken(u - 3))
                w = slot_as(n, KC)
                for k in range(KC):
                    if p in (I_A, G_A, V_B):
                        last = mm(bank[:], uT[:, k, m * P:(m + 1) * P], w[:, k, :], start=k == 0, stop=k == KC - 1)
                    else:
                        cols = T if p in (Q_A, Q_B) else 2 * T
                        last = mm(bank[:, 0:cols], w[:, k, m * P:(m + 1) * P], uT[:, k, 0:cols],
                                  start=k == 0, stop=k == KC - 1)
                last.then_inc(proj_done, 1)

            for u in range(U_EARLY):
                proj_unit(u)

            def fill(n):
                for what in FILL[n]:
                    if isinstance(what, int):
                        proj_unit(what)
                    else:
                        b = int(what[1:])
                        pe.wait_ge(mod_rows, b)
                        mod_bank(b)

            pe.wait_ge(kcd_ready, 1)
            for st in range(NT):
                for i in range(8):
                    last = tr(psum[2 * st + i // 4][:, (i % 4) * P:(i % 4 + 1) * P], kcd[:, i, st * P:(st + 1) * P], ident)
            last.then_inc(kcdT_ps, 1)
            proj_unit(FILL[0][0])
            pe.wait_ge(kcdT_ready, 1)
            for i in range(8):
                for st in range(NT):
                    last = mm(psum[i // 4][:, (i % 4) * P:(i % 4 + 1) * P], kcdT[:, st, i, :],
                              v[:, NT + st, (i % H) * P:(i % H + 1) * P], start=st == 0, stop=st == NT - 1)
            last.then_inc(S_ps, 1)
            for u in FILL[0][1:]:
                proj_unit(u)

            pe.wait_ge(S_ready, 1)
            for lev in range(NLEV):
                if lev < len(LEVELS):
                    pe.wait_ge(z_ready, lev + 1)
                if lev:
                    pe.wait_ge(merged, lev)
                z = Z[lev % 2]
                if lev == 0:
                    for d in range(2):
                        for hd in range(H):
                            i = d * H + hd
                            last = mm(psum[d][:, hd * P:(hd + 1) * P], z[:, i, d * P:(d + 1) * P],
                                      z[:, i, (1 - d) * P:(2 - d) * P], start=True, stop=True)
                elif lev < len(LEVELS):
                    for d in range(2):
                        for tt in range(NT):
                            for hd in range(H):
                                zz = z[:, d * H + hd, tt * P:(tt + 1) * P]
                                last = mm(psum[2 * d + tt][:, hd * P:(hd + 1) * P], zz, zz, start=True, stop=True)
                else:
                    for tt in range(NT):
                        for hd in range(H):
                            for d in range(2):
                                last = mm(psum[tt][:, hd * P:(hd + 1) * P], kl[:, d * H + hd, tt * P:(tt + 1) * P],
                                          qa[:, hd, tt * P:(tt + 1) * P], start=d == 0, stop=d == 1)
                last.then_inc(gram, 1)
                fill(lev + 1)

            pe.wait_ge(merged, NLEV)
            pe.wait_ge(qt_ready, 1)
            for tt in range(NT):
                for hd in range(H):
                    o = psum[tt][:, hd * P:(hd + 1) * P]
                    mm(o, ATd[:, tt, hd, :], v[:, tt, hd * P:(hd + 1) * P], start=True, stop=False)
                    mm(o, ATo[:, 1 - tt, hd, :], v[:, 1 - tt, hd * P:(hd + 1) * P], start=False, stop=False)
                    mm(o, qt[:, 0, hd, tt * P:(tt + 1) * P], S[:, hd, :], start=False, stop=False)
                    last = mm(o, qt[:, 1, hd, tt * P:(tt + 1) * P], S[:, H + hd, :], start=False, stop=True)
                last.then_inc(av_done, 1)

            def attn_scores(i):
                hd, qi = i // NT, i % NT
                r = DH * (hd % 2)
                mm(psum[2 + i % 2][:], qb[r:r + DH, hd // 2, qi * P:(qi + 1) * P], kbT[r:r + DH, hd // 2, :],
                   start=True, stop=False)
                pe.wait_ge(b_ready, i + 1)
                mm(psum[2 + i % 2][:, 0:T], cst[:, C_REV:C_REV + P], bias[i % 4], start=False,
                   stop=True).then_inc(sc_ps, 1)

            pe.wait_ge(*taken(len(UNITS) - 1))
            pe.wait_ge(mod_rows, 6)
            attn_scores(0)
            attn_scores(1)
            for i in range(BH * NT):
                hd, qi = i // NT, i % NT
                pe.wait_ge(p_exp, i + 1)
                for cc in range(4):
                    last = tr(psum[4 + i % 2][:, cc * P:(cc + 1) * P], prob[i % 2][:, cc * P:(cc + 1) * P], ident)
                last.then_inc(pT_ps, 1)
                if i + 2 < BH * NT:
                    attn_scores(i + 2)
                pe.wait_ge(pT_ready, i + 1)
                for cc in range(4):
                    last = mm(psum[6 + qi][:, hd * DH:(hd + 1) * DH], probT[i % 2][:, cc * P:(cc + 1) * P],
                              vb[:, cc, hd * DH:(hd + 1) * DH], start=cc == 0, stop=cc == 3)
                last.then_inc(pv_done, 1)

            def broadcast(first):
                l, p = divmod(first, 6)
                for j in range(4):
                    last = mm(psum[j][:], cst[32 * j:32 * j + 32, C_SEL:C_SEL + P],
                              modrow[32 * j:32 * j + 32, 3 * l + p // 2, :], start=True, stop=True,
                              tile_position=(32 * j, 0))
                last.then_inc(bc_ps, 1)

            pe.wait_ge(a_ready, NT)
            broadcast(2)
            pe.wait_ge(bc_out, 1)
            pe.wait_ge(cat_ready, 1)
            for k in range(KC):
                for tt in range(NT):
                    last = tr(psum[k // 2][:, (k % 2) * T + tt * P:(k % 2) * T + (tt + 1) * P],
                              cat[:, tt, k * P:(k + 1) * P], ident)
            last.then_inc(catT_ps, 1)
            pe.wait_ge(catT_ready, 1)
            for nh in range(2):
                n = SLOT_A[("out", nh)]
                pe.wait_ge(loaded[n % RING], landed(n))
                w = slot_as(n, KC)
                for tt in range(NT):
                    for k in range(KC):
                        last = mm(psum[4 + 2 * nh + tt][:], catT[:, k, tt * P:(tt + 1) * P], w[:, k, :],
                                  start=k == 0, stop=k == KC - 1)
                    last.then_inc(y_done, 1)
            broadcast(4)

            def route(l):
                s = L
                pe.wait_ge(s["u2"], NT * (l + 1))
                pe.wait_ge(bc_out, 2 if l == 0 else 5)
                for k in range(KC):
                    for tt in range(NT):
                        last = tr(psum[k // 2][:, (k % 2) * T + tt * P:(k % 2) * T + (tt + 1) * P],
                                  u2[:, tt, k * P:(k + 1) * P], ident)
                last.then_inc(s["u2T_ps"], 1)
                pe.wait_ge(s["u2T"], l + 1)
                pe.wait_ge(s_rt, 32)
                for tt in range(NT):
                    for k in range(KC):
                        last = mm(psum[4][:, tt * 16:(tt + 1) * 16], u2T[:, k, tt * P:(tt + 1) * P], wr[:, k, :],
                                  start=k == 0, stop=k == KC - 1)
                last.then_inc(s["logits"], 1)
                pe.wait_ge(s["gates"], l + 1)
                G = rs[:, 0:8]
                mm(psum[5][:, 0:4], cst[:, C_TRI:C_TRI + P], G[:, 0:4], start=True, stop=True)
                mm(psum[5][:, 4:8], cst[:, C_ONES:C_ONES + P], G[:, 0:4], start=True, stop=False)
                mm(psum[5][:, 4:8], cst[:, C_TRI:C_TRI + P], G[:, 4:8], start=False, stop=True)
                mm(psum[5][:, 8:12], cst[:, C_ONES:C_ONES + P], G[:, 0:4], start=True, stop=False)
                mm(psum[5][:, 8:12], cst[:, C_ONES:C_ONES + P], G[:, 4:8], start=False, stop=True).then_inc(s["ranks"], 1)

            def experts(sems, tb, gates_c):
                def gather(t):
                    pe.wait_ge(sems["p_ready"], t + 1)
                    for k in range(KC):
                        for tt in range(NT):
                            last = mm(psum[2 + k // 4][:, (k % 4) * P:(k % 4) * P + CAP], u2[:, tt, k * P:(k + 1) * P],
                                      Pg[:, tt, 0:CAP], start=tt == 0, stop=tt == NT - 1)
                    last.then_inc(sems["xg_ps"], 1)

                def slots_of(t):
                    pe.wait_ge(sems["scat"], t + 1)
                    for tt in range(NT):
                        tr(psum[7][0:CAP, P + tt * P:P + (tt + 1) * P], Pg[:, tt, 0:CAP], ident)
                    for tt in range(NT):
                        last = mm(psum[7][0:CAP, 0:4], Pg[:, tt, 0:CAP], gates_c[:, tt * 4:tt * 4 + 4],
                                  start=tt == 0, stop=tt == NT - 1)
                    last.then_inc(sems["route_ps"], 1)

                def up_or_gate(t, kind, e):
                    bank = psum[2 * (e % 2) + (kind == "u")][0:CAP, :]
                    for q in range(PARTS):
                        pe.wait_ge(sems["lo"], t * TP + (PARTS * ITEM[kind, e] + q + 1))
                        for kk in range(2):
                            k = 2 * q + kk
                            hi, lo = w_hi[q][:, kk * F:(kk + 1) * F], w_lo[q][:, kk * F:(kk + 1) * F]
                            mm(bank, x_hi[:, k, :], hi, start=k == 0, stop=False)
                            mm(bank, x_hi[:, k, :], lo, start=False, stop=False)
                            last = mm(bank, x_lo[:, k, :], hi, start=False, stop=k == KC - 1)
                        last.then_inc(sems["part"], 1)

                def hidden_T(t, e):
                    pe.wait_ge(sems["hid"], t * NE + (e + 1))
                    for cc in range(4):
                        last = tr(psum[4][:, cc * P:cc * P + CAP], hh[0:CAP, cc * P:(cc + 1) * P],
                                  cst[0:CAP, C_ID:C_ID + CAP])
                    last.then_inc(sems["hT_ps"], 1)

                def down(t, e):
                    pe.wait_ge(sems["hT_lo"], t * NE + (e + 1))
                    for q in range(PARTS):
                        pe.wait_ge(sems["lo"], t * TP + (PARTS * ITEM["d", e] + q + 1))
                        first, end = e == 0 and q == 0, e == NE - 1 and q == PARTS - 1
                        for nh in range(2):
                            bank = psum[5 + nh][0:CAP, :]
                            hi, lo = w_hi[q][:, nh * F:(nh + 1) * F], w_lo[q][:, nh * F:(nh + 1) * F]
                            mm(bank, hT_hi[:, q, :], hi, start=first, stop=False)
                            mm(bank, hT_hi[:, q, :], lo, start=False, stop=False)
                            last = mm(bank, hT_lo[:, q, :], hi, start=False, stop=end)
                        last.then_inc(sems["part"], 1)

                def scatter(t):
                    pe.wait_ge(sems["gs"], t + 1)
                    pe.wait_ge(sems["yg_lo"], t + 1)
                    for n, b in enumerate(SCAT_BANKS):
                        tt, nh = n // 2, n % 2
                        mm(psum[b][:], PT[0:CAP, tt, :], yg_hi[0:CAP, nh * F:(nh + 1) * F], start=True, stop=False)
                        last = mm(psum[b][:], PT[0:CAP, tt, :], yg_lo[0:CAP, nh * F:(nh + 1) * F], start=False, stop=True)
                    last.then_inc(sems["scat_ps"], 1)

                def start(t):
                    gather(t)
                    pe.wait_ge(sems["xg_lo"], t + 1)
                    up_or_gate(t, "g", 0)
                    up_or_gate(t, "u", 0)

                def tile(t, more):
                    slots_of(t)
                    for e in range(1, NE):
                        up_or_gate(t, "g", e)
                        hidden_T(t, e - 1)
                        up_or_gate(t, "u", e)
                        down(t, e - 1)
                    hidden_T(t, NE - 1)
                    if more:
                        gather(t + 1)
                    down(t, NE - 1)
                    if more:
                        pe.wait_ge(sems["xg_lo"], t + 2)
                        up_or_gate(t + 1, "g", 0)
                    scatter(t)
                    if more:
                        up_or_gate(t + 1, "u", 0)

                start(tb)
                with pe.Fori(0, NG - 1) as i:
                    tile(i + tb, True)
                tile(tb + NG - 1, False)

            def moe(l):
                route(l)
                experts(PASS[0], l * NG, rs[:, 8:16])
                pe.wait_ge(L["routed"], l + 1)
                go = pe.value_load(flag[0:1, l:l + 1])
                with pe.If(go > 0):
                    pe.wait_ge(PASS[0]["scat"], (l + 1) * NG + 1)
                    experts(PASS[1], l * NG, rs[:, 8:16])
                    pe.wait_ge(PASS[1]["scat"], (l + 1) * NG + 1)
                with pe.Else():
                    count_skipped(pe, "pe")

            moe(0)

            pe.wait_ge(L["h_ready"], 1)
            for n, first in enumerate((6, 8, 10)):
                if n:
                    pe.wait_ge(bc_out, 2 + n)
                broadcast(first)
            pe.wait_ge(pool_u, NT)
            pe.wait_ge(bc_out, 5)
            pe.wait_ge(s_bands, 16)
            for g in range(4):
                for cc in range(2):
                    k = 2 * g + cc
                    for st in range(NT):
                        last = mm(psum[g][:, cc * T:(cc + 1) * T], u2[:, st, k * P:(k + 1) * P], bands[:, st, g, :],
                                  start=st == 0, stop=st == NT - 1)
            last.then_inc(pool_ps, 1)
            pe.wait_ge(pool_T, 1)
            pe.wait_ge(loaded[N_POOL % RING], landed(N_POOL))
            w = slot(N_POOL)[:, 0:8 * T].rearrange("p (g n) -> p g n", g=8)
            for tt in range(NT):
                for gh in range(2):
                    for g in (2 * gh, 2 * gh + 1):
                        for cc in range(2):
                            last = mm(psum[4 + 2 * tt + gh][:, (g % 2) * T:(g % 2 + 1) * T],
                                      pT[:, 2 * g + cc, tt * P:(tt + 1) * P], w[:, 2 * g + cc, :],
                                      start=cc == 0, stop=cc == 1)
                    last.then_inc(pool_y, 1)
            pe.wait_ge(pool_h, 1)
            moe(1)

        @block.scalar
        def _(act):
            link = linker(act, act_chain)
            A = nc.scalar.activation
            act.dma_start(cst[:], cst_d).then_inc(s_cst, 16)
            act.dma_start(prow[0:8, :], c.rearrange("b (k p) -> (b k) p", p=P)).then_inc(s_par, 16)
            act.dma_start(prow[8:16, :], c_ctx.rearrange("(k p) -> k p", p=P)).then_inc(s_par, 16)
            act.dma_start(prow[16:24, :], norm1_g[0].rearrange("(k p) -> k p", p=P)).then_inc(s_par, 16)
            act.dma_start(prow[24:40, :], lb_logits.rearrange("l d (h p) -> (l d h) p", p=P)).then_inc(s_par, 16)
            act.wait_ge(par_T, 1)
            A(silc, parT[:, 0:16], ACT.Sigmoid).then_inc(sig_c, 1)
            act.wait_ge(lb_arg, 1)
            A(lbw[:, 0:16], lbw[:, 0:16], ACT.Exp).then_inc(lb_exp, 1)
            act.wait_ge(s_x, 16)
            act.wait_ge(s_cx, 16)
            for tt in range(4):
                link(A(junk, h[:, tt] if tt < NT else cx[:, tt - NT], ACT.Square, accum_out=ss[:, tt:tt + 1]))
            A(half, cst[:, C_ONES:C_ONES + 1], ACT.Copy, scale=-0.5).then_inc(sq_done, 1)
            act.wait_ge(A1_ready, 1)
            for k in range(1, KC, 2):
                act.wait_ge(uT_ps, k + 1)
                for w in range(2):
                    last = A(uT[:, k, w * T:(w + 1) * T], psum[k][:, w * T:(w + 1) * T], ACT.Identity,
                             bias=modT[:, k, w:w + 1], scale=A1T[:, k, w:w + 1])
                last.then_inc(uT_act, 1)
            act.wait_ge(uT_dve, KC // 2)

            def take(u):
                p, m = UNITS[u]
                bank = psum[PROJ_BANKS[u % 3]]
                act.wait_ge(proj_done, u + 1)
                if p == I_A:
                    ins = A(v[:, m, :], bank[:], ACT.Copy)
                elif p in (F_F, F_B):
                    ins = A(lf[:, (p - F_F) * H + m, :], bank[:], ACT.Sigmoid)
                elif p == Q_A:
                    ins = A(qa[:, m, :], bank[:, 0:T], ACT.Copy, scale=float(np.float32(DK ** -0.5)))
                elif p == G_A:
                    A(gn[:, m, :], bank[:], ACT.Sigmoid).then_inc(g_sig, 1)
                    return
                elif p == K_B:
                    ins = A(kbT[:, m, :], bank[:], ACT.Copy)
                elif p == Q_B:
                    ins = A(qb[:, m, :], bank[:, 0:T], ACT.Copy, scale=DH ** -0.5)
                else:
                    ins = A(vb[:, m, :], bank[:], ACT.Copy)
                ins.then_inc(proj_out, 1)

            for u in range(U_EARLY):
                take(u)
            for d in range(2):
                act.wait_ge(f_ready, d + 1)
                A(lf[:, d * H:(d + 1) * H, :], lf[:, d * H:(d + 1) * H, :], ACT.Ln).then_inc(lf_ready, 1)
            act.wait_ge(X_ready, 2)
            for hd in range(H):
                A(kcd[:, hd, :], X[:, hd, 1, 1:T + 1], ACT.Exp, bias=X[:, hd, 1, T:T + 1], scale=-1.0)
            A(kcd[:, H:2 * H, :], X[:, H:2 * H, 1, 0:T], ACT.Exp).then_inc(kcd_exp, 1)
            A(qt[:, 0], X[:, 0:H, 0, 1:T + 1], ACT.Exp)
            for hd in range(H):
                last = A(qt[:, 1, hd, :], X[:, H + hd, 0, 0:T], ACT.Exp, bias=X[:, H + hd, 0, T:T + 1], scale=-1.0)
            last.then_inc(qt_exp, 1)
            for u in FILL[0]:
                take(u)
            for lev in range(NLEV):
                if lev < len(LEVELS):
                    act.wait_ge(z_arg, lev + 1)
                    A(Z[lev % 2], Z[lev % 2], ACT.Exp).then_inc(z_exp, 1)
                if lev:
                    for u in FILL[lev]:
                        if isinstance(u, int):
                            take(u)
            for u in FILL[NLEV]:
                if isinstance(u, int):
                    take(u)
            for tt in range(NT):
                act.wait_ge(av_done, tt + 1)
                for hd in range(H):
                    ins = A(junk2[tt], psum[tt][:, hd * P:(hd + 1) * P], ACT.Square,
                            accum_out=ssq[:, tt * H + hd:tt * H + hd + 1])
                    if hd < H - 1:
                        link(ins)
                ins.then_inc(osq, 1)
            for i in range(BH * NT):
                act.wait_ge(sc_max, i + 1)
                A(prob[i % 2], psum[2 + i % 2][:], ACT.Exp, bias=nmax[:, i % 2:i % 2 + 1],
                  accum_out=den[:, i:i + 1]).then_inc(p_exp, 1)
                act.wait_ge(pT_ps, i + 1)
                A(probT[i % 2], psum[4 + i % 2][:], ACT.Copy).then_inc(pT_ready, 1)
            act.wait_ge(catT_ps, 1)
            for n in range(4):
                last = A(catT[:, 2 * n:2 * n + 2, :], psum[n][:].rearrange("p (k t) -> p k t", k=2), ACT.Copy)
            last.then_inc(catT_ready, 1)

            def stats(ready, count, sq, sq_count):
                act.wait_ge(ready, count)
                for tt in range(NT):
                    ins = A(sq_out, h[:, tt], ACT.Square, accum_out=ss[:, tt:tt + 1])
                    if tt < NT - 1:
                        link(ins)
                ins.then_inc(sq, 1)
                act.wait_ge(sq, sq_count)

            def route(l):
                s = L
                act.wait_ge(s["u2T_ps"], l + 1)
                for n in range(4):
                    last = A(u2T[:, 2 * n:2 * n + 2, :], psum[n][:].rearrange("p (k t) -> p k t", k=2), ACT.Copy)
                last.then_inc(s["u2T"], 1)
                act.wait_ge(s["logits"], l + 1)
                A(rs[:, 16:48], psum[4][:, 0:32], ACT.Sigmoid).then_inc(s["scores"], 1)

            def high(sems, t, j, n, loads, base):
                act.wait_ge(loads[n % RING], base)
                for q in range(PARTS):
                    before = t * TP + (PARTS * j + q + 1 - PARTS)
                    if not isinstance(t, int) or before > 0:
                        act.wait_ge(sems["part"], before)
                    A(w_hi[q], slot(n)[:, q * PW:(q + 1) * PW], ACT.Copy).then_inc(sems["hi"], 1)

            def experts(sems, tb, n0, loads, land0, started):
                def weights(t, tile_, kind, e):
                    n = n0 + ITEM[kind, e]
                    high(sems, t, ITEM[kind, e], n, loads, tile_ * (16 * NM // RING) + (land0 + landed(n)))

                def gathered(t):
                    act.wait_ge(sems["xg_ps"], t + 1)
                    for n in range(2):
                        last = A(x_hi[:, 4 * n:4 * n + 4, :],
                                 psum[2 + n][:].rearrange("p (k n) -> p k n", k=4)[:, :, 0:CAP], ACT.Copy)
                    last.then_inc(sems["xg_hi"], 1)

                def silu(t, e):
                    act.wait_ge(*consumed(sems, t, ITEM["g", e]))
                    A(sg[0:CAP], psum[2 * (e % 2)][0:CAP, :], ACT.Silu).then_inc(sems["silu"], 1)

                def hidden(t, e):
                    act.wait_ge(sems["hT_ps"], t * NE + (e + 1))
                    A(hT_hi, psum[4][:].rearrange("p (c n) -> p c n", c=4)[:, :, 0:CAP],
                      ACT.Copy).then_inc(sems["hT_hi"], 1)

                def tile(t, i, more):
                    for e in range(1, NE):
                        weights(t, i, "g", e)
                        weights(t, i, "u", e)
                        hidden(t, e - 1)
                        silu(t, e)
                        weights(t, i, "d", e - 1)
                    weights(t, i, "d", NE - 1)
                    hidden(t, NE - 1)
                    if more:
                        gathered(t + 1)
                        weights(t + 1, i + 1, "g", 0)
                    act.wait_ge(*consumed(sems, t, ITEM["d", NE - 1]))
                    for nh in range(2):
                        last = A(yg_hi[0:CAP, nh * F:(nh + 1) * F], psum[5 + nh][0:CAP, :], ACT.Copy)
                    last.then_inc(sems["yg_hi"], 1)
                    if more:
                        weights(t + 1, i + 1, "u", 0)
                        silu(t + 1, 0)

                if not started:
                    weights(tb, 0, "g", 0)
                gathered(tb)
                weights(tb, 0, "u", 0)
                silu(tb, 0)
                with act.Fori(0, NG - 1) as i:
                    tile(i + tb, i, True)
                tile(tb + NG - 1, NG - 1, False)

            def moe(l):
                n0 = (N_MOE0, N_MOE1)[l]
                high(PASS[0], l * NG, 0, n0, loaded, landed(n0))
                route(l)
                experts(PASS[0], l * NG, n0, loaded, 0, True)
                act.wait_ge(L["routed"], l + 1)
                go = act.value_load(flag[0:1, l:l + 1])
                with act.If(go > 0):
                    act.wait_ge(PASS[0]["scat"], (l + 1) * NG + 1)
                    experts(PASS[1], l * NG, 0, ov_loaded, l * 16 * NG * NM // RING, False)
                    act.wait_ge(PASS[1]["scat"], (l + 1) * NG + 1)
                with act.Else():
                    count_skipped(act, "act")

            stats(h1_ready, 4, L["sq"], 1)
            moe(0)
            stats(L["h_ready"], 1, fin_sq, 1)
            stats(pool_h, 1, L["sq"], 2)
            moe(1)
            stats(L["h_ready"], 2, fin_sq, 2)

        @block.vector
        def _(dve):
            V = nc.vector
            link = linker(dve, dve_chain)
            dve.wait_ge(par_ps, 1)
            V.tensor_copy(parT[:], psum[0][:, 0:40]).then_inc(par_T, 1)
            dve.wait_ge(par_T, 1)
            l0, l1 = parT[:, 24:32], parT[:, 32:40]
            link(V.tensor_tensor(lbw[:, 16:24], l0, l1, ALU.max))
            V.tensor_tensor(lbw[:, 0:8], l0, lbw[:, 16:24], ALU.subtract)
            V.tensor_tensor(lbw[:, 8:16], l1, lbw[:, 16:24], ALU.subtract).then_inc(lb_arg, 1)
            dve.wait_ge(sig_c, 1)
            link(V.tensor_tensor(silc, silc, parT[:, 0:16], ALU.mult))
            for w in range(2):
                last = V.tensor_copy(csil[:, :, 16 * w:16 * w + 16],
                                     silc[:, 8 * w:8 * w + 8].unsqueeze(2).to_broadcast([P, KC, 16]))
            last.then_inc(csil_ready, 1)
            dve.wait_ge(lb_exp, 1)
            link(V.tensor_tensor(lbw[:, 16:24], lbw[:, 0:8], lbw[:, 8:16], ALU.add))
            link(V.reciprocal(lbw[:, 24:32], lbw[:, 16:24]))
            V.tensor_tensor(lbw[:, 32:40], lbw[:, 0:8], lbw[:, 24:32], ALU.mult)
            link(V.tensor_tensor(lbw[:, 40:48], lbw[:, 8:16], lbw[:, 24:32], ALU.mult))
            link(V.tensor_tensor(lbs[:, 0:8], lbw[:, 32:40], lbw[:, 40:48], ALU.add))
            link(V.tensor_tensor(lbs[:, 0:8], lbs[:, 0:8], lbw[:, 32:40], ALU.subtract))
            link(V.tensor_scalar(lbs[:, 8:16], lbs[:, 0:8], -1.0, 1.0, ALU.mult, ALU.add))
            dve.wait_ge(sq_done, 1)
            V.tensor_scalar(ms, ss, 1.0 / D, EPS, ALU.mult, ALU.add).then_inc(ms_ready, 1)
            dve.wait_ge(rstd_ready, 1)
            for tt in range(4):
                src = h[:, tt] if tt < NT else cx[:, tt - NT]
                dst = xnl[:, tt] if tt < NT else cx[:, tt - NT]
                V.tensor_scalar(dst, src, rstd[:, tt:tt + 1], None, ALU.mult).then_inc(xn_ready, 1)

            def mod_rows_out(b):
                dve.wait_ge(mod_used, 4 * b + 4)
                dve.wait_ge(s_bm, 48)
                V.tensor_tensor(modrow[:, b, :], psum[MOD_BANK][:], modrow[:, b, :], ALU.add).then_inc(mod_rows, 1)

            mod_rows_out(0)
            dve.wait_ge(modT_ps, 1)
            for j in range(4):
                last = V.tensor_copy(modT[:, 4 * j:4 * j + 4, :], psum[2 + j][:, 0:8].rearrange("p (a b) -> p a b", a=4))
            link(last)
            V.scalar_tensor_tensor(A1T, modT[:, KC:2 * KC, :], 1.0,
                                   parT[:, 16:24].unsqueeze(2).to_broadcast([P, KC, 2]), ALU.add,
                                   ALU.mult).then_inc(A1_ready, 1)
            dve.wait_ge(A1_ready, 1)
            for k in range(0, KC, 2):
                dve.wait_ge(uT_ps, k + 1)
                for w in range(2):
                    last = V.tensor_scalar(uT[:, k, w * T:(w + 1) * T], psum[k][:, w * T:(w + 1) * T],
                                           A1T[:, k, w:w + 1], modT[:, k, w:w + 1], ALU.mult, ALU.add)
                last.then_inc(uT_dve, 1)
            dve.wait_ge(uT_dve, KC // 2)
            dve.wait_ge(uT_act, KC // 2)
            for d in range(2):
                for hd in range(H):
                    i = d * H + hd
                    dve.wait_ge(proj_out, 4 + i + 1)
                    link(V.tensor_scalar(lf[:, i, :], lf[:, i, :], lbs[:, 8 + i:9 + i], lbs[:, i:i + 1], ALU.mult, ALU.add))
                    V.tensor_scalar(kl[:, i, :], lf[:, i, 0:T], -1.0, 1.0, ALU.mult, ALU.add)
                    last = V.tensor_scalar(kc[:, i, :], lf[:, i, T:2 * T], -1.0, 1.0, ALU.mult, ALU.add)
                last.then_inc(f_ready, 1)
            dve.wait_ge(s_an, 16)
            for m in range(NT):
                dve.wait_ge(proj_done, U_END[Q_A] + m + 1)
                dve.wait_ge(g_sig, m + 1)
                V.tensor_tensor(gn[:, m, :], psum[PROJ_BANKS[(U_END[Q_A] + m) % 3]][:], gn[:, m, :],
                                ALU.mult).then_inc(g_out, 1)
                dve.wait_ge(g_out, m + 1)
                link(V.tensor_tensor(gn[:, m, :], gn[:, m, :], anorm, ALU.mult))
            dve.wait_ge(masks_ready, 1)
            link(V.memset(X[:, :, :, 0:1], 0.0))
            for d in range(2):
                dve.wait_ge(lf_ready, d + 1)
                for hd in range(H):
                    i = d * H + hd
                    for w in range(2):
                        last = V.tensor_tensor_scan(X[:, i, w, 1:T + 1], cst[:, C_ONES:C_ONES + 1].to_broadcast([P, T]),
                                                    lf[:, i, w * T:(w + 1) * T], 0.0, ALU.mult, ALU.add)
                last.then_inc(X_ready, 1)
            dve.wait_ge(X_ready, 2)
            dve.wait_ge(kcd_exp, 1)
            V.tensor_tensor(kcd, kcd, kc, ALU.mult).then_inc(kcd_ready, 1)
            dve.wait_ge(qt_exp, 1)
            for d in range(2):
                last = V.tensor_tensor(qt[:, d], qt[:, d], qa, ALU.mult)
            last.then_inc(qt_ready, 1)
            dve.wait_ge(kcdT_ps, 1)
            for n in range(4):
                last = V.tensor_copy(kcdT[:, n // 2, (n % 2) * 4:(n % 2) * 4 + 4, :],
                                     psum[n][:].rearrange("p (a b) -> p a b", a=4))
            last.then_inc(kcdT_ready, 1)
            dve.wait_ge(S_ps, 1)
            for n in range(2):
                last = V.tensor_copy(S[:, 4 * n:4 * n + 4, :], psum[n][:].rearrange("p (a b) -> p a b", a=4))
            last.then_inc(S_ready, 1)

            def halves(a, m, second):
                b = a.rearrange("p h (b f m) -> p h b f m", f=2, m=m)
                return b[:, :, :, 1, :] if second else b[:, :, :, 0, :]

            def level_args(lev):
                m = LEVELS[lev]
                if lev >= 2:
                    dve.wait_ge(gram, lev - 1)
                for d in range(2):
                    x0 = X[:, d * H:(d + 1) * H, 0, 0:T]
                    x1 = X[:, d * H:(d + 1) * H, 0, 1 - d:1 - d + T]
                    mid = halves(x0, m, True)[:, :, :, 0:1].to_broadcast([P, H, P // m, m])
                    z = Z[lev % 2][:, d * H:(d + 1) * H, :]
                    V.tensor_tensor(halves(z, m, False), mid, halves(x1, m, False), ALU.subtract)
                    last = V.tensor_tensor(halves(z, m, True), halves(x1, m, True), mid, ALU.subtract)
                last.then_inc(z_arg, 1)

            def level_mult(lev):
                m = LEVELS[lev]
                dve.wait_ge(z_exp, lev + 1)
                for d in range(2):
                    z = Z[lev % 2][:, d * H:(d + 1) * H, :]
                    kk = kl[:, d * H:(d + 1) * H, :]
                    for second in (False, True):
                        src = qa if second == (d == 0) else kk
                        last = V.tensor_tensor(halves(z, m, second), halves(z, m, second), halves(src, m, second), ALU.mult)
                last.then_inc(z_ready, 1)

            def level_merge(lev):
                dve.wait_ge(gram, lev + 1)
                if lev == 0:
                    dve.wait_ge(atd_zero, 1)
                    V.tensor_copy(ATo[:, 0], psum[0][:].rearrange("p (a b) -> p a b", a=H))
                    V.tensor_copy(ATo[:, 1], psum[1][:].rearrange("p (a b) -> p a b", a=H)).then_inc(merged, 1)
                    return
                diag = lev == NLEV - 1
                pairs = [(0, tt) for tt in range(NT)] if diag else [(d, tt) for d in range(2) for tt in range(NT)]
                for n, (d, tt) in enumerate(pairs):
                    mask = masks[:, 14 if diag else 2 * (lev - 1) + d, :].unsqueeze(1).to_broadcast([P, H, P])
                    ins = V.copy_predicated(ATd[:, tt], mask, psum[2 * d + tt][:].rearrange("p (a b) -> p a b", a=H))
                    if n < len(pairs) - 1:
                        link(ins)
                ins.then_inc(merged, 1)
                dve.wait_ge(merged, lev + 1)

            level_args(0)
            level_mult(0)
            for lev in range(NLEV):
                if lev + 1 < len(LEVELS):
                    level_args(lev + 1)
                if lev:
                    for what in FILL[lev]:
                        if isinstance(what, str):
                            mod_rows_out(int(what[1:]))
                level_merge(lev)
                if lev + 1 < len(LEVELS):
                    level_mult(lev + 1)
            for what in FILL[NLEV]:
                if isinstance(what, str):
                    mod_rows_out(int(what[1:]))
            for tt in range(NT):
                dve.wait_ge(osq, tt + 1)
                V.tensor_scalar(ssq[:, tt * H:(tt + 1) * H], ssq[:, tt * H:(tt + 1) * H], 1.0 / DK, EPS, ALU.mult,
                                ALU.add).then_inc(ro_ready, 1)
            for tt in range(NT):
                dve.wait_ge(ro_rstd, tt + 1)
                for hd in range(H):
                    last = V.scalar_tensor_tensor(cat[:, tt, hd * P:(hd + 1) * P], psum[tt][:, hd * P:(hd + 1) * P],
                                                  rstdo[:, tt * H + hd:tt * H + hd + 1],
                                                  gn[:, tt, hd * P:(hd + 1) * P], ALU.mult, ALU.mult)
                last.then_inc(a_ready, 1)
            for i in range(BH * NT):
                bank = psum[2 + i % 2]
                dve.wait_ge(sc_ps, i + 1)
                V.tensor_reduce(nmax[:, i % 2:i % 2 + 1], bank[:], axis=AX.X, op=ALU.max, negate=True).then_inc(sc_max, 1)
            dve.wait_ge(pv_done, BH * NT)
            link(V.reciprocal(rden, den))
            for tt in range(NT):
                r = rden.rearrange("p (h q) -> p h q", q=NT)[:, :, tt:tt + 1].to_broadcast([P, BH, DH])
                last = V.tensor_tensor(cat[:, tt, F:2 * F].rearrange("p (h d) -> p h d", h=BH),
                                       psum[6 + tt][:].rearrange("p (h d) -> p h d", h=BH), r, ALU.mult)
            last.then_inc(cat_ready, 1)

            def broadcast_out(n, first):
                dve.wait_ge(bc_ps, n + 1)
                for j in range(4):
                    p = first % 6 + j // 2
                    dst = MB[:, p, (j % 2) * F:(j % 2 + 1) * F]
                    if p in (1, 4):
                        dve.wait_ge(mb_dma, 16 if first < 6 else 48)
                        last = V.scalar_tensor_tensor(dst, psum[j][:], 1.0, dst, ALU.add, ALU.mult)
                    else:
                        last = V.tensor_copy(dst, psum[j][:])
                last.then_inc(bc_out, 1)
                dve.wait_ge(bc_out, n + 1)

            broadcast_out(0, 2)
            for n in range(4):
                nh, tt = n // 2, n % 2
                dve.wait_ge(y_done, n + 1)
                link(V.tensor_tensor(ytmp[:, n % 2, :], psum[4 + n][:], MB[:, 2, nh * F:(nh + 1) * F], ALU.mult))
                V.tensor_tensor(h[:, tt, nh * F:(nh + 1) * F], h[:, tt, nh * F:(nh + 1) * F], ytmp[:, n % 2, :],
                                ALU.add).then_inc(h1_ready, 1)
            broadcast_out(1, 4)

            def mean_square(sq, count, out_sem):
                dve.wait_ge(sq, count)
                V.tensor_scalar(ms[:, 0:NT], ss[:, 0:NT], 1.0 / D, EPS, ALU.mult, ALU.add).then_inc(out_sem, 1)

            def norm_mod(rstd_sem, count, gain, shift, done, done_count):
                dve.wait_ge(rstd_sem, count)
                for tt in range(NT):
                    link(V.scalar_tensor_tensor(u2[:, tt], h[:, tt], rstd[:, tt:tt + 1], MB[:, gain], ALU.mult, ALU.mult))
                    V.tensor_tensor(u2[:, tt], u2[:, tt], MB[:, shift], ALU.add).then_inc(done, 1)
                dve.wait_ge(done, done_count)

            G, gc, s_, sbi = rs[:, 0:8], rs[:, 8:16], rs[:, 16:48], rs[:, 48:80]
            d1, d2, d3 = rs[:, 80:104], rs[:, 104:120], rs[:, 120:128]
            gsc, gm, w4 = rs[:, 128:136], rs[:, 136:138], rs[:, 138:146]
            m16, o1, m2 = rs[:, 146:178], rs[:, 178:210], rs[:, 210:242]
            t32, red, gts = rs[:, 242:274], rs[:, 274:276], rs[:, 276:308]
            rk, cnt, rg = rs[:, 308:316], rs[:, 316:318], rs[:, 320:328]
            gslot = rs[:, 328:332]

            def v3(a, b, c_):
                return a.rearrange("p (a b c) -> p a b c", a=NT, b=b, c=c_)

            def v2(a, b):
                return a.rearrange("p (a b) -> p a b", a=NT, b=b)

            def bc1(a, n):
                return a.unsqueeze(2).to_broadcast([P, NT, n])

            def first_max(dst, src, n, weights, tmp):
                link(V.tensor_reduce(red, v2(src, n), axis=AX.X, op=ALU.max))
                link(V.tensor_tensor(v2(tmp, n), v2(src, n), bc1(red, n), ALU.is_equal))
                link(V.tensor_tensor(v2(tmp, n), v2(tmp, n), weights.unsqueeze(1).to_broadcast([P, NT, n]), ALU.mult))
                link(V.tensor_reduce(red, v2(tmp, n), axis=AX.X, op=ALU.max))
                link(V.tensor_tensor(v2(dst, n), v2(tmp, n), bc1(red, n), ALU.is_equal))

            def route(l):
                s = L
                dve.wait_ge(s["scores"], l + 1)
                link(V.tensor_tensor(v2(sbi, 16), v2(s_, 16), brt.unsqueeze(1).to_broadcast([P, NT, 16]), ALU.add))
                a = v3(sbi, NG, NE)
                V.tensor_tensor(v3(d1, NG, 3), a[:, :, :, 0:3], a[:, :, :, 1:4], ALU.add)
                V.tensor_tensor(v3(d2, NG, 2), a[:, :, :, 0:2], a[:, :, :, 2:4], ALU.add)
                link(V.tensor_tensor(v3(d3, NG, 1), a[:, :, :, 0:1], a[:, :, :, 3:4], ALU.add))
                V.tensor_reduce(v2(gsc, NG), v3(d1, NG, 3), axis=AX.X, op=ALU.max)
                link(V.tensor_reduce(v2(w4, NG), v3(d2, NG, 2), axis=AX.X, op=ALU.max))
                link(V.tensor_tensor(gsc, gsc, w4, ALU.max))
                link(V.tensor_tensor(gsc, gsc, d3, ALU.max))
                first_max(G, gsc, NG, cst[:, C_W4:C_W4 + 4], w4)
                in_g = v2(G, NG).unsqueeze(3).to_broadcast([P, NT, NG, NE])
                link(V.tensor_scalar(w4, G, -NEG, NEG, ALU.mult, ALU.add))
                link(V.tensor_tensor(v3(m16, NG, NE), v3(sbi, NG, NE), in_g, ALU.mult))
                link(V.tensor_tensor(v3(m16, NG, NE), v3(m16, NG, NE),
                                     v2(w4, NG).unsqueeze(3).to_broadcast([P, NT, NG, NE]), ALU.add))
                first_max(o1, m16, 16, cst[:, C_W16:C_W16 + 16], t32)
                link(V.scalar_tensor_tensor(m16, o1, 2 * NEG, m16, ALU.mult, ALU.add))
                first_max(m2, m16, 16, cst[:, C_W16:C_W16 + 16], t32)
                link(V.tensor_tensor(o1, o1, m2, ALU.add))
                link(V.tensor_tensor(gts, o1, s_, ALU.mult))
                link(V.tensor_reduce(red, v2(gts, 16), axis=AX.X, op=ALU.add))
                link(V.reciprocal(red, red))
                link(V.tensor_tensor(v2(gts, 16), v2(gts, 16), bc1(red, 16), ALU.mult))
                V.tensor_reduce(v2(gc, NE), v3(gts, NG, NE).rearrange("p a g e -> p a e g"), axis=AX.X,
                                op=ALU.add).then_inc(s["gates"], 1)
                dve.wait_ge(s["ranks"], l + 1)
                link(V.tensor_scalar(rk, psum[5][:, 0:8], 1.0, None, ALU.add))
                link(V.tensor_tensor(rk, rk, G, ALU.mult))
                V.tensor_scalar(rg, rk, -1.0, None, ALU.add)
                link(V.tensor_reduce(cnt[:, 0:1], psum[5][:, 8:12], axis=AX.X, op=ALU.max))
                V.tensor_scalar(flag[0:1, l:l + 1], cnt[0:1, 0:1], CAP + 0.5, None, ALU.is_gt).then_inc(s["routed"], 1)
                dve.wait_ge(s["routed"], l + 1)

            def low(sems, t, j, n, qs=range(PARTS)):
                for q in qs:
                    dve.wait_ge(sems["hi"], t * TP + (PARTS * j + q + 1))
                    V.tensor_tensor(w_lo[q], slot(n)[:, q * PW:(q + 1) * PW], w_hi[q].bitcast(F32),
                                    ALU.subtract).then_inc(sems["lo"], 1)

            def experts(sems, tb, n0, started):
                def weights(t, kind, e, qs=range(PARTS)):
                    low(sems, t, ITEM[kind, e], n0 + ITEM[kind, e], qs)

                def choose(t, i):
                    for tt in range(NT):
                        last = V.tensor_scalar(Pg[:, tt, :], cst[:, C_IOTA:C_IOTA + P], rg[:, bass.ds(i + 4 * tt, 1)],
                                               None, ALU.is_equal)
                    last.then_inc(sems["p_ready"], 1)

                def slots_of(t):
                    dve.wait_ge(sems["route_ps"], t + 1)
                    V.tensor_copy(gslot[0:CAP], psum[7][0:CAP, 0:4])
                    V.tensor_copy(PT[0:CAP], psum[7][0:CAP, P:3 * P].rearrange("p (a b) -> p a b", a=NT)).then_inc(sems["gs"], 1)
                    dve.wait_ge(sems["gs"], t + 1)

                def gathered(t):
                    dve.wait_ge(sems["xg_hi"], t + 1)
                    for n in range(2):
                        last = V.tensor_tensor(x_lo[:, 4 * n:4 * n + 4, :],
                                               psum[2 + n][:].rearrange("p (k n) -> p k n", k=4)[:, :, 0:CAP],
                                               x_hi[:, 4 * n:4 * n + 4, :].bitcast(F32), ALU.subtract)
                    last.then_inc(sems["xg_lo"], 1)

                def gate_hidden(t, e):
                    dve.wait_ge(sems["silu"], t * NE + (e + 1))
                    dve.wait_ge(*consumed(sems, t, ITEM["u", e]))
                    V.scalar_tensor_tensor(hh[0:CAP], sg[0:CAP], gslot[0:CAP, e:e + 1], psum[2 * (e % 2) + 1][0:CAP, :],
                                           ALU.mult, ALU.mult).then_inc(sems["hid"], 1)

                def hidden(t, e):
                    dve.wait_ge(sems["hT_hi"], t * NE + (e + 1))
                    V.tensor_tensor(hT_lo, psum[4][:].rearrange("p (c n) -> p c n", c=4)[:, :, 0:CAP],
                                    hT_hi.bitcast(F32), ALU.subtract).then_inc(sems["hT_lo"], 1)

                def add(n):
                    tt, nh = n // 2, n % 2
                    return V.tensor_tensor(yacc[:, tt, nh * F:(nh + 1) * F], psum[SCAT_BANKS[n]][:],
                                           yacc[:, tt, nh * F:(nh + 1) * F], ALU.add)

                def tile(t, i, more):
                    slots_of(t)
                    for e in range(1, NE):
                        weights(t, "g", e)
                        gate_hidden(t, e - 1)
                        weights(t, "u", e)
                        hidden(t, e - 1)
                        weights(t, "d", e - 1)
                    gate_hidden(t, NE - 1)
                    if more:
                        choose(t + 1, i + 1)
                    weights(t, "d", NE - 1)
                    hidden(t, NE - 1)
                    if more:
                        gathered(t + 1)
                        weights(t + 1, "g", 0)
                    dve.wait_ge(sems["yg_hi"], t + 1)
                    for nh in range(2):
                        last = V.tensor_tensor(yg_lo[0:CAP, nh * F:(nh + 1) * F], psum[5 + nh][0:CAP, :],
                                               yg_hi[0:CAP, nh * F:(nh + 1) * F].bitcast(F32), ALU.subtract)
                    last.then_inc(sems["yg_lo"], 1)
                    if more:
                        weights(t + 1, "u", 0, range(0, 2))
                    dve.wait_ge(sems["scat_ps"], t + 1)
                    add(0)
                    add(1)
                    if more:
                        weights(t + 1, "u", 0, range(2, PARTS))
                    add(2)
                    add(3).then_inc(sems["scat"], 1)
                    dve.wait_ge(sems["scat"], t + 2)

                choose(tb, 0)
                if not started:
                    weights(tb, "g", 0)
                gathered(tb)
                weights(tb, "u", 0)
                with dve.Fori(0, NG - 1) as i:
                    tile(i + tb, i, True)
                tile(tb + NG - 1, NG - 1, False)

            def moe(l):
                n0 = (N_MOE0, N_MOE1)[l]
                low(PASS[0], l * NG, 0, n0)
                route(l)
                dve.wait_ge(L["yacc0"], l + 1)
                if l == 0:
                    for k in range(2):
                        dve.sem_inc(PASS[k]["scat"], 1)
                experts(PASS[0], l * NG, n0, True)
                go = dve.value_load(flag[0:1, l:l + 1])
                with dve.If(go > 0):
                    V.tensor_scalar(rg, rg, -float(CAP), None, ALU.add).then_inc(ov_chain, 1)
                    dve.wait_ge(ov_chain, l + 1)
                    experts(PASS[1], l * NG, 0, False)
                with dve.Else():
                    dve.sem_inc(ov_chain, 1)
                    count_skipped(dve, "dve")
                for tt in range(NT):
                    link(V.tensor_tensor(yacc[:, tt], yacc[:, tt], MB[:, 5], ALU.mult))
                    ins = V.tensor_tensor(h[:, tt], h[:, tt], yacc[:, tt], ALU.add)
                    if tt == 0:
                        link(ins)
                ins.then_inc(L["h_ready"], 1)
                dve.wait_ge(L["h_ready"], l + 1)

            dve.wait_ge(h1_ready, 4)
            mean_square(L["sq"], 1, L["ms"])
            norm_mod(L["rstd"], 1, 4, 3, L["u2"], NT)
            dve.wait_ge(s_rt, 32)
            moe(0)
            for n, first in enumerate((6, 8, 10)):
                broadcast_out(2 + n, first)
            dve.wait_ge(s_scl, 16)
            link(V.tensor_tensor(MB[:, 2], MB[:, 2], scl, ALU.mult))
            mean_square(fin_sq, 1, fin_ms)
            norm_mod(fin_rstd, 1, 1, 0, pool_u, NT)
            dve.wait_ge(pool_ps, 1)
            for g in range(4):
                last = V.tensor_copy(pT[:, 2 * g:2 * g + 2, :], psum[g][:].rearrange("p (a b) -> p a b", a=2))
            last.then_inc(pool_T, 1)
            for n in range(4):
                tt, gh = n // 2, n % 2
                dve.wait_ge(pool_y, n + 1)
                link(V.tensor_tensor(mtmp[:, n % 2 * F:(n % 2 + 1) * F], psum[4 + n][:], MB[:, 2, gh * F:(gh + 1) * F], ALU.mult))
                ins = V.tensor_tensor(h[:, tt, gh * F:(gh + 1) * F], h[:, tt, gh * F:(gh + 1) * F],
                                      mtmp[:, n % 2 * F:(n % 2 + 1) * F], ALU.add)
                if n < 3:
                    link(ins)
            ins.then_inc(pool_h, 1)
            dve.wait_ge(pool_h, 1)
            mean_square(L["sq"], 2, L["ms"])
            norm_mod(L["rstd"], 2, 4, 3, L["u2"], 2 * NT)
            moe(1)
            mean_square(fin_sq, 2, fin_ms)
            dve.wait_ge(fin_rstd, 2)
            dve.wait_ge(s_scl, 32)
            for tt in range(NT):
                V.scalar_tensor_tensor(mtmp[:, tt * D:(tt + 1) * D], h[:, tt], rstd[:, tt:tt + 1], scl, ALU.mult,
                                       ALU.mult).then_inc(fin_out, 1)

        @block.gpsimd
        def _(pool):
            Gp = nc.gpsimd

            Gp.memset(modrow[:], 0.0).then_inc(modrow_zero, 1)
            pool.wait_ge(modrow_zero, 1)
            for l in range(2):
                pool.dma_start(modrow[0:P:32, 3 * l:3 * l + 3, :],
                               b_mod[l].rearrange("(b j n) -> j b n", b=3, j=4)).then_inc(s_bm, 16)
            pool.dma_start(modrow[16:P:32, 0, :], b_mod[0, 0:2048].rearrange("(j n) -> j n", j=4)).then_inc(s_bm, 16)
            pool.dma_start(masksf, masks_d).then_inc(s_masks, 16)
            pool.dma_start(anorm, a_norm_g[0:1, :].to_broadcast([P, F])).then_inc(s_an, 16)

            pool.wait_ge(s_masks, 16)
            Gp.tensor_copy(masks[:], masksf).then_inc(masks_ready, 1)

            def power(ready, count, dst, src, done):
                pool.wait_ge(ready, count)
                Gp.tensor_tensor(dst, src, half.to_broadcast([P, src.shape[1]]), ALU.pow).then_inc(done, 1)

            pool.wait_ge(sq_done, 1)
            power(ms_ready, 1, rstd, ms, rstd_ready)

            pool.wait_ge(kcdT_ps, 1)
            Gp.memset(ATd, 0.0).then_inc(atd_zero, 1)

            def load_bias(i):
                hd, qi = i // NT, i % NT
                for half_ in range(2):
                    r = 2 * qi + half_
                    off = hd * RPB_R * RPB_C + (7 - r) * RPB_C + 15 - (GW - 1)
                    src = bass.AP(tensor=rpb.tensor, offset=off, ap=[[1, GW], [RPB_C, 4], [1, GW]])
                    pool.dma_start(bias[i % 4][half_ * GW:(half_ + 1) * GW].rearrange("p (a b) -> p a b", a=4),
                                   src).then_inc(b_dma[i % 4], 16)

            pool.wait_ge(merged, NLEV)
            for i in range(4):
                load_bias(i)
            for i in range(BH * NT):
                pool.wait_ge(b_dma[i % 4], 32 * (i // 4 + 1))
                Gp.tensor_tensor(bias[i % 4], bias[i % 4], cst[:, C_COLM:C_COLM + T], ALU.add).then_inc(b_ready, 1)
                if i == 2:
                    for tt in range(NT):
                        power(ro_ready, tt + 1, rstdo[:, tt * H:(tt + 1) * H], ssq[:, tt * H:(tt + 1) * H], ro_rstd)
                if i >= 3 and i + 1 < BH * NT:
                    pool.wait_ge(sc_ps, i - 2)
                    load_bias(i + 1)
            pool.wait_ge(a_ready, NT)
            pool.dma_start(MB[:, 4], norm2_g[0:1, :].to_broadcast([P, D])).then_inc(mb_dma, 16)
            pool.wait_ge(h1_ready, 4)
            pool.dma_start(wr, w_router.rearrange("(k p) e -> p k e", p=P)).then_inc(s_rt, 16)
            pool.dma_start(brt, b_router.rearrange("(a e) -> a e", a=1).to_broadcast([P, 16])).then_inc(s_rt, 16)
            pool.dma_start(scl, pool_scale[0:1, :].to_broadcast([P, D])).then_inc(s_scl, 16)

            Gp.memset(yacc, 0.0).then_inc(L["yacc0"], 1)
            power(L["ms"], 1, rstd[:, 0:NT], ms[:, 0:NT], L["rstd"])
            pool.wait_ge(L["h_ready"], 1)
            pool.dma_start(bands, bands_d.rearrange("(t p) g n -> p t g n", p=P)).then_inc(s_bands, 16)
            pool.dma_start(MB[:, 1], norm1_g[1:2, :].to_broadcast([P, D])).then_inc(mb_dma, 16)
            pool.dma_start(MB[:, 4], norm2_g[1:2, :].to_broadcast([P, D])).then_inc(mb_dma, 16)
            Gp.memset(yacc, 0.0).then_inc(L["yacc0"], 1)
            power(fin_ms, 1, rstd[:, 0:NT], ms[:, 0:NT], fin_rstd)
            pool.wait_ge(pool_h, 1)
            pool.dma_start(scl, final_g.rearrange("(a n) -> a n", a=1).to_broadcast([P, D])).then_inc(s_scl, 16)
            power(L["ms"], 2, rstd[:, 0:NT], ms[:, 0:NT], L["rstd"])
            power(fin_ms, 2, rstd[:, 0:NT], ms[:, 0:NT], fin_rstd)


_INS = ["x", "c", "ctx", "c_ctx", "w_mod", "b_mod", "norm1_g", "norm2_g", "w_in", "w_out", "lb_logits", "a_norm_g",
        "rpb", "w_pool", "pool_scale", "w_router", "b_router", "w_gate", "w_up", "w_down", "final_g"]
_CONSTS = ["cst", "masks", "bands"]


def kernel(**inputs):
    import concourse.bacc as bacc
    from concourse.bass_utils import run_bass_kernel_spmd

    nc = bacc.Bacc("TRN2", target_bir_lowering=False, num_devices=1)
    named = {name: np.ascontiguousarray(inputs[name]) for name in _INS}
    named.update(zip(_CONSTS, shape_constants()))
    arrays, args = {}, []
    for name, a in named.items():
        arrays[f"in_{name}"] = a
        args.append(nc.dram_tensor(f"in_{name}", a.shape, mybir.dt.from_np(a.dtype), kind="ExternalInput").ap())
    out = nc.dram_tensor("out_0", (1, T, D), F32, kind="ExternalOutput").ap()
    build(nc, *args, out)
    r = run_bass_kernel_spmd(nc, [arrays], core_ids=[0])
    return r.results[0]["out_0"]
```

```python
from contextlib import ExitStack

import numpy as np

import concourse.bass as bass
from concourse import mybir

F32 = mybir.dt.float32
F32R = mybir.dt.float32r
U8 = mybir.dt.uint8
I32 = mybir.dt.int32
ACT = mybir.ActivationFunctionType
ALU = mybir.AluOpType
AX = mybir.AxisListType

P = 128
D = 1024
KC = D // P
T = 256
NT = T // P
F = 512
H = 4
DK = 128
BH = 8
DH = 64
GW = 64
RPB_R, RPB_C = 15, 31
NG, NE = 4, 4
EPS = 1e-6
CAP = 128
RING = 4
PARTS = 4
PW = KC * F // PARTS
NEG = -1.0e30

C_ID, C_TRI, C_IOTA, C_SEL, C_ONES, C_COLM = 0, 128, 256, 384, 512, 640
C_W4, C_W16, C_E2, C_REV, C_GROW, C_N = 896, 900, 916, 918, 1046, 1049
LEVELS = (128, 64, 32, 16, 8, 4, 2, 1)
WINDOWS = (2, 4, 8, 16)


def shape_constants():
    cst = np.zeros((P, C_N), np.float32)
    i = np.arange(P)
    cst[:, C_ID:C_ID + P] = np.eye(P)
    cst[:, C_TRI:C_TRI + P] = i[:, None] < i[None, :]
    cst[:, C_IOTA:C_IOTA + P] = i[None, :]
    cst[:, C_SEL:C_SEL + P] = (i % 32 == 0)[:, None]
    cst[:, C_ONES:C_ONES + P] = 1.0
    col, key = i % GW, np.arange(T) % GW
    low = np.clip(col - 8, 0, GW - 16)
    inside = (key[None, :] >= low[:, None]) & (key[None, :] < low[:, None] + 16)
    backwards = i + GW - 1 - 2 * col
    cst[:, C_COLM:C_COLM + T] = np.where(inside, 0.0, NEG)[backwards]
    cst[i, C_REV + backwards] = 1.0
    for n, b in enumerate(GAIN_BANKS):
        cst[0:P:32, C_GROW + n] = [GAIN_PIECES[b][0] <= j < GAIN_PIECES[b][1] for j in range(4)]
    cst[:, C_W4:C_W4 + 4] = np.arange(4, 0, -1)
    cst[:, C_W16:C_W16 + 16] = np.arange(16, 0, -1)
    cst[:, C_E2] = i % 32 == 0
    cst[:, C_E2 + 1] = i % 32 == 16
    masks = np.zeros((P, 15, P), np.float32)
    for n, m in enumerate(LEVELS[1:]):
        same = (i[:, None] // (2 * m)) == (i[None, :] // (2 * m))
        first, second = i % (2 * m) < m, i % (2 * m) >= m
        masks[:, 2 * n] = same & first[:, None] & second[None, :]
        masks[:, 2 * n + 1] = same & second[:, None] & first[None, :]
    masks[:, 14] = np.eye(P)
    t = np.arange(T)
    bands = np.zeros((T, len(WINDOWS), T), np.float32)
    for g, w in enumerate(WINDOWS):
        lo, hi = np.clip(t - w // 2, 0, T), np.clip(t + w // 2, 0, T)
        inside = (t[:, None] >= lo[None, :]) & (t[:, None] < hi[None, :])
        bands[:, g] = inside / (hi - lo).astype(np.float32)[None, :] - np.eye(T)
    return cst, masks, bands


Q_A, F_F, F_B, I_A, G_A, Q_B, K_B, V_B = range(8)
UNITS = ([(I_A, m) for m in range(4)] + [(G_A, m) for m in range(2)] + [(F_F, m) for m in range(4)]
         + [(F_B, m) for m in range(4)] + [(Q_A, m) for m in range(4)] + [(K_B, m) for m in range(4)]
         + [(Q_B, m) for m in range(4)] + [(V_B, m) for m in range(4)])
U_END = {p: max(n for n, u in enumerate(UNITS) if u[0] == p) + 1 for p in range(8)}
U_EARLY = U_END[Q_A]
MODS = (0, 2, 3, 5, 1, 4)
MPOS = {b: n for n, b in enumerate(MODS)}
GAIN_BANKS = (2, 3, 5)
GAIN_PIECES = {2: (0, 2), 3: (2, 4), 5: (0, 2)}
SPLIT_PROJ = (I_A, G_A, F_F, F_B)
Q_AFTER = ((4, 6), (2, 5), (2, 5), (2, 5))
W_BUFS = 3
_m = "m"
PLAN = [
    [14, _m, 15, _m, 16, 17],
    [18, _m], [19, _m], [20], [21], [22, _m], [23, _m], [24], [25], [26, _m], [27, _m], [28, 29], [_m, _m, _m, _m],
]


def number_quarters():
    n = 4 + sum(len(a) for a in Q_AFTER)
    for stage in PLAN:
        for at, what in enumerate(stage):
            if what == _m:
                stage[at] = ("mod", MODS[n // 4], n % 4)
                n += 1
    assert n == 4 * len(MODS)


number_quarters()


def split_quarter(n, i):
    q = 4 + sum(len(a) for a in Q_AFTER[:n]) + i
    return ("mod", MODS[q // 4], q % 4)


def ring_order():
    order = [("mod", MODS[0], q) for q in range(4)]
    for n, p in enumerate(SPLIT_PROJ):
        order += [("in", p)] + [split_quarter(n, i) for i in range(len(Q_AFTER[n]))]
    for stage in PLAN:
        if stage is PLAN[-1]:
            order += [("out", 0), ("out", 1)]
        for what in stage:
            item = ("in", UNITS[what][0]) if isinstance(what, int) else what
            if item not in order:
                order.append(item)
    return order


RING_A = ring_order()


def ends(stage):
    return [w[1] for w in PLAN[stage] if not isinstance(w, int) and w[2] == 3]


MOE_ORDER = [("g", 0), ("u", 0), ("g", 1), ("u", 1), ("d", 0), ("g", 2), ("u", 2), ("d", 1),
             ("g", 3), ("u", 3), ("d", 2), ("d", 3)]
NM = len(MOE_ORDER)
ITEM = {item: n for n, item in enumerate(MOE_ORDER)}
N_MOE0 = len(RING_A)
N_POOL = N_MOE0 + NG * NM
N_MOE1 = N_POOL + 1
SLOT_A = {item: n for n, item in enumerate(RING_A)}

NLEV = len(LEVELS) + 1
K_ORDER = (0, 1, 6, 2, 3, 4, 5, 7)
K_FIRST = 3
SPREAD = [(p, (0, 1)) for p in (2, 3, 4, 5, 6, 7)] + [(10, (5, 6)), (8, (0, 1)), (9, (2, 3)), (11, (4, 5))]
S_AT = (4, 6, 8, 10, 12, 14)
CAT_AT = 3
OUT_AT = 8
N_BIAS = 8
PROJ_BANKS = (4, 5, 6)
SCAT_BANKS = (2, 3, 4, 7)
SPLIT_BANKS = K_ORDER[:7]
MOD_BANK = 7


def build(nc, x, c, ctx, c_ctx, w_mod, b_mod, norm1_g, norm2_g, w_in, w_out, lb_logits, a_norm_g, rpb,
          w_pool, pool_scale, w_router, b_router, w_gate, w_up, w_down, final_g, cst_d, masks_d, bands_d, out):
    with ExitStack() as stack:
        def sb(name, shape, dt=F32):
            return stack.enter_context(nc.sbuf_tensor("sb_" + name, shape, dt))

        def sem(name):
            return stack.enter_context(nc.semaphore(name))

        ring = sb("ring", [P, RING, KC * F])
        h = sb("h", [P, NT, D])
        cst = sb("cst", [P, C_N])
        masks = sb("masks", [P, 15, P], U8)
        modrow = sb("modrow", [P, 6, F])
        prow = sb("prow", [40, P])
        parT = sb("parT", [P, 40])
        small = sb("small", [P, 400])
        flag = sb("flag", [1, 2], I32)
        KB = 256
        with nc.sbuf_tensor("sb_mixer_arena", [P, int(114.25 * KB)], F32) as mixer_arena:
            pass
        with (nc.sbuf_tensor("sb_mixer_below", [P, 48 * KB], F32),
              nc.sbuf_tensor("sb_mixer_split", [P, int(64.25 * KB)], F32R) as mixer_split):
            pass
        with (nc.sbuf_tensor("sb_cat_below", [P, 8 * KB], F32),
              nc.sbuf_tensor("sb_cat_split", [P, 28 * KB], F32R) as cat_split):
            pass
        moe_arena = sb("moe_arena", [P, int(60.75 * KB)])
        with nc.sbuf_tensor("sb_between", [P, 28 * KB], F32) as between:
            pass
        split = sb("split", [P, 53 * KB], F32R)
        psum = [stack.enter_context(nc.psum_tensor(f"bank{i}", [P, F], F32)) for i in range(8)]

        def area(kb, shape, of=None):
            n = int(np.prod(shape))
            a = (mixer_arena if of is None else of)[:, int(kb * KB):int(kb * KB) + n]
            if len(shape) == 2:
                return a.rearrange("p (a b) -> p a b", a=shape[0])
            if len(shape) == 3:
                return a.rearrange("p (a b c) -> p a b c", a=shape[0], b=shape[1])
            return a

        uT = area(0, [KC, 2 * T])
        lf = area(16, [8, 2 * T])
        kl = area(32, [8, T])
        kc = area(40, [8, T])
        X = area(48, [8, 2, T + 1])
        v = area(64.25, [2 * NT, F])
        qa = area(72.25, [H, T])
        gn = area(76.25, [NT, F])
        qb = area(80.25, [4, T])
        kbT = area(84.25, [4, 2 * T])
        vb = area(92.25, [2 * NT, F])
        S = area(100.25, [8, P])
        qt = area(104.25, [2, H, T])
        anorm = area(112.25, [F])
        junk = area(16, [D])
        masksf = area(24, [15, P])
        uT_hi = area(48 - 48, [KC, 2 * T], mixer_split)
        uT_lo_a, uT_lo_b = area(100.25 - 48, [4, 2 * T], mixer_split), area(84.25 - 48, [4, 2 * T], mixer_split)
        uT_lo = [None] * KC
        for n, k in enumerate(K_ORDER):
            uT_lo[k] = (uT_lo_a, uT_lo_b)[n // 4][:, n % 4, :]
        in_w = [(area(kb - 48, [F], mixer_split), area(kb - 46, [F], mixer_split)) for kb in (72.25, 80.25, 108.25)]
        xnl = area(84.25, [NT, D])
        cx = area(92.25, [NT, D])
        gain_row = area(92.25, [3, F])
        csil = small[:, 0:256].rearrange("p (k n) -> p k n", k=KC)
        modT = area(20, [16, 2])
        A1T = area(21, [KC, 2])
        kcdT = area(24, [NT, 8, P])
        kcd = area(24, [8, T])
        Z = [area(16, [8, T]), area(24, [8, T])]
        ATd = area(40, [NT, H, P])
        ATo = area(44, [2, H, P])
        cat = area(0, [NT, D])
        catT_hi = area(0, [KC, T], cat_split)
        catT_lo = [area(24, [4, T], cat_split), area(8, [4, T], cat_split)]
        prob = [area(16, [F]), area(18, [F])]
        probT = [area(20, [F]), area(22, [F])]
        bias = [area(24 + n, [T]) for n in range(N_BIAS)]
        ytmp = area(28, [2, F])
        M = moe_arena
        yacc = area(0, [NT, D], M)
        u2 = area(8, [NT, D], M)
        u2T = area(16, [KC, T], M)
        sg = area(24, [F], M)
        hh = area(26, [F], M)
        scl = area(28, [D], M)
        Pg = area(32, [NT, P], M)
        wr = area(33, [KC, 16], M)
        brt = area(33.5, [16], M)
        rs = area(33.5625, [3 * KB], M)
        MB = area(36.75, [6, D], M)
        w_hi = [area(8 * q, [PW], split) for q in range(PARTS)]
        w_lo = [area(8 * q + 4, [PW], split) for q in range(PARTS)]
        x_hi, x_lo = area(32, [KC, CAP], split), area(36, [KC, CAP], split)
        hT_hi, hT_lo = area(40, [4, CAP], split), area(42, [4, CAP], split)
        yg_hi, yg_lo = area(44, [D], split), area(48, [D], split)
        PT = area(52, [NT, P], split)
        bands = area(16, [NT, 4, T], M)
        pT = area(8, [8, T], between)
        mtmp = area(16, [2 * D], between)
        sq_out = area(24, [D], between)

        ss = small[:, 256:260]
        ms = small[:, 260:264]
        rstd = small[:, 264:268]
        ssq = small[:, 268:276]
        rstdo = small[:, 276:284]
        nmax = small[:, 284:286]
        den = small[:, 286:302]
        rden = small[:, 302:318]
        half = small[:, 318:319]
        junk2 = [area(20 + 0.5 * n, [P]) for n in range(NT)]
        silc = small[:, 320:336]
        lbs = small[:, 336:352]
        lbw = small[:, 352:400]
        ident = cst[:, C_ID:C_ID + P]

        s_cst, s_par, s_x, s_cx = sem("s_cst"), sem("s_par"), sem("s_x"), sem("s_cx")
        s_bm, s_an, s_gain, gain_done = sem("s_bm"), sem("s_an"), sem("s_gain"), sem("gain_done")
        s_masks, masks_ready, g_sig, ro_rstd = (
            sem("s_masks"), sem("masks_ready"), sem("g_sig"), sem("ro_rstd"))
        loaded = [sem(f"loaded{i}") for i in range(RING)]
        pool_chain = sem("pool_chain")
        par_ps, par_T, sig_c, csil_ready = sem("par_ps"), sem("par_T"), sem("sig_c"), sem("csil_ready")
        mod_used, mod_rows, modT_ps, A1_ready = sem("mod_used"), sem("mod_rows"), sem("modT_ps"), sem("A1_ready")
        sq_done, ms_ready, rstd_ready, xn_ready = sem("sq_done"), sem("ms_ready"), sem("rstd_ready"), sem("xn_ready")
        uT_ps, uT_full, uT_high = sem("uT_ps"), sem("uT_full"), sem("uT_high")
        in_hi, in_lo, in_part = sem("in_hi"), sem("in_lo"), sem("in_part")
        proj_done, proj_out, g_out = sem("proj_done"), sem("proj_out"), sem("g_out")
        f_ready, lf_ready, X_ready = sem("f_ready"), sem("lf_ready"), sem("X_ready")
        kcd_exp, kcd_ready, kcdT_ps, kcdT_ready = sem("kcd_exp"), sem("kcd_ready"), sem("kcdT_ps"), sem("kcdT_ready")
        S_ps, S_ready, qt_exp, qt_ready = sem("S_ps"), sem("S_ready"), sem("qt_exp"), sem("qt_ready")
        z_arg, z_exp, z_ready, gram, merged = sem("z_arg"), sem("z_exp"), sem("z_ready"), sem("gram"), sem("merged")
        atd_zero = sem("atd_zero")
        av_done, osq, ro_ready, a_ready = sem("av_done"), sem("osq"), sem("ro_ready"), sem("a_ready")
        b_dma, b_ready = [sem(f"b_dma{n}") for n in range(N_BIAS)], sem("b_ready")
        sc_ps, sc_max, p_exp = sem("sc_ps"), sem("sc_max"), sem("p_exp")
        pT_ps, pT_ready, pv_done = sem("pT_ps"), sem("pT_ready"), sem("pv_done")
        cat_ready, catT_ps, catT_high, catT_ready = sem("cat_ready"), sem("catT_ps"), sem("catT_high"), sem("catT_ready")
        y_done, out_hi, out_lo, out_part = sem("y_done"), sem("out_hi"), sem("out_lo"), sem("out_part")
        h1_ready = sem("h1_ready")
        bc_ps, bc_out = sem("bc_ps"), sem("bc_out")
        dve_chain, act_chain = sem("dve_chain"), sem("act_chain")
        s_rt, s_scl, s_out = sem("s_rt"), sem("s_scl"), sem("s_out")
        L = dict((n, sem(f"moe_{n}")) for n in (
            "u2", "u2T_ps", "u2T", "logits", "scores", "gates", "ranks", "routed",
            "h_ready", "yacc0"))
        pool_u, pool_ps, pool_T, pool_Ta, pool_y, pool_h, s_bands = (
            sem("pool_u"), sem("pool_ps"), sem("pool_T"), sem("pool_Ta"), sem("pool_y"), sem("pool_h"), sem("s_bands"))
        n_sq, n_ms, n_rstd, fin_out, gate_scaled = sem("n_sq"), sem("n_ms"), sem("n_rstd"), sem("fin_out"), sem("gate_scaled")
        NORM_MOE, NORM_POOL, NORM_LAST = (0, 2), 1, 3
        PASS = [dict((n, sem(f"pass{k}_{n}")) for n in (
            "hi", "lo", "part", "p_ready", "xg_ps", "xg_hi", "xg_lo", "route_ps", "gs", "silu", "hid", "hT_ps",
            "hT_hi", "hT_lo", "yg_hi", "yg_lo", "scat_ps", "scat")) for k in range(2)]
        TP = NM * PARTS
        PER_TILE = {"hi": TP, "lo": TP, "part": TP, "silu": NE, "hid": NE, "hT_ps": NE, "hT_hi": NE, "hT_lo": NE}
        BY = {"pe": ("xg_ps", "route_ps", "part", "hT_ps", "scat_ps"),
              "act": ("hi", "xg_hi", "silu", "hT_hi", "yg_hi"),
              "dve": ("lo", "p_ready", "xg_lo", "gs", "hid", "hT_lo", "yg_lo", "scat")}
        ov_loaded = [sem(f"ov_loaded{i}") for i in range(RING)]
        ov_chain = sem("ov_chain")

        def count_skipped(eng, name):
            for n in BY[name]:
                eng.sem_inc(PASS[1][n], NG * PER_TILE.get(n, 1))

        def chunks(w):
            return w.rearrange("(k p) n -> p k n", p=P)

        def slot(n):
            return ring[:, n % RING, :]

        def landed(n):
            return 16 * (n // RING + 1)

        def used_a(n):
            kind = RING_A[n][0]
            if kind == "mod":
                return mod_used, 4 * MPOS[RING_A[n][1]] + RING_A[n][2] + 1
            if kind == "in":
                p = RING_A[n][1]
                return (in_lo, KC * (SPLIT_PROJ.index(p) + 1)) if p in SPLIT_PROJ else (proj_done, U_END[p])
            return out_lo, PARTS * (RING_A[n][1] + 1)

        def part_used(n):
            i, kn = divmod(n, KC)
            return (in_part, (KC - 1) * i + kn + 1) if kn < KC - 1 else (proj_done, U_END[SPLIT_PROJ[i]])

        def chunk(i, kn):
            return K_ORDER[kn] if i == 0 else kn

        def unit_bank(u):
            return psum[SPLIT_BANKS[u % 7] if u < U_END[F_B] else PROJ_BANKS[u % 3]]

        def taken(u):
            if UNITS[u][0] == G_A:
                return g_out, UNITS[u][1] + 1
            return proj_out, sum(p != G_A for p, _ in UNITS[:u + 1])

        def used_moe(sems, t, j):
            t, j = t + j // NM, j % NM
            return sems["lo"], t * TP + PARTS * (j + 1)

        def consumed(sems, t, j):
            return sems["part"], t * TP + PARTS * (j + 1)

        def moe_src(l, t, j):
            kind, e = MOE_ORDER[j]
            w = {"g": w_gate, "u": w_up, "d": w_down}[kind]
            at = t * NE + e
            w = w[l, at] if isinstance(at, int) else w[l, bass.ds(at, 1)].rearrange("o a n -> (o a) n")
            return w.rearrange("(k p) n -> p k n", p=P)

        def slot_as(n, k):
            return slot(n).rearrange("p (k n) -> p k n", k=k)

        def linker(eng, s, base=0):
            count = [0]

            def link(ins):
                count[0] += 1
                ins.then_inc(s, 1)
                eng.wait_ge(s, base + count[0])
            link.count = count
            return link

        block = stack.enter_context(nc.Block())

        @block.sync
        def _(sp):
            sp.dma_start(h[:], x[0].rearrange("(t p) d -> p t d", p=P)).then_inc(s_x, 16)
            sp.dma_start(cx, ctx[0].rearrange("(t p) d -> p t d", p=P)).then_inc(s_cx, 16)
            sp.wait_ge(s_cst, 16)
            sp.wait_ge(s_par, 64)
            for n, item in enumerate(RING_A):
                if n >= RING:
                    sp.wait_ge(*used_a(n - RING))
                if item[0] == "mod":
                    _, b, s = item
                    src = w_mod[b // 3, 256 * s:256 * s + 256, 2048 * (b % 3):2048 * (b % 3) + 2048]
                elif item[0] == "in":
                    src = w_in[0][:, item[1] * F:(item[1] + 1) * F]
                else:
                    src = w_out[0][:, item[1] * F:(item[1] + 1) * F]
                src = src.rearrange("(k p) n -> p k n", p=P)
                sp.dma_start(slot_as(n, src.shape[1]), src).then_inc(loaded[n % RING], 16)

            def stream_moe(l, n0, before):
                sems, tb = PASS[0], l * NG

                def load(t, j):
                    n = n0 + j
                    src = moe_src(l, t, j)
                    sp.dma_start(slot_as(n, src.shape[1]), src).then_inc(loaded[n % RING], 16)

                for j in range(RING):
                    before(n0 + j - RING)
                    load(0, j)
                with sp.Fori(0, NG - 1) as t:
                    for j in range(RING, NM):
                        sp.wait_ge(*used_moe(sems, tb + t, j - RING))
                        load(t, j)
                    for j in range(RING):
                        sp.wait_ge(*used_moe(sems, tb + t, NM + j - RING))
                        load(t + 1, j)
                for j in range(RING, NM):
                    sp.wait_ge(*used_moe(sems, tb + NG - 1, j - RING))
                    load(NG - 1, j)

            def overflow_moe(l):
                sp.wait_ge(L["routed"], l + 1)
                go = sp.value_load(flag[0:1, l:l + 1])
                sems, tb = PASS[1], l * NG
                with sp.If(go > 0):
                    sp.wait_ge(PASS[0]["lo"], (tb + NG) * TP)
                    for j in range(RING):
                        src = moe_src(l, 0, j)
                        sp.dma_start(slot_as(j, src.shape[1]), src).then_inc(ov_loaded[j], 16)
                    with sp.Fori(0, NG - 1) as t:
                        for j in range(RING, NM + RING):
                            sp.wait_ge(*used_moe(sems, tb + t, j - RING))
                            src = moe_src(l, t if j < NM else t + 1, j % NM)
                            sp.dma_start(slot_as(j, src.shape[1]), src).then_inc(ov_loaded[j % RING], 16)
                    for j in range(RING, NM):
                        sp.wait_ge(*used_moe(sems, tb + NG - 1, j - RING))
                        src = moe_src(l, NG - 1, j)
                        sp.dma_start(slot_as(j, src.shape[1]), src).then_inc(ov_loaded[j % RING], 16)
                    sp.wait_ge(sems["lo"], (tb + NG) * TP)
                with sp.Else():
                    for i in range(RING):
                        sp.sem_inc(ov_loaded[i], 16 * NG * NM // RING)

            stream_moe(0, N_MOE0, lambda n: sp.wait_ge(*used_a(n)))
            overflow_moe(0)

            def before_pool(n):
                sp.wait_ge(*used_moe(PASS[0], NG - 1, n - N_MOE0 - (NG - 1) * NM))
            before_pool(N_POOL - RING)
            sp.dma_start(slot(N_POOL)[:, 0:8 * T].rearrange("p (g n) -> p g n", g=8),
                         w_pool[0].rearrange("g (c p) n -> p (g c) n", p=P)).then_inc(loaded[N_POOL % RING], 16)

            def before_moe1(n):
                if n == N_POOL:
                    sp.wait_ge(pool_y, 4)
                else:
                    before_pool(n)
            stream_moe(1, N_MOE1, before_moe1)
            overflow_moe(1)
            for tt in range(NT):
                sp.wait_ge(fin_out, tt + 1)
                sp.dma_start(out[0, tt * P:(tt + 1) * P, :], mtmp[:, tt * D:(tt + 1) * D]).then_inc(s_out, 16)
            sp.wait_ge(s_out, 16 * NT)

        @block.tensor
        def _(pe):
            mm = nc.tensor.matmul
            tr = nc.tensor.transpose
            pe.wait_ge(s_cst, 16)
            pe.wait_ge(s_par, 64)
            tr(psum[0][:, 0:40], prow[:], cst[0:40, C_ID:C_ID + 40]).then_inc(par_ps, 1)

            def mod_quarter(b, s):
                if s == 0 and MPOS[b]:
                    pe.wait_ge(mod_rows, MPOS[b])
                n = SLOT_A[("mod", b, s)]
                pe.wait_ge(loaded[n % RING], landed(n))
                w = slot(n).rearrange("p (k j n) -> p k j n", k=2, j=4)
                for kk in range(2):
                    k = 2 * s + kk
                    for j in range(4):
                        last = mm(psum[MOD_BANK][32 * j:32 * j + 32, :], csil[:, k, :], w[:, kk, j, :],
                                  start=k == 0, stop=k == KC - 1, tile_position=(0, 32 * j),
                                  skip_group_check=True)
                last.then_inc(mod_used, 1)

            def input_T(n):
                k = K_ORDER[n]
                for tt in range(4):
                    src = xnl if tt < NT else cx
                    last = tr(psum[k][:, tt * P:(tt + 1) * P], src[:, tt % NT, k * P:(k + 1) * P], ident)
                last.then_inc(uT_ps, 1)

            pe.wait_ge(csil_ready, 1)
            for s in range(4):
                if s == 3:
                    pe.wait_ge(xn_ready, 4)
                    for n in range(K_FIRST):
                        input_T(n)
                mod_quarter(MODS[0], s)
            pe.wait_ge(mod_rows, 1)
            for cc in range(4):
                for j in range(4):
                    last = mm(psum[2 + j][:, 2 * cc:2 * cc + 2], modrow[32 * j:32 * j + 32, 0, cc * P:(cc + 1) * P],
                              cst[32 * j:32 * j + 32, C_E2:C_E2 + 2], start=True, stop=True,
                              tile_position=(32 * j, 0))
            last.then_inc(modT_ps, 1)
            pe.wait_ge(A1_ready, 1)
            for n in range(K_FIRST, KC):
                input_T(n)

            def bank_free(u):
                b = unit_bank(u)
                before = [x for x in range(u) if unit_bank(x) is b]
                if before:
                    pe.wait_ge(*taken(before[-1]))

            def split_projection(i):
                p = SPLIT_PROJ[i]
                us = [u for u in range(len(UNITS)) if UNITS[u][0] == p]
                for kn in range(KC):
                    k = chunk(i, kn)
                    pe.wait_ge(in_lo, KC * i + kn + 1)
                    w_h, w_l = in_w[(KC * i + kn) % W_BUFS]
                    for u in us:
                        m = UNITS[u][1]
                        if kn == 0:
                            if i == 0:
                                pe.wait_ge(uT_full, m + 1)
                            else:
                                bank_free(u)
                        cols = slice(m * P, (m + 1) * P)
                        if p in (I_A, G_A):
                            x_h, x_l, y_h, y_l = uT_hi[:, k, cols], uT_lo[k][:, cols], w_h, w_l
                        else:
                            x_h, x_l, y_h, y_l = w_h[:, cols], w_l[:, cols], uT_hi[:, k, :], uT_lo[k]
                        bank = unit_bank(u)[:]
                        mm(bank, x_h, y_h, start=kn == 0, stop=False)
                        mm(bank, x_h, y_l, start=False, stop=False)
                        last = mm(bank, x_l, y_h, start=False, stop=kn == KC - 1)
                        if kn == KC - 1:
                            last.then_inc(proj_done, 1)
                    if kn < KC - 1:
                        last.then_inc(in_part, 1)
                    if kn in Q_AFTER[i]:
                        if i == 0:
                            pe.wait_ge(uT_full, KC)
                        mod_quarter(*split_quarter(i, Q_AFTER[i].index(kn))[1:])

            for i in range(len(SPLIT_PROJ)):
                split_projection(i)

            def proj_unit(u):
                p, m = UNITS[u]
                n = SLOT_A[("in", p)]
                bank = unit_bank(u)
                if m == 0:
                    pe.wait_ge(loaded[n % RING], landed(n))
                bank_free(u)
                w = slot_as(n, KC)
                for k in range(KC):
                    if p in (I_A, G_A, V_B):
                        last = mm(bank[:], uT[:, k, m * P:(m + 1) * P], w[:, k, :], start=k == 0, stop=k == KC - 1)
                    else:
                        cols = T if p in (Q_A, Q_B) else 2 * T
                        last = mm(bank[:, 0:cols], w[:, k, m * P:(m + 1) * P], uT[:, k, 0:cols],
                                  start=k == 0, stop=k == KC - 1)
                last.then_inc(proj_done, 1)

            def planned(stage):
                for what in PLAN[stage]:
                    if isinstance(what, int):
                        proj_unit(what)
                    else:
                        mod_quarter(*what[1:])

            planned(0)

            pe.wait_ge(kcd_ready, 1)
            for st in range(NT):
                for i in range(8):
                    last = tr(psum[2 * st + i // 4][:, (i % 4) * P:(i % 4 + 1) * P], kc[:, i, st * P:(st + 1) * P], ident)
            last.then_inc(kcdT_ps, 1)
            planned(1)
            pe.wait_ge(kcdT_ready, 1)
            for i in range(8):
                for st in range(NT):
                    last = mm(psum[i // 4][:, (i % 4) * P:(i % 4 + 1) * P], kcdT[:, st, i, :],
                              v[:, NT + st, (i % H) * P:(i % H + 1) * P], start=st == 0, stop=st == NT - 1)
            last.then_inc(S_ps, 1)
            planned(2)

            for lev in range(NLEV):
                if lev < len(LEVELS):
                    pe.wait_ge(z_ready, lev + 1)
                if lev:
                    pe.wait_ge(merged, lev)
                if lev == 1:
                    pe.wait_ge(S_ready, 1)
                z = Z[lev % 2]
                if lev == 0:
                    for d in range(2):
                        for hd in range(H):
                            i = d * H + hd
                            last = mm(psum[2 + d][:, hd * P:(hd + 1) * P], z[:, i, d * P:(d + 1) * P],
                                      z[:, i, (1 - d) * P:(2 - d) * P], start=True, stop=True)
                elif lev < len(LEVELS):
                    for d in range(2):
                        for tt in range(NT):
                            for hd in range(H):
                                zz = z[:, d * H + hd, tt * P:(tt + 1) * P]
                                last = mm(psum[2 * d + tt][:, hd * P:(hd + 1) * P], zz, zz, start=True, stop=True)
                else:
                    for tt in range(NT):
                        for hd in range(H):
                            for d in range(2):
                                last = mm(psum[tt][:, hd * P:(hd + 1) * P], kl[:, d * H + hd, tt * P:(tt + 1) * P],
                                          qa[:, hd, tt * P:(tt + 1) * P], start=d == 0, stop=d == 1)
                last.then_inc(gram, 1)
                planned(3 + lev)

            pe.wait_ge(merged, NLEV)
            pe.wait_ge(qt_ready, 1)
            for tt in range(NT):
                for hd in range(H):
                    o = psum[tt][:, hd * P:(hd + 1) * P]
                    mm(o, ATd[:, tt, hd, :], v[:, tt, hd * P:(hd + 1) * P], start=True, stop=False)
                    mm(o, ATo[:, 1 - tt, hd, :], v[:, 1 - tt, hd * P:(hd + 1) * P], start=False, stop=False)
                    mm(o, qt[:, 0, hd, tt * P:(tt + 1) * P], S[:, hd, :], start=False, stop=False)
                    last = mm(o, qt[:, 1, hd, tt * P:(tt + 1) * P], S[:, H + hd, :], start=False, stop=True)
                last.then_inc(av_done, 1)

            def attn_scores(i):
                hd, qi = i // NT, i % NT
                r = DH * (hd % 2)
                mm(psum[2 + i % 2][:], qb[r:r + DH, hd // 2, qi * P:(qi + 1) * P], kbT[r:r + DH, hd // 2, :],
                   start=True, stop=False)
                pe.wait_ge(b_ready, i + 1)
                mm(psum[2 + i % 2][:, 0:T], cst[:, C_REV:C_REV + P], bias[i % N_BIAS], start=False,
                   stop=True).then_inc(sc_ps, 1)

            def attn_values(i):
                hd, qi = i // NT, i % NT
                pe.wait_ge(pT_ready, i + 1)
                for cc in range(4):
                    last = mm(psum[6 + qi][:, hd * DH:(hd + 1) * DH], probT[i % 2][:, cc * P:(cc + 1) * P],
                              vb[:, cc, hd * DH:(hd + 1) * DH], start=cc == 0, stop=cc == 3)
                last.then_inc(pv_done, 1)

            def cat_T(ks, bank):
                for k in ks:
                    for tt in range(NT):
                        last = tr(psum[bank + k % 4 // 2][:, (k % 2) * T + tt * P:(k % 2) * T + (tt + 1) * P],
                                  cat[:, tt, k * P:(k + 1) * P], ident)
                last.then_inc(catT_ps, 1)

            def spread(n):
                p, banks = SPREAD[n]
                l = p // 6
                before = [m for m in range(n) if set(SPREAD[m][1]) & set(banks)]
                if before:
                    pe.wait_ge(bc_out, before[-1] + 1)
                for half_ in range(2):
                    j = 2 * (p % 2) + half_
                    last = mm(psum[banks[half_]][:], cst[32 * j:32 * j + 32, C_SEL:C_SEL + P],
                              modrow[32 * j:32 * j + 32, 3 * l + p % 6 // 2, :], start=True, stop=True,
                              tile_position=(32 * j, 0))
                last.then_inc(bc_ps, 1)

            pe.wait_ge(*taken(len(UNITS) - 1))
            pe.wait_ge(mod_rows, 5)
            pe.wait_ge(gain_done, 3)
            attn_scores(0)
            attn_scores(1)
            for i in range(BH * NT):
                pe.wait_ge(p_exp, i + 1)
                for cc in range(4):
                    last = tr(psum[4 + i % 2][:, cc * P:(cc + 1) * P], prob[i % 2][:, cc * P:(cc + 1) * P], ident)
                last.then_inc(pT_ps, 1)
                if i + 2 < BH * NT:
                    attn_scores(i + 2)
                if i:
                    attn_values(i - 1)
                if i == CAT_AT:
                    pe.wait_ge(a_ready, NT)
                    cat_T(range(KC // 2), 0)
                if i == S_AT[0]:
                    pe.wait_ge(catT_ready, 1)
                if i in S_AT:
                    spread(S_AT.index(i))
            attn_values(BH * NT - 1)

            def project_out(n):
                nh, q = divmod(n, PARTS)
                pe.wait_ge(out_lo, n + 1)
                for kk in range(2):
                    k = 2 * q + kk
                    hi, lo = w_hi[q][:, kk * F:(kk + 1) * F], w_lo[q][:, kk * F:(kk + 1) * F]
                    for tt in range(NT):
                        bank, cols = psum[4 + 2 * nh + tt][:], slice(tt * P, (tt + 1) * P)
                        mm(bank, catT_hi[:, k, cols], hi, start=k == 0, stop=False)
                        mm(bank, catT_hi[:, k, cols], lo, start=False, stop=False)
                        last = mm(bank, catT_lo[k // 4][:, k % 4, cols], hi, start=False, stop=k == KC - 1)
                        if k == KC - 1:
                            last.then_inc(y_done, 1)
                if q < PARTS - 1:
                    last.then_inc(out_part, 1)

            project_out(0)
            project_out(1)
            pe.wait_ge(cat_ready, 1)
            cat_T(range(KC // 2, KC), 2)
            pe.wait_ge(catT_ready, 2)
            for n in range(2, 2 * PARTS):
                project_out(n)
            pe.wait_ge(h1_ready, 4)
            planned(len(PLAN) - 1)

            def keep_clock(bank, n):
                for _ in range(n):
                    mm(psum[bank][:], ident, cst[:, 0:F], start=True, stop=True)

            def route(l):
                s = L
                for tt in range(NT):
                    pe.wait_ge(s["u2"], NT * l + tt + 1)
                    for k in range(KC):
                        last = tr(psum[2 * tt + k // 4][:, (k % 4) * P:(k % 4 + 1) * P], u2[:, tt, k * P:(k + 1) * P], ident)
                    last.then_inc(s["u2T_ps"], 1)
                if l == 0:
                    pe.wait_ge(mod_rows, 6)
                    spread(len(S_AT))
                pe.wait_ge(s_rt, 32)
                for tt in range(NT):
                    pe.wait_ge(s["u2T"], NT * l + tt + 1)
                    for k in range(KC):
                        last = mm(psum[4][:, tt * 16:(tt + 1) * 16], u2T[:, k, tt * P:(tt + 1) * P], wr[:, k, :],
                                  start=k == 0, stop=k == KC - 1)
                last.then_inc(s["logits"], 1)
                if l == 0:
                    spread(len(S_AT) + 1)
                    spread(len(S_AT) + 2)
                    pe.wait_ge(bc_out, len(S_AT) + 1)
                else:
                    keep_clock(7, 4)
                pe.wait_ge(s["gates"], l + 1)
                G = rs[:, 0:8]
                mm(psum[5][:, 0:4], cst[:, C_TRI:C_TRI + P], G[:, 0:4], start=True, stop=True)
                mm(psum[5][:, 4:8], cst[:, C_ONES:C_ONES + P], G[:, 0:4], start=True, stop=False)
                mm(psum[5][:, 4:8], cst[:, C_TRI:C_TRI + P], G[:, 4:8], start=False, stop=True)
                mm(psum[5][:, 8:12], cst[:, C_ONES:C_ONES + P], G[:, 0:4], start=True, stop=False)
                mm(psum[5][:, 8:12], cst[:, C_ONES:C_ONES + P], G[:, 4:8], start=False, stop=True).then_inc(s["ranks"], 1)

            def experts(sems, tb, gates_c):
                def gather(t):
                    pe.wait_ge(sems["p_ready"], t + 1)
                    for k in range(KC):
                        for tt in range(NT):
                            last = mm(psum[2 + k // 4][:, (k % 4) * P:(k % 4) * P + CAP], u2[:, tt, k * P:(k + 1) * P],
                                      Pg[:, tt, 0:CAP], start=tt == 0, stop=tt == NT - 1)
                    last.then_inc(sems["xg_ps"], 1)

                def slots_of(t):
                    pe.wait_ge(sems["scat"], t + 1)
                    for tt in range(NT):
                        tr(psum[7][0:CAP, P + tt * P:P + (tt + 1) * P], Pg[:, tt, 0:CAP], ident)
                    for tt in range(NT):
                        last = mm(psum[7][0:CAP, 0:4], Pg[:, tt, 0:CAP], gates_c[:, tt * 4:tt * 4 + 4],
                                  start=tt == 0, stop=tt == NT - 1)
                    last.then_inc(sems["route_ps"], 1)

                def up_or_gate(t, kind, e):
                    bank = psum[2 * (e % 2) + (kind == "u")][0:CAP, :]
                    for q in range(PARTS):
                        pe.wait_ge(sems["lo"], t * TP + (PARTS * ITEM[kind, e] + q + 1))
                        for kk in range(2):
                            k = 2 * q + kk
                            hi, lo = w_hi[q][:, kk * F:(kk + 1) * F], w_lo[q][:, kk * F:(kk + 1) * F]
                            mm(bank, x_hi[:, k, :], hi, start=k == 0, stop=False)
                            mm(bank, x_hi[:, k, :], lo, start=False, stop=False)
                            last = mm(bank, x_lo[:, k, :], hi, start=False, stop=k == KC - 1)
                        last.then_inc(sems["part"], 1)

                def hidden_T(t, e):
                    pe.wait_ge(sems["hid"], t * NE + (e + 1))
                    for cc in range(4):
                        last = tr(psum[4][:, cc * P:cc * P + CAP], hh[0:CAP, cc * P:(cc + 1) * P],
                                  cst[0:CAP, C_ID:C_ID + CAP])
                    last.then_inc(sems["hT_ps"], 1)

                def down(t, e):
                    pe.wait_ge(sems["hT_lo"], t * NE + (e + 1))
                    for q in range(PARTS):
                        pe.wait_ge(sems["lo"], t * TP + (PARTS * ITEM["d", e] + q + 1))
                        first, end = e == 0 and q == 0, e == NE - 1 and q == PARTS - 1
                        for nh in range(2):
                            bank = psum[5 + nh][0:CAP, :]
                            hi, lo = w_hi[q][:, nh * F:(nh + 1) * F], w_lo[q][:, nh * F:(nh + 1) * F]
                            mm(bank, hT_hi[:, q, :], hi, start=first, stop=False)
                            mm(bank, hT_hi[:, q, :], lo, start=False, stop=False)
                            last = mm(bank, hT_lo[:, q, :], hi, start=False, stop=end)
                        last.then_inc(sems["part"], 1)

                def scatter(t):
                    pe.wait_ge(sems["gs"], t + 1)
                    pe.wait_ge(sems["yg_lo"], t + 1)
                    for n, b in enumerate(SCAT_BANKS):
                        tt, nh = n // 2, n % 2
                        mm(psum[b][:], PT[0:CAP, tt, :], yg_hi[0:CAP, nh * F:(nh + 1) * F], start=True, stop=False)
                        last = mm(psum[b][:], PT[0:CAP, tt, :], yg_lo[0:CAP, nh * F:(nh + 1) * F], start=False, stop=True)
                    last.then_inc(sems["scat_ps"], 1)

                def start(t):
                    gather(t)
                    pe.wait_ge(sems["xg_lo"], t + 1)
                    up_or_gate(t, "g", 0)
                    up_or_gate(t, "u", 0)

                def tile(t, more):
                    slots_of(t)
                    for e in range(1, NE):
                        up_or_gate(t, "g", e)
                        hidden_T(t, e - 1)
                        up_or_gate(t, "u", e)
                        down(t, e - 1)
                    hidden_T(t, NE - 1)
                    if more:
                        gather(t + 1)
                    down(t, NE - 1)
                    if more:
                        pe.wait_ge(sems["xg_lo"], t + 2)
                        up_or_gate(t + 1, "g", 0)
                    scatter(t)
                    if more:
                        up_or_gate(t + 1, "u", 0)

                start(tb)
                with pe.Fori(0, NG - 1) as i:
                    tile(i + tb, True)
                tile(tb + NG - 1, False)

            def moe(l):
                route(l)
                pe.wait_ge(bc_out, len(SPREAD) - 1 + l)
                experts(PASS[0], l * NG, rs[:, 8:16])
                pe.wait_ge(L["routed"], l + 1)
                go = pe.value_load(flag[0:1, l:l + 1])
                with pe.If(go > 0):
                    pe.wait_ge(PASS[0]["scat"], (l + 1) * NG + 1)
                    experts(PASS[1], l * NG, rs[:, 8:16])
                    pe.wait_ge(PASS[1]["scat"], (l + 1) * NG + 1)
                with pe.Else():
                    count_skipped(pe, "pe")

            moe(0)

            pe.wait_ge(PASS[1]["scat"], NG + 1)
            keep_clock(7, 8)
            pe.wait_ge(pool_u, NT)
            pe.wait_ge(s_bands, 16)
            for g in range(4):
                for cc in range(2):
                    k = 2 * g + cc
                    for st in range(NT):
                        last = mm(psum[g][:, cc * T:(cc + 1) * T], u2[:, st, k * P:(k + 1) * P], bands[:, st, g, :],
                                  start=st == 0, stop=st == NT - 1)
                last.then_inc(pool_ps, 1)
            pe.wait_ge(L["h_ready"], NT)
            spread(len(SPREAD) - 1)
            pe.wait_ge(pool_T, 1)
            pe.wait_ge(pool_Ta, 1)
            pe.wait_ge(bc_out, len(SPREAD))
            pe.wait_ge(loaded[N_POOL % RING], landed(N_POOL))
            w = slot(N_POOL)[:, 0:8 * T].rearrange("p (g n) -> p g n", g=8)
            for tt in range(NT):
                for gh in range(2):
                    for g in (2 * gh, 2 * gh + 1):
                        for cc in range(2):
                            last = mm(psum[4 + 2 * tt + gh][:, (g % 2) * T:(g % 2 + 1) * T],
                                      pT[:, 2 * g + cc, tt * P:(tt + 1) * P], w[:, 2 * g + cc, :],
                                      start=cc == 0, stop=cc == 1)
                    last.then_inc(pool_y, 1)
            keep_clock(0, 5)
            moe(1)

        @block.scalar
        def _(act):
            link = linker(act, act_chain)
            A = nc.scalar.activation
            act.dma_start(cst[:], cst_d).then_inc(s_cst, 16)
            act.dma_start(prow[0:8, :], c.rearrange("b (k p) -> (b k) p", p=P)).then_inc(s_par, 16)
            act.dma_start(prow[8:16, :], c_ctx.rearrange("(k p) -> k p", p=P)).then_inc(s_par, 16)
            act.dma_start(prow[16:24, :], norm1_g[0].rearrange("(k p) -> k p", p=P)).then_inc(s_par, 16)
            act.dma_start(prow[24:40, :], lb_logits.rearrange("l d (h p) -> (l d h) p", p=P)).then_inc(s_par, 16)
            act.wait_ge(par_T, 1)
            A(silc, parT[:, 0:16], ACT.Sigmoid).then_inc(sig_c, 1)
            act.wait_ge(par_T, 2)
            A(lbw[:, 0:16], lbw[:, 0:16], ACT.Exp).then_inc(sig_c, 1)
            act.wait_ge(s_x, 16)
            act.wait_ge(s_cx, 16)
            for tt in range(4):
                link(A(junk, h[:, tt] if tt < NT else cx[:, tt - NT], ACT.Square, accum_out=ss[:, tt:tt + 1]))
            A(half, cst[:, C_ONES:C_ONES + 1], ACT.Copy, scale=-0.5).then_inc(sq_done, 1)
            act.wait_ge(A1_ready, 1)
            def take(u):
                p, m = UNITS[u]
                bank = unit_bank(u)
                act.wait_ge(proj_done, u + 1)
                if p == I_A:
                    ins = A(v[:, m, :], bank[:], ACT.Copy)
                elif p in (F_F, F_B):
                    ins = A(lf[:, (p - F_F) * H + m, :], bank[:], ACT.Sigmoid)
                elif p == Q_A:
                    ins = A(qa[:, m, :], bank[:, 0:T], ACT.Copy, scale=float(np.float32(DK ** -0.5)))
                elif p == G_A:
                    A(gn[:, m, :], bank[:], ACT.Sigmoid).then_inc(g_sig, 1)
                    return
                elif p == K_B:
                    ins = A(kbT[:, m, :], bank[:], ACT.Copy)
                elif p == Q_B:
                    ins = A(qb[:, m, :], bank[:, 0:T], ACT.Copy, scale=DH ** -0.5)
                else:
                    ins = A(vb[:, m, :], bank[:], ACT.Copy)
                ins.then_inc(proj_out, 1)

            def input_high(n):
                k = K_ORDER[n]
                act.wait_ge(uT_full, n + 1)
                A(uT_hi[:, k, :], uT[:, k, :], ACT.Copy).then_inc(uT_high, 1)

            def weights_high(i, kn):
                n, at = KC * i + kn, SLOT_A[("in", SPLIT_PROJ[i])]
                if kn == 0:
                    act.wait_ge(loaded[at % RING], landed(at))
                if n >= W_BUFS:
                    act.wait_ge(*part_used(n - W_BUFS))
                A(in_w[n % W_BUFS][0], slot_as(at, KC)[:, chunk(i, kn), :], ACT.Copy).then_inc(in_hi, 1)

            for kn in range(KC):
                input_high(kn)
                weights_high(0, kn)
            for i in range(1, len(SPLIT_PROJ) + 1):
                for kn in range(KC if i < len(SPLIT_PROJ) else 3):
                    if kn == 3 or i == len(SPLIT_PROJ):
                        if kn in (0, 3):
                            if SPLIT_PROJ[i - 1] == F_F:
                                act.wait_ge(masks_ready, 1)
                            for u, unit in enumerate(UNITS):
                                if unit[0] == SPLIT_PROJ[i - 1]:
                                    take(u)
                    if i < len(SPLIT_PROJ):
                        weights_high(i, kn)
            for d in range(2):
                act.wait_ge(f_ready, d + 1)
                A(lf[:, d * H:(d + 1) * H, :], lf[:, d * H:(d + 1) * H, :], ACT.Ln).then_inc(lf_ready, 1)
            for u in range(U_END[F_B], U_EARLY - 2):
                take(u)
            act.wait_ge(X_ready, 2)
            for hd in range(H):
                A(kcd[:, hd, :], X[:, hd, 1, 1:T + 1], ACT.Exp, bias=X[:, hd, 1, T:T + 1], scale=-1.0)
            A(kcd[:, H:2 * H, :], X[:, H:2 * H, 1, 0:T], ACT.Exp).then_inc(kcd_exp, 1)
            def exp_level(lev):
                act.wait_ge(z_arg, lev + 1)
                A(Z[lev % 2], Z[lev % 2], ACT.Exp).then_inc(z_exp, 1)

            for u in range(U_EARLY - 2, U_EARLY):
                take(u)
            exp_level(0)
            A(qt[:, 0], X[:, 0:H, 0, 1:T + 1], ACT.Exp)
            for hd in range(H):
                last = A(qt[:, 1, hd, :], X[:, H + hd, 0, 0:T], ACT.Exp, bias=X[:, H + hd, 0, T:T + 1], scale=-1.0)
            last.then_inc(qt_exp, 1)
            def take_stage(stage):
                for what in PLAN[stage]:
                    if isinstance(what, int):
                        take(what)

            take_stage(1)
            take_stage(2)
            for lev in range(NLEV):
                if 0 < lev < len(LEVELS):
                    exp_level(lev)
                if lev:
                    take_stage(2 + lev)
            take_stage(2 + NLEV)
            for tt in range(NT):
                act.wait_ge(av_done, tt + 1)
                for hd in range(H):
                    ins = A(junk2[tt], psum[tt][:, hd * P:(hd + 1) * P], ACT.Square,
                            accum_out=ssq[:, tt * H + hd:tt * H + hd + 1])
                    if hd < H - 1:
                        link(ins)
                ins.then_inc(osq, 1)
            def cat_taken(n):
                act.wait_ge(catT_ps, n + 1)
                for b in range(2):
                    last = A(catT_hi[:, 4 * n + 2 * b:4 * n + 2 * b + 2, :],
                             psum[2 * n + b][:].rearrange("p (k t) -> p k t", k=2), ACT.Copy)
                last.then_inc(catT_high, 1)

            def out_high(n):
                nh, q = divmod(n, PARTS)
                at = SLOT_A[("out", nh)]
                if q == 0:
                    act.wait_ge(loaded[at % RING], landed(at))
                if nh:
                    act.wait_ge(*((out_part, q + 1) if q < PARTS - 1 else (y_done, NT)))
                A(w_hi[q], slot(at)[:, q * PW:(q + 1) * PW], ACT.Copy).then_inc(out_hi, 1)

            def spread_out(n):
                p, banks = SPREAD[n]
                act.wait_ge(bc_ps, n + 1)
                for half_ in range(2):
                    last = A(MB[:, p % 6, half_ * F:(half_ + 1) * F], psum[banks[half_]][:], ACT.Copy)
                last.then_inc(bc_out, 1)

            def probabilities(i):
                act.wait_ge(sc_max, i + 1)
                A(prob[i % 2], psum[2 + i % 2][:], ACT.Exp, bias=nmax[:, i % 2:i % 2 + 1],
                  accum_out=den[:, i:i + 1]).then_inc(p_exp, 1)

            probabilities(0)
            for i in range(BH * NT):
                if i + 1 < BH * NT:
                    probabilities(i + 1)
                act.wait_ge(pT_ps, i + 1)
                A(probT[i % 2], psum[4 + i % 2][:], ACT.Copy).then_inc(pT_ready, 1)
                if i == CAT_AT:
                    cat_taken(0)
                if i in S_AT:
                    spread_out(S_AT.index(i))
                if i == OUT_AT:
                    act.wait_ge(a_ready, NT)
                if i in (OUT_AT, OUT_AT + 1):
                    out_high(i - OUT_AT)
            act.wait_ge(pv_done, BH * NT)
            out_high(2)
            out_high(3)
            cat_taken(1)
            for n in range(PARTS, 2 * PARTS):
                out_high(n)

            def stats(norm, *ready):
                for tt in range(NT):
                    act.wait_ge(*ready[tt])
                    A(sq_out, h[:, tt], ACT.Square, accum_out=ss[:, tt:tt + 1]).then_inc(n_sq, 1)
                    act.wait_ge(n_sq, NT * norm + tt + 1)

            def load_table(func):
                link(A(den[:, 0:1], half, func))

            def route(l):
                s = L
                for tt in range(NT):
                    act.wait_ge(s["u2T_ps"], NT * l + tt + 1)
                    for n in range(2):
                        last = A(u2T[:, 4 * n:4 * n + 4, tt * P:(tt + 1) * P],
                                 psum[2 * tt + n][:].rearrange("p (k t) -> p k t", k=4), ACT.Copy)
                    last.then_inc(s["u2T"], 1)
                if l == 0:
                    spread_out(len(S_AT))
                act.wait_ge(s["logits"], l + 1)
                A(rs[:, 16:48], psum[4][:, 0:32], ACT.Sigmoid).then_inc(s["scores"], 1)
                load_table(ACT.Silu)

            def high(sems, t, j, n, loads, base):
                act.wait_ge(loads[n % RING], base)
                for q in range(PARTS):
                    before = t * TP + (PARTS * j + q + 1 - PARTS)
                    if not isinstance(t, int) or before > 0:
                        act.wait_ge(sems["part"], before)
                    A(w_hi[q], slot(n)[:, q * PW:(q + 1) * PW], ACT.Copy).then_inc(sems["hi"], 1)

            def experts(sems, tb, n0, loads, land0, started):
                def weights(t, tile_, kind, e):
                    n = n0 + ITEM[kind, e]
                    high(sems, t, ITEM[kind, e], n, loads, tile_ * (16 * NM // RING) + (land0 + landed(n)))

                def gathered(t):
                    act.wait_ge(sems["xg_ps"], t + 1)
                    for n in range(2):
                        last = A(x_hi[:, 4 * n:4 * n + 4, :],
                                 psum[2 + n][:].rearrange("p (k n) -> p k n", k=4)[:, :, 0:CAP], ACT.Copy)
                    last.then_inc(sems["xg_hi"], 1)

                def silu(t, e):
                    act.wait_ge(*consumed(sems, t, ITEM["g", e]))
                    A(sg[0:CAP], psum[2 * (e % 2)][0:CAP, :], ACT.Silu).then_inc(sems["silu"], 1)

                def hidden(t, e):
                    act.wait_ge(sems["hT_ps"], t * NE + (e + 1))
                    A(hT_hi, psum[4][:].rearrange("p (c n) -> p c n", c=4)[:, :, 0:CAP],
                      ACT.Copy).then_inc(sems["hT_hi"], 1)

                def tile(t, i, more):
                    for e in range(1, NE):
                        weights(t, i, "g", e)
                        weights(t, i, "u", e)
                        hidden(t, e - 1)
                        silu(t, e)
                        weights(t, i, "d", e - 1)
                    weights(t, i, "d", NE - 1)
                    hidden(t, NE - 1)
                    if more:
                        gathered(t + 1)
                        weights(t + 1, i + 1, "g", 0)
                    act.wait_ge(*consumed(sems, t, ITEM["d", NE - 1]))
                    for nh in range(2):
                        last = A(yg_hi[0:CAP, nh * F:(nh + 1) * F], psum[5 + nh][0:CAP, :], ACT.Copy)
                    last.then_inc(sems["yg_hi"], 1)
                    if more:
                        weights(t + 1, i + 1, "u", 0)
                        silu(t + 1, 0)

                if not started:
                    weights(tb, 0, "g", 0)
                gathered(tb)
                weights(tb, 0, "u", 0)
                silu(tb, 0)
                with act.Fori(0, NG - 1) as i:
                    tile(i + tb, i, True)
                tile(tb + NG - 1, NG - 1, False)

            def moe(l):
                n0 = (N_MOE0, N_MOE1)[l]
                load_table(ACT.Sigmoid)
                if l:
                    high(PASS[0], l * NG, 0, n0, loaded, landed(n0))
                route(l)
                if l == 0:
                    for n in (1, 2):
                        spread_out(len(S_AT) + n)
                    high(PASS[0], l * NG, 0, n0, loaded, landed(n0))
                experts(PASS[0], l * NG, n0, loaded, 0, True)
                act.wait_ge(L["routed"], l + 1)
                go = act.value_load(flag[0:1, l:l + 1])
                with act.If(go > 0):
                    act.wait_ge(PASS[0]["scat"], (l + 1) * NG + 1)
                    experts(PASS[1], l * NG, 0, ov_loaded, l * 16 * NG * NM // RING, False)
                    act.wait_ge(PASS[1]["scat"], (l + 1) * NG + 1)
                with act.Else():
                    count_skipped(act, "act")

            act.wait_ge(y_done, 2 * NT)
            stats(NORM_MOE[0], (h1_ready, 3), (h1_ready, 4))
            moe(0)
            stats(NORM_POOL, (L["h_ready"], 1), (L["h_ready"], 2))
            act.wait_ge(pool_ps, 2)
            for g in range(2):
                last = A(pT[:, 2 * g:2 * g + 2, :], psum[g][:].rearrange("p (a b) -> p a b", a=2), ACT.Copy)
            last.then_inc(pool_Ta, 1)
            spread_out(len(SPREAD) - 1)
            stats(NORM_MOE[1], (pool_h, 1), (pool_h, 2))
            moe(1)
            stats(NORM_LAST, (L["h_ready"], 3), (L["h_ready"], 4))

        @block.vector
        def _(dve):
            V = nc.vector
            link = linker(dve, dve_chain)
            dve.wait_ge(par_ps, 1)
            V.tensor_copy(parT[:], psum[0][:, 0:40]).then_inc(par_T, 1)
            dve.wait_ge(par_T, 1)
            l0, l1 = parT[:, 24:32], parT[:, 32:40]
            link(V.tensor_tensor(lbw[:, 16:24], l0, l1, ALU.max))
            V.tensor_tensor(lbw[:, 0:8], l0, lbw[:, 16:24], ALU.subtract)
            V.tensor_tensor(lbw[:, 8:16], l1, lbw[:, 16:24], ALU.subtract).then_inc(par_T, 1)
            dve.wait_ge(sig_c, 1)
            link(V.tensor_tensor(silc, silc, parT[:, 0:16], ALU.mult))
            for w in range(2):
                last = V.tensor_copy(csil[:, :, 16 * w:16 * w + 16],
                                     silc[:, 8 * w:8 * w + 8].unsqueeze(2).to_broadcast([P, KC, 16]))
            last.then_inc(csil_ready, 1)
            dve.wait_ge(sig_c, 2)
            link(V.tensor_tensor(lbw[:, 16:24], lbw[:, 0:8], lbw[:, 8:16], ALU.add))
            link(V.reciprocal(lbw[:, 24:32], lbw[:, 16:24]))
            V.tensor_tensor(lbw[:, 32:40], lbw[:, 0:8], lbw[:, 24:32], ALU.mult)
            link(V.tensor_tensor(lbw[:, 40:48], lbw[:, 8:16], lbw[:, 24:32], ALU.mult))
            link(V.tensor_tensor(lbs[:, 0:8], lbw[:, 32:40], lbw[:, 40:48], ALU.add))
            link(V.tensor_tensor(lbs[:, 0:8], lbs[:, 0:8], lbw[:, 32:40], ALU.subtract))
            link(V.tensor_scalar(lbs[:, 8:16], lbs[:, 0:8], -1.0, 1.0, ALU.mult, ALU.add))
            dve.wait_ge(sq_done, 1)
            V.tensor_scalar(ms, ss, 1.0 / D, EPS, ALU.mult, ALU.add).then_inc(ms_ready, 1)
            dve.wait_ge(rstd_ready, 1)
            for tt in range(4):
                src = h[:, tt] if tt < NT else cx[:, tt - NT]
                dst = xnl[:, tt] if tt < NT else cx[:, tt - NT]
                V.tensor_scalar(dst, src, rstd[:, tt:tt + 1], None, ALU.mult).then_inc(xn_ready, 1)

            def mod_rows_out(b):
                dve.wait_ge(mod_used, 4 * MPOS[b] + 4)
                dve.wait_ge(s_bm, 48)
                V.tensor_tensor(modrow[:, b, :], psum[MOD_BANK][:], modrow[:, b, :], ALU.add).then_inc(mod_rows, 1)
                if b in GAIN_BANKS:
                    n = GAIN_BANKS.index(b)
                    dve.wait_ge(mod_rows, MPOS[b] + 1)
                    dve.wait_ge(s_gain, 48)
                    V.scalar_tensor_tensor(modrow[:, b, :], modrow[:, b, :], cst[:, C_GROW + n:C_GROW + n + 1],
                                           gain_row[:, n], ALU.add, ALU.mult).then_inc(gain_done, 1)

            mod_rows_out(0)
            dve.wait_ge(modT_ps, 1)
            for j in range(4):
                last = V.tensor_copy(modT[:, 4 * j:4 * j + 4, :], psum[2 + j][:, 0:8].rearrange("p (a b) -> p a b", a=4))
            link(last)
            V.scalar_tensor_tensor(A1T, modT[:, KC:2 * KC, :], 1.0,
                                   parT[:, 16:24].unsqueeze(2).to_broadcast([P, KC, 2]), ALU.add,
                                   ALU.mult).then_inc(A1_ready, 1)
            dve.wait_ge(A1_ready, 1)
            def input_full(n):
                k = K_ORDER[n]
                dve.wait_ge(uT_ps, n + 1)
                for w in range(2):
                    last = V.tensor_scalar(uT[:, k, w * T:(w + 1) * T], psum[k][:, w * T:(w + 1) * T],
                                           A1T[:, k, w:w + 1], modT[:, k, w:w + 1], ALU.mult, ALU.add)
                last.then_inc(uT_full, 1)

            def input_low(n):
                k = K_ORDER[n]
                dve.wait_ge(uT_high, n + 1)
                if n == 4:
                    dve.wait_ge(uT_ps, KC)
                V.tensor_tensor(uT_lo[k], uT[:, k, :], uT_hi[:, k, :].bitcast(F32), ALU.subtract)

            def weights_low(i, kn):
                n, at = KC * i + kn, SLOT_A[("in", SPLIT_PROJ[i])]
                dve.wait_ge(in_hi, n + 1)
                hi, lo = in_w[n % W_BUFS]
                V.tensor_tensor(lo, slot_as(at, KC)[:, chunk(i, kn), :], hi.bitcast(F32), ALU.subtract).then_inc(in_lo, 1)

            def gate_out():
                dve.wait_ge(s_an, 16)
                for m in range(NT):
                    u = U_END[I_A] + m
                    dve.wait_ge(g_sig, m + 1)
                    V.tensor_tensor(gn[:, m, :], unit_bank(u)[:], gn[:, m, :], ALU.mult).then_inc(g_out, 1)
                    dve.wait_ge(g_out, m + 1)
                    link(V.tensor_tensor(gn[:, m, :], gn[:, m, :], anorm, ALU.mult))

            def forget_out(d):
                for hd in range(H):
                    i = d * H + hd
                    dve.wait_ge(proj_out, 4 + i + 1)
                    link(V.tensor_scalar(lf[:, i, :], lf[:, i, :], lbs[:, 8 + i:9 + i], lbs[:, i:i + 1], ALU.mult, ALU.add))
                    V.tensor_scalar(kl[:, i, :], lf[:, i, 0:T], -1.0, 1.0, ALU.mult, ALU.add)
                    last = V.tensor_scalar(kc[:, i, :], lf[:, i, T:2 * T], -1.0, 1.0, ALU.mult, ALU.add)
                last.then_inc(f_ready, 1)

            for n in range(4):
                input_full(n)
            for kn in range(KC):
                input_low(kn)
                weights_low(0, kn)
                if kn + 4 < KC:
                    input_full(kn + 4)
            for i in range(1, len(SPLIT_PROJ)):
                for kn in range(KC):
                    weights_low(i, kn)
                    if kn == 2:
                        if i == 2:
                            mod_rows_out(MODS[1])
                            gate_out()
                        if i == 3:
                            forget_out(0)
            forget_out(1)
            mod_rows_out(MODS[2])
            dve.wait_ge(proj_done, U_END[F_B])
            link(V.memset(X[:, :, :, 0:1], 0.0))
            for d in range(2):
                dve.wait_ge(lf_ready, d + 1)
                for hd in range(H):
                    i = d * H + hd
                    for w in range(2):
                        last = V.tensor_tensor_scan(X[:, i, w, 1:T + 1], cst[:, C_ONES:C_ONES + 1].to_broadcast([P, T]),
                                                    lf[:, i, w * T:(w + 1) * T], 0.0, ALU.mult, ALU.add)
                last.then_inc(X_ready, 1)

            def halves(a, m, second):
                b = a.rearrange("p h (b f m) -> p h b f m", f=2, m=m)
                return b[:, :, :, 1, :] if second else b[:, :, :, 0, :]

            def level_args(lev):
                m = LEVELS[lev]
                if lev >= 2:
                    dve.wait_ge(gram, lev - 1)
                for d in range(2):
                    x0 = X[:, d * H:(d + 1) * H, 0, 0:T]
                    x1 = X[:, d * H:(d + 1) * H, 0, 1 - d:1 - d + T]
                    mid = halves(x0, m, True)[:, :, :, 0:1].to_broadcast([P, H, P // m, m])
                    z = Z[lev % 2][:, d * H:(d + 1) * H, :]
                    V.tensor_tensor(halves(z, m, False), mid, halves(x1, m, False), ALU.subtract)
                    last = V.tensor_tensor(halves(z, m, True), halves(x1, m, True), mid, ALU.subtract)
                last.then_inc(z_arg, 1)

            def level_mult(lev):
                m = LEVELS[lev]
                dve.wait_ge(z_exp, lev + 1)
                for d in range(2):
                    z = Z[lev % 2][:, d * H:(d + 1) * H, :]
                    kk = kl[:, d * H:(d + 1) * H, :]
                    for second in (False, True):
                        src = qa if second == (d == 0) else kk
                        last = V.tensor_tensor(halves(z, m, second), halves(z, m, second), halves(src, m, second), ALU.mult)
                last.then_inc(z_ready, 1)

            def level_merge(lev):
                dve.wait_ge(gram, lev + 1)
                if lev == 0:
                    dve.wait_ge(atd_zero, 1)
                    V.tensor_copy(ATo[:, 0], psum[2][:].rearrange("p (a b) -> p a b", a=H))
                    V.tensor_copy(ATo[:, 1], psum[3][:].rearrange("p (a b) -> p a b", a=H)).then_inc(merged, 1)
                    return
                diag = lev == NLEV - 1
                pairs = [(0, tt) for tt in range(NT)] if diag else [(d, tt) for d in range(2) for tt in range(NT)]
                for n, (d, tt) in enumerate(pairs):
                    mask = masks[:, 14 if diag else 2 * (lev - 1) + d, :].unsqueeze(1).to_broadcast([P, H, P])
                    ins = V.copy_predicated(ATd[:, tt], mask, psum[2 * d + tt][:].rearrange("p (a b) -> p a b", a=H))
                    if n < len(pairs) - 1:
                        link(ins)
                ins.then_inc(merged, 1)
                dve.wait_ge(merged, lev + 1)

            dve.wait_ge(X_ready, 2)
            level_args(0)
            dve.wait_ge(kcd_exp, 1)
            V.tensor_tensor(kc, kcd, kc, ALU.mult).then_inc(kcd_ready, 1)
            level_mult(0)
            dve.wait_ge(kcdT_ps, 1)
            for n in range(4):
                last = V.tensor_copy(kcdT[:, n // 2, (n % 2) * 4:(n % 2) * 4 + 4, :],
                                     psum[n][:].rearrange("p (a b) -> p a b", a=4))
            last.then_inc(kcdT_ready, 1)
            dve.wait_ge(qt_exp, 1)
            for d in range(2):
                last = V.tensor_tensor(qt[:, d], qt[:, d], qa, ALU.mult)
            last.then_inc(qt_ready, 1)
            dve.wait_ge(S_ps, 1)
            for n in range(2):
                last = V.tensor_copy(S[:, 4 * n:4 * n + 4, :], psum[n][:].rearrange("p (a b) -> p a b", a=4))
            last.then_inc(S_ready, 1)
            for stage in (1, 2):
                for b in ends(stage):
                    mod_rows_out(b)
            for lev in range(NLEV):
                if lev + 1 < len(LEVELS):
                    level_args(lev + 1)
                if lev:
                    for b in ends(2 + lev):
                        mod_rows_out(b)
                level_merge(lev)
                if lev + 1 < len(LEVELS):
                    level_mult(lev + 1)
            for b in ends(2 + NLEV):
                mod_rows_out(b)
            for tt in range(NT):
                dve.wait_ge(osq, tt + 1)
                V.tensor_scalar(ssq[:, tt * H:(tt + 1) * H], ssq[:, tt * H:(tt + 1) * H], 1.0 / DK, EPS, ALU.mult,
                                ALU.add).then_inc(ro_ready, 1)
            for tt in range(NT):
                dve.wait_ge(ro_rstd, tt + 1)
                for hd in range(H):
                    last = V.scalar_tensor_tensor(cat[:, tt, hd * P:(hd + 1) * P], psum[tt][:, hd * P:(hd + 1) * P],
                                                  rstdo[:, tt * H + hd:tt * H + hd + 1],
                                                  gn[:, tt, hd * P:(hd + 1) * P], ALU.mult, ALU.mult)
                last.then_inc(a_ready, 1)
            def cat_low(n):
                dve.wait_ge(catT_high, n + 1)
                for b in range(2):
                    last = V.tensor_tensor(catT_lo[n][:, 2 * b:2 * b + 2, :],
                                           psum[2 * n + b][:].rearrange("p (k t) -> p k t", k=2),
                                           catT_hi[:, 4 * n + 2 * b:4 * n + 2 * b + 2, :].bitcast(F32), ALU.subtract)
                last.then_inc(catT_ready, 1)

            def out_low(n):
                nh, q = divmod(n, PARTS)
                dve.wait_ge(out_hi, n + 1)
                V.tensor_tensor(w_lo[q], slot(SLOT_A[("out", nh)])[:, q * PW:(q + 1) * PW], w_hi[q].bitcast(F32),
                                ALU.subtract).then_inc(out_lo, 1)

            for i in range(BH * NT):
                bank = psum[2 + i % 2]
                dve.wait_ge(sc_ps, i + 1)
                V.tensor_reduce(nmax[:, i % 2:i % 2 + 1], bank[:], axis=AX.X, op=ALU.max, negate=True).then_inc(sc_max, 1)
                if i == CAT_AT + 2:
                    cat_low(0)
                if i in (OUT_AT + 3, OUT_AT + 4):
                    out_low(i - OUT_AT - 3)
            dve.wait_ge(pv_done, BH * NT)
            link(V.reciprocal(rden, den))
            for tt in range(NT):
                r = rden.rearrange("p (h q) -> p h q", q=NT)[:, :, tt:tt + 1].to_broadcast([P, BH, DH])
                last = V.tensor_tensor(cat[:, tt, F:2 * F].rearrange("p (h d) -> p h d", h=BH),
                                       psum[6 + tt][:].rearrange("p (h d) -> p h d", h=BH), r, ALU.mult)
            last.then_inc(cat_ready, 1)

            out_low(2)
            cat_low(1)
            for n in range(3, PARTS + 2):
                out_low(n)
            dve.wait_ge(bc_out, len(S_AT))
            for n in range(4):
                nh, tt = n // 2, n % 2
                if n == 2:
                    for m in range(PARTS + 2, 2 * PARTS):
                        out_low(m)
                dve.wait_ge(y_done, n + 1)
                link(V.tensor_tensor(ytmp[:, n % 2, :], psum[4 + n][:], MB[:, 2, nh * F:(nh + 1) * F], ALU.mult))
                V.tensor_tensor(h[:, tt, nh * F:(nh + 1) * F], h[:, tt, nh * F:(nh + 1) * F], ytmp[:, n % 2, :],
                                ALU.add).then_inc(h1_ready, 1)

            def mean_square(norm):
                for tt in range(NT):
                    dve.wait_ge(n_sq, NT * norm + tt + 1)
                    V.tensor_scalar(ms[:, tt:tt + 1], ss[:, tt:tt + 1], 1.0 / D, EPS, ALU.mult, ALU.add).then_inc(n_ms, 1)

            def norm_mod(norm, gain, shift, done, before):
                for tt in range(NT):
                    dve.wait_ge(n_rstd, NT * norm + tt + 1)
                    link(V.scalar_tensor_tensor(u2[:, tt], h[:, tt], rstd[:, tt:tt + 1], MB[:, gain], ALU.mult, ALU.mult))
                    V.tensor_tensor(u2[:, tt], u2[:, tt], MB[:, shift], ALU.add).then_inc(done, 1)
                dve.wait_ge(done, before + NT)

            G, gc, s_, sbi = rs[:, 0:8], rs[:, 8:16], rs[:, 16:48], rs[:, 48:80]
            d1, d2, d3 = rs[:, 80:104], rs[:, 104:120], rs[:, 120:128]
            gsc, gm, w4 = rs[:, 128:136], rs[:, 136:138], rs[:, 138:146]
            m16, o1, m2 = rs[:, 146:178], rs[:, 178:210], rs[:, 210:242]
            t32, red, gts = rs[:, 242:274], rs[:, 274:276], rs[:, 276:308]
            rk, cnt, rg = rs[:, 308:316], rs[:, 316:318], rs[:, 320:328]
            gslot = rs[:, 328:332]

            def v3(a, b, c_):
                return a.rearrange("p (a b c) -> p a b c", a=NT, b=b, c=c_)

            def v2(a, b):
                return a.rearrange("p (a b) -> p a b", a=NT, b=b)

            def bc1(a, n):
                return a.unsqueeze(2).to_broadcast([P, NT, n])

            def first_max(dst, src, n, weights, tmp):
                link(V.tensor_reduce(red, v2(src, n), axis=AX.X, op=ALU.max))
                link(V.tensor_tensor(v2(tmp, n), v2(src, n), bc1(red, n), ALU.is_equal))
                link(V.tensor_tensor(v2(tmp, n), v2(tmp, n), weights.unsqueeze(1).to_broadcast([P, NT, n]), ALU.mult))
                link(V.tensor_reduce(red, v2(tmp, n), axis=AX.X, op=ALU.max))
                link(V.tensor_tensor(v2(dst, n), v2(tmp, n), bc1(red, n), ALU.is_equal))

            def route(l):
                s = L
                dve.wait_ge(s["scores"], l + 1)
                link(V.tensor_tensor(v2(sbi, 16), v2(s_, 16), brt.unsqueeze(1).to_broadcast([P, NT, 16]), ALU.add))
                a = v3(sbi, NG, NE)
                V.tensor_tensor(v3(d1, NG, 3), a[:, :, :, 0:3], a[:, :, :, 1:4], ALU.add)
                V.tensor_tensor(v3(d2, NG, 2), a[:, :, :, 0:2], a[:, :, :, 2:4], ALU.add)
                link(V.tensor_tensor(v3(d3, NG, 1), a[:, :, :, 0:1], a[:, :, :, 3:4], ALU.add))
                V.tensor_reduce(v2(gsc, NG), v3(d1, NG, 3), axis=AX.X, op=ALU.max)
                link(V.tensor_reduce(v2(w4, NG), v3(d2, NG, 2), axis=AX.X, op=ALU.max))
                link(V.tensor_tensor(gsc, gsc, w4, ALU.max))
                link(V.tensor_tensor(gsc, gsc, d3, ALU.max))
                first_max(G, gsc, NG, cst[:, C_W4:C_W4 + 4], w4)
                in_g = v2(G, NG).unsqueeze(3).to_broadcast([P, NT, NG, NE])
                link(V.tensor_scalar(w4, G, -NEG, NEG, ALU.mult, ALU.add))
                link(V.tensor_tensor(v3(m16, NG, NE), v3(sbi, NG, NE), in_g, ALU.mult))
                link(V.tensor_tensor(v3(m16, NG, NE), v3(m16, NG, NE),
                                     v2(w4, NG).unsqueeze(3).to_broadcast([P, NT, NG, NE]), ALU.add))
                first_max(o1, m16, 16, cst[:, C_W16:C_W16 + 16], t32)
                link(V.scalar_tensor_tensor(m16, o1, 2 * NEG, m16, ALU.mult, ALU.add))
                first_max(m2, m16, 16, cst[:, C_W16:C_W16 + 16], t32)
                link(V.tensor_tensor(o1, o1, m2, ALU.add))
                link(V.tensor_tensor(gts, o1, s_, ALU.mult))
                link(V.tensor_reduce(red, v2(gts, 16), axis=AX.X, op=ALU.add))
                link(V.reciprocal(red, red))
                link(V.tensor_tensor(v2(gts, 16), v2(gts, 16), bc1(red, 16), ALU.mult))
                V.tensor_reduce(v2(gc, NE), v3(gts, NG, NE).rearrange("p a g e -> p a e g"), axis=AX.X,
                                op=ALU.add).then_inc(s["gates"], 1)
                dve.wait_ge(s["ranks"], l + 1)
                link(V.tensor_scalar(rk, psum[5][:, 0:8], 1.0, None, ALU.add))
                link(V.tensor_tensor(rk, rk, G, ALU.mult))
                V.tensor_scalar(rg, rk, -1.0, None, ALU.add)
                link(V.tensor_reduce(cnt[:, 0:1], psum[5][:, 8:12], axis=AX.X, op=ALU.max))
                V.tensor_scalar(flag[0:1, l:l + 1], cnt[0:1, 0:1], CAP + 0.5, None, ALU.is_gt).then_inc(s["routed"], 1)
                dve.wait_ge(s["routed"], l + 1)

            def low(sems, t, j, n, qs=range(PARTS)):
                for q in qs:
                    dve.wait_ge(sems["hi"], t * TP + (PARTS * j + q + 1))
                    V.tensor_tensor(w_lo[q], slot(n)[:, q * PW:(q + 1) * PW], w_hi[q].bitcast(F32),
                                    ALU.subtract).then_inc(sems["lo"], 1)

            def experts(sems, tb, n0, started):
                def weights(t, kind, e, qs=range(PARTS)):
                    low(sems, t, ITEM[kind, e], n0 + ITEM[kind, e], qs)

                def choose(t, i):
                    for tt in range(NT):
                        last = V.tensor_scalar(Pg[:, tt, :], cst[:, C_IOTA:C_IOTA + P], rg[:, bass.ds(i + 4 * tt, 1)],
                                               None, ALU.is_equal)
                    last.then_inc(sems["p_ready"], 1)

                def slots_of(t):
                    dve.wait_ge(sems["route_ps"], t + 1)
                    V.tensor_copy(gslot[0:CAP], psum[7][0:CAP, 0:4])
                    V.tensor_copy(PT[0:CAP], psum[7][0:CAP, P:3 * P].rearrange("p (a b) -> p a b", a=NT)).then_inc(sems["gs"], 1)
                    dve.wait_ge(sems["gs"], t + 1)

                def gathered(t):
                    dve.wait_ge(sems["xg_hi"], t + 1)
                    for n in range(2):
                        last = V.tensor_tensor(x_lo[:, 4 * n:4 * n + 4, :],
                                               psum[2 + n][:].rearrange("p (k n) -> p k n", k=4)[:, :, 0:CAP],
                                               x_hi[:, 4 * n:4 * n + 4, :].bitcast(F32), ALU.subtract)
                    last.then_inc(sems["xg_lo"], 1)

                def gate_hidden(t, e):
                    dve.wait_ge(sems["silu"], t * NE + (e + 1))
                    dve.wait_ge(*consumed(sems, t, ITEM["u", e]))
                    V.scalar_tensor_tensor(hh[0:CAP], sg[0:CAP], gslot[0:CAP, e:e + 1], psum[2 * (e % 2) + 1][0:CAP, :],
                                           ALU.mult, ALU.mult).then_inc(sems["hid"], 1)

                def hidden(t, e):
                    dve.wait_ge(sems["hT_hi"], t * NE + (e + 1))
                    V.tensor_tensor(hT_lo, psum[4][:].rearrange("p (c n) -> p c n", c=4)[:, :, 0:CAP],
                                    hT_hi.bitcast(F32), ALU.subtract).then_inc(sems["hT_lo"], 1)

                def add(n):
                    tt, nh = n // 2, n % 2
                    part = yacc[:, tt, nh * F:(nh + 1) * F]
                    return V.tensor_tensor(part, psum[SCAT_BANKS[n]][:], part, ALU.add)

                def tile(t, i, more):
                    for e in range(1, NE):
                        weights(t, "g", e)
                        if e == 1:
                            slots_of(t)
                        gate_hidden(t, e - 1)
                        weights(t, "u", e)
                        hidden(t, e - 1)
                        weights(t, "d", e - 1, range(0, 2))
                        if e == NE - 1:
                            gate_hidden(t, e)
                        weights(t, "d", e - 1, range(2, PARTS))
                    if more:
                        choose(t + 1, i + 1)
                    weights(t, "d", NE - 1)
                    hidden(t, NE - 1)
                    if more:
                        gathered(t + 1)
                        weights(t + 1, "g", 0)
                    dve.wait_ge(sems["yg_hi"], t + 1)
                    for nh in range(2):
                        last = V.tensor_tensor(yg_lo[0:CAP, nh * F:(nh + 1) * F], psum[5 + nh][0:CAP, :],
                                               yg_hi[0:CAP, nh * F:(nh + 1) * F].bitcast(F32), ALU.subtract)
                    last.then_inc(sems["yg_lo"], 1)
                    if more:
                        weights(t + 1, "u", 0, range(0, 2))
                    dve.wait_ge(sems["scat_ps"], t + 1)
                    add(0)
                    add(1)
                    if more:
                        weights(t + 1, "u", 0, range(2, PARTS))
                    add(2)
                    add(3).then_inc(sems["scat"], 1)
                    dve.wait_ge(sems["scat"], t + 2)

                choose(tb, 0)
                if not started:
                    weights(tb, "g", 0)
                gathered(tb)
                weights(tb, "u", 0)
                with dve.Fori(0, NG - 1) as i:
                    tile(i + tb, i, True)
                tile(tb + NG - 1, NG - 1, False)

            def moe(l):
                n0 = (N_MOE0, N_MOE1)[l]
                if l:
                    low(PASS[0], l * NG, 0, n0)
                route(l)
                if l == 0:
                    for k in range(2):
                        dve.sem_inc(PASS[k]["scat"], 1)
                dve.wait_ge(L["yacc0"], l + 1)
                experts(PASS[0], l * NG, n0, bool(l))
                go = dve.value_load(flag[0:1, l:l + 1])
                with dve.If(go > 0):
                    V.tensor_scalar(rg, rg, -float(CAP), None, ALU.add).then_inc(ov_chain, 1)
                    dve.wait_ge(ov_chain, l + 1)
                    experts(PASS[1], l * NG, 0, False)
                with dve.Else():
                    dve.sem_inc(ov_chain, 1)
                    count_skipped(dve, "dve")
                for tt in range(NT):
                    link(V.tensor_tensor(yacc[:, tt], yacc[:, tt], MB[:, 5], ALU.mult))
                    V.tensor_tensor(h[:, tt], h[:, tt], yacc[:, tt], ALU.add).then_inc(L["h_ready"], 1)
                dve.wait_ge(L["h_ready"], NT * (l + 1))

            dve.wait_ge(h1_ready, 4)
            mean_square(NORM_MOE[0])
            norm_mod(NORM_MOE[0], 4, 3, L["u2"], 0)
            for b in ends(len(PLAN) - 1):
                mod_rows_out(b)
            dve.wait_ge(s_rt, 32)
            moe(0)
            dve.wait_ge(bc_out, len(SPREAD) - 1)
            mean_square(NORM_POOL)
            norm_mod(NORM_POOL, 1, 0, pool_u, 0)
            dve.wait_ge(pool_ps, 4)
            for g in range(2, 4):
                last = V.tensor_copy(pT[:, 2 * g:2 * g + 2, :], psum[g][:].rearrange("p (a b) -> p a b", a=2))
            last.then_inc(pool_T, 1)
            dve.wait_ge(gate_scaled, 1)
            for n in range(4):
                tt, gh = n // 2, n % 2
                dve.wait_ge(pool_y, n + 1)
                link(V.tensor_tensor(mtmp[:, n % 2 * F:(n % 2 + 1) * F], psum[4 + n][:], MB[:, 2, gh * F:(gh + 1) * F], ALU.mult))
                ins = V.tensor_tensor(h[:, tt, gh * F:(gh + 1) * F], h[:, tt, gh * F:(gh + 1) * F],
                                      mtmp[:, n % 2 * F:(n % 2 + 1) * F], ALU.add)
                if gh:
                    ins.then_inc(pool_h, 1)
                    dve.wait_ge(pool_h, tt + 1)
                else:
                    link(ins)
            mean_square(NORM_MOE[1])
            norm_mod(NORM_MOE[1], 4, 3, L["u2"], NT)
            moe(1)
            mean_square(NORM_LAST)
            dve.wait_ge(s_scl, 32)
            for tt in range(NT):
                dve.wait_ge(n_rstd, NT * NORM_LAST + tt + 1)
                V.scalar_tensor_tensor(mtmp[:, tt * D:(tt + 1) * D], h[:, tt], rstd[:, tt:tt + 1], scl, ALU.mult,
                                       ALU.mult).then_inc(fin_out, 1)

        @block.gpsimd
        def _(pool):
            Gp = nc.gpsimd

            Gp.memset(modrow[:], 0.0).then_inc(pool_chain, 1)
            pool.wait_ge(pool_chain, 1)
            for l in range(2):
                pool.dma_start(modrow[0:P:32, 3 * l:3 * l + 3, :],
                               b_mod[l].rearrange("(b j n) -> j b n", b=3, j=4)).then_inc(s_bm, 16)
            pool.dma_start(modrow[16:P:32, 0, :], b_mod[0, 0:2048].rearrange("(j n) -> j n", j=4)).then_inc(s_bm, 16)
            pool.dma_start(anorm, a_norm_g[0:1, :].to_broadcast([P, F])).then_inc(s_an, 16)

            def power(ready, count, dst, src, done):
                pool.wait_ge(ready, count)
                Gp.tensor_tensor(dst, src, half.to_broadcast([P, src.shape[1]]), ALU.pow).then_inc(done, 1)

            pool.wait_ge(sq_done, 1)
            power(ms_ready, 1, rstd, ms, rstd_ready)
            pool.dma_start(masksf, masks_d).then_inc(s_masks, 16)
            pool.wait_ge(s_masks, 16)
            Gp.tensor_copy(masks[:], masksf).then_inc(masks_ready, 1)
            pool.wait_ge(uT_ps, KC)
            Gp.memset(gain_row, 1.0).then_inc(pool_chain, 1)
            pool.wait_ge(pool_chain, 2)
            for n, (b, g) in enumerate(zip(GAIN_BANKS, (norm2_g[0], norm1_g[1], norm2_g[1]))):
                j = GAIN_PIECES[b][0]
                pool.dma_start(gain_row[32 * j:32 * j + 64:32, n, :],
                               g.rearrange("(j n) -> j n", j=2)).then_inc(s_gain, 16)

            pool.wait_ge(kcdT_ps, 1)
            Gp.memset(ATd, 0.0).then_inc(atd_zero, 1)

            def load_bias(i):
                hd, qi = i // NT, i % NT
                for half_ in range(2):
                    r = 2 * qi + half_
                    off = hd * RPB_R * RPB_C + (7 - r) * RPB_C + 15 - (GW - 1)
                    src = bass.AP(tensor=rpb.tensor, offset=off, ap=[[1, GW], [RPB_C, 4], [1, GW]])
                    pool.dma_start(bias[i % N_BIAS][half_ * GW:(half_ + 1) * GW].rearrange("p (a b) -> p a b", a=4),
                                   src).then_inc(b_dma[i % N_BIAS], 16)

            pool.wait_ge(gram, len(LEVELS))
            for i in range(4):
                load_bias(i)
            for i in range(BH * NT):
                pool.wait_ge(b_dma[i % N_BIAS], 32 * (i // N_BIAS + 1))
                Gp.tensor_tensor(bias[i % N_BIAS], bias[i % N_BIAS], cst[:, C_COLM:C_COLM + T],
                                 ALU.add).then_inc(b_ready, 1)
                if i == 2:
                    for tt in range(NT):
                        power(ro_ready, tt + 1, rstdo[:, tt * H:(tt + 1) * H], ssq[:, tt * H:(tt + 1) * H], ro_rstd)
                if i + 4 < BH * NT:
                    if i + 4 >= N_BIAS:
                        pool.wait_ge(sc_ps, i + 5 - N_BIAS)
                    load_bias(i + 4)
            pool.wait_ge(y_done, 2 * NT)
            pool.dma_start(wr, w_router.rearrange("(k p) e -> p k e", p=P)).then_inc(s_rt, 16)
            pool.dma_start(brt, b_router.rearrange("(a e) -> a e", a=1).to_broadcast([P, 16])).then_inc(s_rt, 16)

            def norm_power(norm):
                for tt in range(NT):
                    power(n_ms, NT * norm + tt + 1, rstd[:, tt:tt + 1], ms[:, tt:tt + 1], n_rstd)

            norm_power(NORM_MOE[0])
            pool.wait_ge(h1_ready, 4)
            pool.dma_start(scl, pool_scale[0:1, :].to_broadcast([P, D])).then_inc(s_scl, 16)
            Gp.memset(yacc, 0.0).then_inc(L["yacc0"], 1)
            pool.wait_ge(L["logits"], 1)
            pool.dma_start(bands, bands_d.rearrange("(t p) g n -> p t g n", p=P)).then_inc(s_bands, 16)
            norm_power(NORM_POOL)
            pool.wait_ge(bc_out, [p for p, _ in SPREAD].index(8) + 1)
            pool.wait_ge(s_scl, 16)
            Gp.tensor_tensor(MB[:, 2], MB[:, 2], scl, ALU.mult).then_inc(gate_scaled, 1)
            Gp.memset(yacc, 0.0).then_inc(L["yacc0"], 1)
            pool.wait_ge(gate_scaled, 1)
            pool.dma_start(scl, final_g.rearrange("(a n) -> a n", a=1).to_broadcast([P, D])).then_inc(s_scl, 16)
            norm_power(NORM_MOE[1])
            norm_power(NORM_LAST)


_INS = ["x", "c", "ctx", "c_ctx", "w_mod", "b_mod", "norm1_g", "norm2_g", "w_in", "w_out", "lb_logits", "a_norm_g",
        "rpb", "w_pool", "pool_scale", "w_router", "b_router", "w_gate", "w_up", "w_down", "final_g"]
_CONSTS = ["cst", "masks", "bands"]


def kernel(**inputs):
    import concourse.bacc as bacc
    from concourse.bass_utils import run_bass_kernel_spmd

    nc = bacc.Bacc("TRN2", target_bir_lowering=False, num_devices=1)
    named = {name: np.ascontiguousarray(inputs[name]) for name in _INS}
    named.update(zip(_CONSTS, shape_constants()))
    arrays, args = {}, []
    for name, a in named.items():
        arrays[f"in_{name}"] = a
        args.append(nc.dram_tensor(f"in_{name}", a.shape, mybir.dt.from_np(a.dtype), kind="ExternalInput").ap())
    out = nc.dram_tensor("out_0", (1, T, D), F32, kind="ExternalOutput").ap()
    build(nc, *args, out)
    r = run_bass_kernel_spmd(nc, [arrays], core_ids=[0])
    return r.results[0]["out_0"]
```
